# Optimizing a Trainium2 kernel written in Bass

```python
import jax, jax.numpy as jnp
from jax import lax
import numpy as np

D_MODEL = 1024
BATCH = 1
SEQ = 256
DEPTH = 2

CTX_LEN = 256
GRID_W = 64
D_MIX = D_MODEL
D_HGRN = D_MIX // 2
HGRN_HEAD_DIM = 128
HGRN_HEADS = D_HGRN // HGRN_HEAD_DIM
HGRN_CHUNK = 16
D_POOL = D_MIX - D_HGRN
POOL_WINDOWS = (2, 4, 8, 16)
POOL_GROUPS = len(POOL_WINDOWS)
POOL_GROUP_DIM = D_POOL // POOL_GROUPS
D_IN = 5 * D_HGRN + D_POOL
D_FF_DENSE = 2816
N_EXPERTS = 8
TOP_K = 2
D_FF_EXPERT = 3584
N_ADA = 6
EPS = 1e-6

kernel_name = "hybrid_hgrn2_pool_moe_dit_trunk"

def rms_norm(x, w):
    xf = x.astype(jnp.float32)
    y = xf * lax.rsqrt(jnp.mean(xf * xf, axis=-1, keepdims=True) + EPS)
    return (y * w.astype(jnp.float32)).astype(x.dtype)

def modulate(h, shift, scale):
    return h * (1 + scale) + shift

def gla_chunk_scan(q, k, v, log_f, state0):
    B, L, H, DK = q.shape
    DV = v.shape[-1]
    C = HGRN_CHUNK
    nc = L // C

    def chunks(a):
        return a.reshape(B, nc, C, H, a.shape[-1]).transpose(1, 0, 3, 2, 4)

    incl = jnp.tril(jnp.ones((C, C), dtype=bool))[:, :, None]

    def step(state, blk):
        qb, kb, vb, gb = blk
        b = jnp.cumsum(gb, axis=2)
        rel = jnp.where(incl, b[:, :, :, None, :] - b[:, :, None, :, :], -jnp.inf)
        scores = jnp.einsum('bhtk,bhsk,bhtsk->bhts', qb, kb, jnp.exp(rel))
        o = (jnp.einsum('bhts,bhsv->bhtv', scores, vb)
             + jnp.einsum('bhtk,bhkv->bhtv', qb * jnp.exp(b), state))
        b_end = b[:, :, -1:, :]
        state = (jnp.exp(b_end[:, :, 0, :, None]) * state
                 + jnp.einsum('bhsk,bhsv->bhkv', kb * jnp.exp(b_end - b), vb))
        return state, o

    state, o = lax.scan(step, state0, tuple(map(chunks, (q, k, v, log_f))))
    return o.transpose(1, 0, 3, 2, 4).reshape(B, L, H, DV), state

def hgrn_inputs(z, lb):
    B, L = z.shape[:2]
    q, i, f_fwd, f_bwd, g = jnp.split(z, 5, axis=-1)
    heads = lambda a: a.reshape(B, L, HGRN_HEADS, HGRN_HEAD_DIM)
    log_fs, ks = [], []
    for d, zf in enumerate((f_fwd, f_bwd)):
        f = lb[d] + (1 - lb[d]) * jax.nn.sigmoid(zf)
        log_fs.append(heads(jnp.log(f)))
        ks.append(heads(1 - f))
    return heads(q) * HGRN_HEAD_DIM ** -0.5, heads(i), log_fs, ks, g

def hgrn_readout(o, g, w):
    B, L = o.shape[:2]
    o = o * lax.rsqrt(jnp.mean(o * o, axis=-1, keepdims=True) + EPS) * w.reshape(HGRN_HEADS, HGRN_HEAD_DIM)
    return o.reshape(B, L, D_HGRN) * jax.nn.silu(g)

def hgrn_mixer(z_ctx, z_lat, lb, out_norm_w):
    q_c, i_c, lf_c, k_c, g_c = hgrn_inputs(z_ctx, lb)
    q_l, i_l, lf_l, k_l, g_l = hgrn_inputs(z_lat, lb)
    B = z_lat.shape[0]
    state0 = jnp.zeros((B, HGRN_HEADS, HGRN_HEAD_DIM, HGRN_HEAD_DIM), jnp.float32)
    o_ctx, o_lat = 0.0, 0.0
    for d in range(2):
        rev = (lambda a: jnp.flip(a, axis=1)) if d else (lambda a: a)
        oc, s_ctx = gla_chunk_scan(rev(q_c), rev(k_c[d]), rev(i_c), rev(lf_c[d]), state0)
        ol, _ = gla_chunk_scan(rev(q_l), rev(k_l[d]), rev(i_l), rev(lf_l[d]), s_ctx)
        o_ctx = o_ctx + rev(oc)
        o_lat = o_lat + rev(ol)
    return hgrn_readout(o_ctx, g_c, out_norm_w), hgrn_readout(o_lat, g_l, out_norm_w)

def centred_window_sum(x, axis, k):
    n = x.shape[axis]
    lo, hi = k // 2, k - 1 - k // 2
    cs = jnp.cumsum(x, axis=axis)
    cs = jnp.concatenate([jnp.zeros_like(lax.slice_in_dim(cs, 0, 1, axis=axis)), cs], axis=axis)
    pos = np.arange(n)
    end = np.minimum(pos + hi + 1, n)
    start = np.maximum(pos - lo, 0)
    total = jnp.take(cs, end, axis=axis) - jnp.take(cs, start, axis=axis)
    return total, (end - start).astype(np.float32)

def pool_latent(v):
    B, T = v.shape[:2]
    rows = T // GRID_W
    grid = v.reshape(B, rows, GRID_W, POOL_GROUPS, POOL_GROUP_DIM)
    means = []
    for j, k in enumerate(POOL_WINDOWS):
        s_col, n_col = centred_window_sum(grid[:, :, :, j, :], 2, k)
        s, n_row = centred_window_sum(s_col, 1, k)
        means.append(s / (n_row[:, None] * n_col[None, :])[None, :, :, None])
    return jnp.stack(means, axis=3).reshape(B, T, POOL_GROUPS, POOL_GROUP_DIM) - v

def pool_context(v):
    means = []
    for j, k in enumerate(POOL_WINDOWS):
        s, n = centred_window_sum(v[:, :, j, :], 1, k)
        means.append(s / n[None, :, None])
    return jnp.stack(means, axis=2) - v

def pool_mixer(diff, w, scale):
    B, L = diff.shape[:2]
    return jnp.einsum('blgc,gcd->blgd', diff, w).reshape(B, L, D_POOL) * scale

def swiglu(h, wg, wu, wd):
    return (jax.nn.silu(h @ wg) * (h @ wu)) @ wd

def moe_swiglu(h, w_router, wg, wu, wd):
    logits = jnp.einsum('bld,de->ble', h.astype(jnp.float32), w_router.astype(jnp.float32))
    top_logits, top_idx = lax.top_k(logits, TOP_K)
    top_w = jax.nn.softmax(top_logits, axis=-1)
    combine = jnp.einsum('blk,blke->ble', top_w, jax.nn.one_hot(top_idx, N_EXPERTS, dtype=jnp.float32))
    out = jnp.zeros(h.shape, jnp.float32)
    for e in range(N_EXPERTS):
        out = out + combine[..., e:e + 1] * swiglu(h, wg[e], wu[e], wd[e]).astype(jnp.float32)
    return out

def setup_inputs(seed: int = 0) -> dict:
    key = jax.random.key(seed)
    ks = jax.random.split(key, 24)
    n_dense, n_moe = (DEPTH + 1) // 2, DEPTH // 2
    f32 = jnp.float32
    nrm = lambda k, shape: jax.random.normal(k, shape, f32)
    return {
        "x": nrm(ks[0], (BATCH, SEQ, D_MODEL)),
        "c": nrm(ks[1], (BATCH, D_MODEL)),
        "ctx": nrm(ks[2], (BATCH, CTX_LEN, D_MODEL)),
        "c_ctx": nrm(ks[3], (D_MODEL,)),
        "w_ada": nrm(ks[4], (DEPTH, D_MODEL, N_ADA * D_MODEL)) * 0.5 * D_MODEL ** -0.5,
        "b_ada": nrm(ks[5], (DEPTH, N_ADA * D_MODEL)) * 0.02,
        "norm_w": 1 + 0.1 * nrm(ks[6], (DEPTH, 2, D_MODEL)),
        "w_in": nrm(ks[7], (DEPTH, D_MODEL, D_IN)) * D_MODEL ** -0.5,
        "hgrn_lb_raw": 0.5 * nrm(ks[8], (DEPTH, 2, D_HGRN)),
        "hgrn_norm_w": 1 + 0.1 * nrm(ks[9], (DEPTH, D_HGRN)),
        "w_pool": nrm(ks[10], (DEPTH, POOL_GROUPS, POOL_GROUP_DIM, POOL_GROUP_DIM)) * POOL_GROUP_DIM ** -0.5,
        "pool_scale": 0.5 + 0.1 * nrm(ks[11], (DEPTH, D_POOL)),
        "w_out": nrm(ks[12], (DEPTH, D_MIX, D_MODEL)) * D_MIX ** -0.5,
        "ffn_wg": nrm(ks[13], (n_dense, D_MODEL, D_FF_DENSE)) * D_MODEL ** -0.5,
        "ffn_wu": nrm(ks[14], (n_dense, D_MODEL, D_FF_DENSE)) * D_MODEL ** -0.5,
        "ffn_wd": nrm(ks[15], (n_dense, D_FF_DENSE, D_MODEL)) * D_FF_DENSE ** -0.5,
        "router_w": nrm(ks[16], (n_moe, D_MODEL, N_EXPERTS)) * D_MODEL ** -0.5,
        "moe_wg": nrm(ks[17], (n_moe, N_EXPERTS, D_MODEL, D_FF_EXPERT)) * D_MODEL ** -0.5,
        "moe_wu": nrm(ks[18], (n_moe, N_EXPERTS, D_MODEL, D_FF_EXPERT)) * D_MODEL ** -0.5,
        "moe_wd": nrm(ks[19], (n_moe, N_EXPERTS, D_FF_EXPERT, D_MODEL)) * D_FF_EXPERT ** -0.5,
        "final_norm_w": 1 + 0.1 * nrm(ks[20], (D_MODEL,)),
    }

def reference(x, c, ctx, c_ctx, w_ada, b_ada, norm_w, w_in, hgrn_lb_raw, hgrn_norm_w, w_pool,
              pool_scale, w_out, ffn_wg, ffn_wu, ffn_wd, router_w, moe_wg, moe_wu, moe_wd,
              final_norm_w):
    f32 = jnp.float32
    B, T, D = x.shape
    Lc = ctx.shape[1]
    lb_cum = jnp.cumsum(jax.nn.softmax(hgrn_lb_raw.astype(f32), axis=0), axis=0)
    lower_bounds = lb_cum - lb_cum[:1]
    h_lat, h_ctx = x, ctx
    for l in range(DEPTH):
        last = l == DEPTH - 1
        mod_l = (jax.nn.silu(c) @ w_ada[l] + b_ada[l]).reshape(B, N_ADA, 1, D)
        mod_c = (jax.nn.silu(c_ctx) @ w_ada[l] + b_ada[l]).reshape(N_ADA, 1, 1, D)
        u_lat = modulate(rms_norm(h_lat, norm_w[l, 0]), mod_l[:, 0], mod_l[:, 1])
        u_ctx = modulate(rms_norm(h_ctx, norm_w[l, 0]), mod_c[0], mod_c[1])
        z = (jnp.concatenate([u_ctx, u_lat], axis=1) @ w_in[l]).astype(f32)
        z_ctx, z_lat = z[:, :Lc], z[:, Lc:]
        a_ctx, a_lat = hgrn_mixer(z_ctx[..., :5 * D_HGRN], z_lat[..., :5 * D_HGRN],
                                  lower_bounds[l], hgrn_norm_w[l])
        pv_lat = z_lat[..., 5 * D_HGRN:].reshape(B, T, POOL_GROUPS, POOL_GROUP_DIM)
        p_lat = pool_mixer(pool_latent(pv_lat), w_pool[l], pool_scale[l])
        y_lat = jnp.concatenate([a_lat, p_lat], axis=-1) @ w_out[l]
        h_lat = h_lat + (mod_l[:, 2] * y_lat).astype(h_lat.dtype)
        if not last:
            pv_ctx = z_ctx[..., 5 * D_HGRN:].reshape(B, Lc, POOL_GROUPS, POOL_GROUP_DIM)
            p_ctx = pool_mixer(pool_context(pv_ctx), w_pool[l], pool_scale[l])
            y_ctx = jnp.concatenate([a_ctx, p_ctx], axis=-1) @ w_out[l]
            h_ctx = h_ctx + (mod_c[2] * y_ctx).astype(h_ctx.dtype)
        v = modulate(rms_norm(h_lat, norm_w[l, 1]), mod_l[:, 3], mod_l[:, 4])
        if not last:
            v = jnp.concatenate([modulate(rms_norm(h_ctx, norm_w[l, 1]), mod_c[3], mod_c[4]), v], axis=1)
        if l % 2 == 0:
            y = swiglu(v, ffn_wg[l // 2], ffn_wu[l // 2], ffn_wd[l // 2])
        else:
            y = moe_swiglu(v, router_w[l // 2], moe_wg[l // 2], moe_wu[l // 2], moe_wd[l // 2])
        h_lat = h_lat + (mod_l[:, 5] * y[:, -T:]).astype(h_lat.dtype)
        if not last:
            h_ctx = h_ctx + (mod_c[5] * y[:, :Lc]).astype(h_ctx.dtype)
    return rms_norm(h_lat, final_norm_w)


_drawn_inputs = setup_inputs


def setup_inputs(seed=0):
    import zlib

    import numpy as np

    out = dict(_drawn_inputs(seed))
    spreads = {}
    factors = {'ctx': 4.115, 'c_ctx': 5.674}
    for name, (base, spread) in spreads.items():
        noise = np.random.default_rng([zlib.crc32(name.encode()), seed]).standard_normal(out[name].shape)
        drawn = base * np.exp(spread * noise) if base else spread * noise
        out[name] = __import__('jax').numpy.asarray(drawn.astype(out[name].dtype))
    for name, factor in factors.items():
        out[name] = (out[name] * factor).astype(out[name].dtype)
    return out
```

```python
import concourse.bass as bass
from concourse import mybir
from contextlib import ExitStack

D = 1024
KT = D // 128
CTX = LAT = 256
NTOK = CTX + LAT
HEADS = 4
HD = 128
NCH = NTOK // 128
LEVELS = 7
NADA = 6
ADA_BLKS = NADA * KT
F_DENSE = 2816
F_EXP = 3584
NE = 8
DEPTH = 2
EPS = 1e-6
UNIT = 2048
SUB = UNIT // 2
NR = 4
NRM = 6
NS = 4
FFN_IT = F_DENSE // 256
DOWN_U = F_DENSE // 256
FC = F_EXP // 512
SLOTS = 128
V_BADA, V_NORM, V_LB, V_HNW, V_PSC, V_FIN, V_C = 0, 96, 128, 144, 152, 160, 168
V_ROWS = 184


MOE_ORDER = [("g", 0, 0), ("g", 0, 1), ("u", 0, 0), ("u", 0, 1)]
for _c in range(1, FC):
    MOE_ORDER += [("g", _c, 0), ("g", _c, 1), ("u", _c, 0), ("u", _c, 1), ("d", _c - 1, 0), ("d", _c - 1, 1)]
MOE_ORDER += [("d", FC - 1, 0), ("d", FC - 1, 1)]
MOE_U = len(MOE_ORDER)
MOE_S = 2 * MOE_U
assert MOE_U % NRM == 0 and MOE_S % NS == 0


def plan():
    seq = [("ada0", 24, "d")]
    for l in range(DEPTH):
        seq += [(f"pv{l}", 2, "s"), (f"f0{l}", 2, "s"), (f"q{l}", 2, "s"), (f"i{l}", 2, "s"),
                (f"f1{l}", 2, "s"), (f"g{l}", 2, "s"), (f"pm{l}", 2 - l, f"p{l}"), (f"wo{l}", 4, "s")]
        if l == 0:
            seq += [("ffn", 4 * FFN_IT, "m"), ("ada1", 2, "d"), ("down", DOWN_U, "s")]
    unit, sub, direct, free = {}, {}, {}, []
    u = s = d = 0
    for name, n, kind in seq:
        unit[name], sub[name], direct[name] = u, s, d
        for i in range(n):
            split = kind == "s" or (kind == "m" and i % 4 < 2)
            if kind == "m":
                if i % 4 == 0:
                    s += 4
                if not split:
                    d += 1
            elif split:
                s += 2
            elif kind[0] == "p":
                pass
            else:
                d += 1
            free.append(("s", s) if split else (kind, 4) if kind[0] == "p" else ("d", d))
        u += n
    unit["moe"], sub["moe"], direct["moe"] = u, s, d
    return unit, sub, direct, free


def bass_hybrid_trunk(nc, x, ctx_in, vecs, w_ada, w_in, w_pool, w_out, ffn_wg, ffn_wu, ffn_wd, router_w,
                      moe_wg, moe_wu, moe_wd, cf32, pool_mats, masks, out):
    f32, f32r, i32, ui32, u8 = (mybir.dt.float32, mybir.dt.float32r, mybir.dt.int32, mybir.dt.uint32,
                               mybir.dt.uint8)
    ACT = mybir.ActivationFunctionType
    ALU = mybir.AluOpType
    AX = mybir.AxisListType
    U0, S0, D0, FREE = plan()

    st = ExitStack()
    with st:
        def sb(name, shape, dt=f32):
            return st.enter_context(nc.sbuf_tensor(name, shape, dt))

        def sem(name):
            return st.enter_context(nc.semaphore(name))

        h = sb("h", [128, KT, NTOK])
        raw = sb("raw", [128, NR, UNIT])
        w_hi = sb("w_hi", [128, NS, SUB], f32r)
        w_lo = sb("w_lo", [128, NS, SUB], f32r)
        u_hi = sb("u_hi", [128, KT, NTOK], f32r)
        u_lo = sb("u_lo", [128, KT, NTOK], f32r)
        cst = sb("cst", [128, 3 * 128 + 8])
        ident, tri, slot_iota, e_iota = cst[:, 0:128], cst[:, 128:256], cst[:, 256:384], cst[:, 384:392]
        ones = sb("ones", [128, 128])
        ones_d = sb("ones_d", [128, 128])
        ones_hd = sb("ones_hd", [128, 128])
        msk = sb("msk", [128, 2, LEVELS, 64], u8)
        vec = sb("vec", [128, V_ROWS])
        silu_c = sb("silu_c", [128, KT, 2])
        mod = sb("mod", [128, 2, ADA_BLKS, 2])
        gain = sb("gain", [128, 2, 2, KT, 2])
        lb = sb("lb", [128, 2, 2 * HEADS])
        lb1 = sb("lb1", [128, 2, 2 * HEADS])
        lbt = sb("lbt", [128, 4, 8])
        wp = sb("wp", [128, 4, 128])
        eps_t = sb("eps_t", [128, 1])
        ARENA = 20992
        arena = sb("arena", [128, ARENA])
        top = [0]

        def take(n, at=None):
            if at is None:
                at = top[0]
                top[0] += n
            assert at + n <= ARENA
            return at

        a_q, a_f0, a_f1, a_t2 = take(2048), take(2048), take(2048), take(1024)
        a_qp, a_ks, a_a, a_v = take(2048), take(2048), take(2048), take(2048)
        a_sg, a_pv, a_s = take(2048), take(2048), take(1536)

        def ar(at, n):
            return arena[:, at:at + n]

        q_t = ar(a_q, 2048)
        f_t = [ar(a_f0, 2048), ar(a_f1, 2048)]
        t2 = ar(a_t2, 1024)
        qp, ks, amat = ar(a_qp, 2048), ar(a_ks, 2048), ar(a_a, 2048)
        v_t = ar(a_v, 2048).rearrange("p (c n) -> p c n", c=NCH)
        sg = ar(a_sg, 2048).rearrange("p (h n) -> p h n", h=HEADS)
        pv = ar(a_pv, 2048).rearrange("p (c n) -> p c n", c=NCH)
        s_t = ar(a_s, 1536).rearrange("p (c h n) -> p c h n", c=3, h=HEADS)
        o_t = ar(a_f0, 2048).rearrange("p (h n) -> p h n", h=HEADS)
        diff = ar(a_t2, 1024).rearrange("p (b n) -> p b n", b=2)
        rr = ar(a_qp, 2048).rearrange("p (h n) -> p h n", h=HEADS)
        sq_o = ar(a_ks, 2048).rearrange("p (h n) -> p h n", h=HEADS)
        a32 = ar(a_a, 2048).rearrange("p (h n) -> p h n", h=HEADS)
        sq = ar(a_sg, 1024).rearrange("p (b n) -> p b n", b=2)
        u32 = ar(a_pv, 1024).rearrange("p (b n) -> p b n", b=2)
        rstd = ar(a_v, 512)
        vrow = ar(a_q, 256).rearrange("p (b n) -> p b n", b=2)
        xin = ar(a_qp, 4096).rearrange("p (c n) -> p c n", c=NCH)
        msk_in = ar(a_sg, 2 * LEVELS * 64)
        a_hid = 0
        hid = ar(a_hid, 22 * NTOK).rearrange("p (f n) -> p f n", f=22)
        sil = ar(22 * NTOK, 1024).rearrange("p (b n) -> p b n", b=2)
        assert 22 * NTOK + 1024 <= a_v
        mraw = ar(0, 2 * UNIT).rearrange("p (b n) -> p b n", b=2)
        m0 = 2 * UNIT
        v32 = ar(m0, 2048).rearrange("p (k n) -> p k n", k=KT)
        vtok = ar(m0 + 2048, 2048).rearrange("p (c n) -> p c n", c=2)
        yacc = ar(m0 + 4096, 2048).rearrange("p (k n) -> p k n", k=KT)
        ybuf = ar(m0 + 6144, 1024)
        assert m0 + 7168 <= a_v
        m1 = a_v + 512
        msil = ar(m1, 512)
        mh = ar(m1 + 512, 1024).rearrange("p (b n) -> p b n", b=2)
        assert m1 + 1536 <= a_sg
        m2 = a_sg + 1024
        pbuf = ar(m2, 256).rearrange("p (c n) -> p c n", c=2)
        pw = ar(m2 + 256, 256).rearrange("p (c n) -> p c n", c=2)
        pwt = ar(m2 + 512, 256)
        rt = ar(m2 + 768, 256)
        assert m2 + 1024 <= a_pv
        xg_hi = u_hi[:, 0:2, :].rearrange("p k n -> p (k n)").rearrange("p (k n) -> p k n", k=KT)
        xg_lo = u_lo[:, 0:2, :].rearrange("p k n -> p (k n)").rearrange("p (k n) -> p k n", k=KT)
        ht_hi, ht_lo = u_hi[:, 2:4, :], u_lo[:, 2:4, :]
        npass_i = sb("npass_i", [128, 1], i32)
        r_log, r_top, r_idf = rt[:, 64:80], rt[:, 80:96], rt[:, 112:128]
        r_idx = rt[:, 96:112].bitcast(ui32)
        r_d, r_e, r_w = rt[:, 128:130], rt[:, 130:132], rt[:, 132:136]
        r_m = rt[:, 136:168].rearrange("p (k n) -> p k n", k=2)
        r_mask, r_comb, r_pos = rt[:, 168:184], rt[:, 184:200], rt[:, 200:216]
        M_EVENTS = {}
        for n_, (kind, c_, b_) in enumerate(MOE_ORDER):
            if b_ == 1:
                ev = M_EVENTS.setdefault(2 * n_ + 1, [])
                if kind == "g":
                    ev += [("gate", c_)] + [("ht", c_ - 1)] * (c_ > 0)
                elif kind == "u":
                    ev += [("up", c_)]
                elif c_ == FC - 2:
                    ev += [("ht", FC - 1)]
        osb = ar(0, 2048).rearrange("p (c n) -> p c n", c=2)

        B = [st.enter_context(nc.psum_tensor(f"bank{i}", [128, 512], f32)) for i in range(8)]

        vec_in, const_in, x_in = sem("vec_in"), sem("const_in"), sem("x_in")
        raw_in = [sem(f"raw_in{i}") for i in range(NR)]
        hi_done, lo_done, sub_used, direct_used = sem("hi_done"), sem("lo_done"), sem("sub_used"), sem("direct_used")
        dve_step = sem("dve_step")
        vec_tr, x_tr, x_ev, vec_ready, silu_ready = (sem("vec_tr"), sem("x_tr"), sem("x_ev"), sem("vec_ready"),
                                                     sem("silu_ready"))
        mod_ready, ones_ready = sem("mod_ready"), sem("ones_ready")
        h_ready = sem("h_ready")
        sq_ready = sem("sq_ready")
        sq_used = sem("sq_used")
        inv_ready = sem("inv_ready")
        rstd_ready = sem("rstd_ready")
        hn_ready = sem("hn_ready")
        uh_ready = sem("uh_ready")
        u_ready = sem("u_ready")
        per_layer = lambda name: [sem(f"{name}{l}") for l in range(DEPTH)]
        proj_ev, pv_ev, i_ev = per_layer("proj_ev"), per_layer("pv_ev"), per_layer("i_ev")
        scan_ready = [[sem(f"scan_ready{l}{d}") for d in range(2)] for l in range(DEPTH)]
        diag_mm = [[sem(f"diag_mm{l}{d}") for d in range(2)] for l in range(DEPTH)]
        diag_ev = [[sem(f"diag_ev{l}{d}") for d in range(2)] for l in range(DEPTH)]
        lvl_mm = [[sem(f"lvl_mm{l}{d}") for d in range(2)] for l in range(DEPTH)]
        lvl_ev = [[sem(f"lvl_ev{l}{d}") for d in range(2)] for l in range(DEPTH)]
        kst_tr = [[sem(f"kst_tr{l}{d}") for d in range(2)] for l in range(DEPTH)]
        kst_ev = [[sem(f"kst_ev{l}{d}") for d in range(2)] for l in range(DEPTH)]
        st_mm = [[sem(f"st_mm{l}{d}") for d in range(2)] for l in range(DEPTH)]
        st_ev = [[sem(f"st_ev{l}{d}") for d in range(2)] for l in range(DEPTH)]
        o_mm = [[sem(f"o_mm{l}{d}") for d in range(2)] for l in range(DEPTH)]
        o_ev = [[sem(f"o_ev{l}{d}") for d in range(2)] for l in range(DEPTH)]
        diff_mm, diff_ev, pool_mm = per_layer("diff_mm"), per_layer("diff_ev"), per_layer("pool_mm")
        pool_hi, pool_lo = per_layer("pool_hi"), per_layer("pool_lo")
        osq, oms, oinv, orstd, a_f = (per_layer("osq"), per_layer("oms"), per_layer("oinv"),
                                      per_layer("orstd"), per_layer("a_f"))
        a_hi, a_lo = per_layer("a_hi"), per_layer("a_lo")
        sil_ready, hid_ready, ffn_tail = sem("sil_ready"), sem("hid_ready"), sem("ffn_tail")
        hs_hi, hs_lo, hs_used, down_mm = sem("hs_hi"), sem("hs_lo"), sem("hs_used"), sem("down_mm")
        rt_mm, vtok_tr, vtok_ev, mask_ready, pos_mm, route_ready = (
            sem("rt_mm"), sem("vtok_tr"), sem("vtok_ev"), sem("mask_ready"), sem("pos_mm"), sem("route_ready"))
        d_ready, e_ready, rt_in = sem("d_ready"), sem("e_ready"), sem("rt_in")
        p_ready, xg_mm, xg_h, xg_l = sem("p_ready"), sem("xg_mm"), sem("xg_h"), sem("xg_l")
        gu_mm, msil_ready, mh_ready, ht_tr, ht_h, ht_l = (sem("gu_mm"), sem("msil_ready"), sem("mh_ready"),
                                                         sem("ht_tr"), sem("ht_h"), sem("ht_l"))
        y_mm, y_ev, pwt_tr, pwt_ev, sc_mm, sc_ev = (sem("y_mm"), sem("y_ev"), sem("pwt_tr"), sem("pwt_ev"),
                                                    sem("sc_mm"), sem("sc_ev"))
        out_tr, out_ev, out_dma = sem("out_tr"), sem("out_ev"), sem("out_dma")
        rw_in, wp_in = sem("rw_in"), sem("wp_in")
        mraw_in = [sem(f"mraw_in{i}") for i in range(NRM)]
        slot_step = sem("slot_step")

        def m_slot(r):
            return raw[:, (U0["moe"] + r) % NR, :] if r < NR else mraw[:, r - NR, :]

        block = st.enter_context(nc.Block())

        class Steps:
            def __init__(self, eng, s):
                self.eng, self.s, self.n = eng, s, 0

            def __call__(self, ins):
                self.n += 1
                ins.then_inc(self.s, 1)
                self.eng.wait_ge(self.s, self.n)

        def sub_hi(j, shape=None):
            s = w_hi[:, j % NS, :]
            return s

        MIX, FFN = [0, 2], [1, 3]
        c0s = [0, CTX]
        outs_ch = [[0, 1, 2, 3], [2, 3]]
        order = [[0, 1, 2, 3], [1, 0, 3, 2]]

        def tiles(l):
            return [c * HEADS + hh for c in outs_ch[l] for hh in range(HEADS)]

        def seg(ap, lo_tile, n_tiles, m, half):
            return ap[:, lo_tile * 128:(lo_tile + n_tiles) * 128].rearrange(
                "p (s b m) -> p s b m", b=2, m=m)[:, :, half, :]

        def tbuf(d, L):
            src = f_t[d] if L % 2 == 0 else t2
            return src[:, 0:2048 >> L]

        @block.sync
        def _(sp):
            sp.dma_start(vrow[0:96, 0, :], vecs[0:96, :]).then_inc(vec_in, 16)
            sp.dma_start(vrow[0:88, 1, :], vecs[96:184, :]).then_inc(vec_in, 16)
            sp.dma_start(cst[:], cf32).then_inc(const_in, 16)
            sp.dma_start(msk_in, masks).then_inc(const_in, 16)

            def slot_free(u):
                if u >= NR:
                    kind, n = FREE[u - NR]
                    if kind == "s":
                        sp.wait_ge(lo_done, n)
                    elif kind[0] == "p":
                        sp.wait_ge(pool_mm[int(kind[1])], n)
                    else:
                        sp.wait_ge(direct_used, n)

            def load(u, dst_shape, src):
                slot_free(u)
                pat, kw = dst_shape
                sp.dma_start(raw[:, u % NR, :].rearrange(pat, **kw), src).then_inc(raw_in[u % NR], 16)

            K8 = ("p (k n) -> p k n", dict(k=8))
            K4 = ("p (k n) -> p k n", dict(k=4))
            K2 = ("p (k n) -> p k n", dict(k=2))
            ada = [w_ada[l].rearrange("(k p) n -> p k n", p=128) for l in range(2)]
            win = [w_in[l].rearrange("(k p) n -> p k n", p=128) for l in range(2)]
            wo = [w_out[l].rearrange("(k p) n -> p k n", p=128) for l in range(2)]
            for i in range(4):
                load(i, K8, ada[0][:, :, i * 256:(i + 1) * 256])
            sp.dma_start(xin[:, 0:2, :], ctx_in.rearrange("(c p) n -> p c n", p=128)).then_inc(x_in, 16)
            sp.dma_start(xin[:, 2:4, :], x.rearrange("(c p) n -> p c n", p=128)).then_inc(x_in, 16)
            with sp.Fori(1, 6) as i:
                for k in range(4):
                    sp.wait_ge(direct_used, i * 4 + (k - 3))
                    sp.dma_start(raw[:, k, :].rearrange("p (k n) -> p k n", k=8),
                                 ada[0][:, :, bass.ds(i * 1024 + k * 256, 256)]).then_inc(raw_in[k], 16)
            for l in range(2):
                def tok_major(name, col):
                    for b in range(2):
                        load(U0[name] + b, K4, win[l][:, 4 * b:4 * b + 4, col:col + 512])

                def feat_major(name, col):
                    for b in range(2):
                        load(U0[name] + b, K8, win[l][:, :, col + 256 * b:col + 256 * (b + 1)])

                tok_major(f"pv{l}", 5 * 512)
                feat_major(f"f0{l}", 2 * 512)
                feat_major(f"q{l}", 0)
                tok_major(f"i{l}", 512)
                feat_major(f"f1{l}", 3 * 512)
                feat_major(f"g{l}", 4 * 512)
                for b in range(2 - l):
                    load(U0[f"pm{l}"] + b, ("p (s g n) -> p s g n", dict(s=2, g=4)), pool_mats[1 - (1 - l) * (1 - b)])
                if l == 1:
                    sp.wait_ge(pool_mm[0], 4)
                sp.dma_start(wp[:], w_pool[l].rearrange("g c d -> c g d")).then_inc(wp_in, 16)
                for b in range(4):
                    load(U0[f"wo{l}"] + b, K8, wo[l][:, :, 256 * b:256 * (b + 1)])
                if l == 0:
                    wg = ffn_wg.rearrange("(k p) n -> p k n", p=128)
                    wu = ffn_wu.rearrange("(k p) n -> p k n", p=128)
                    wd = ffn_wd.rearrange("(f p) n -> p f n", p=128)
                    base = U0["ffn"]
                    for k, src in enumerate([wg[:, :, 0:256], wu[:, :, 0:256], ada[1][:, :, 0:256], ada[1][:, :, 256:512]]):
                        load(base + k, K8, src)
                    with sp.Fori(1, FFN_IT) as i:
                        for k in range(4):
                            r = (base + k) % NR
                            if k < 2:
                                sp.wait_ge(lo_done, i * 4 + S0["ffn"])
                                src = (wg, wu)[k][:, :, bass.ds(i * 256, 256)]
                            else:
                                sp.wait_ge(direct_used, i * 2 + (D0["ffn"] + k - 3))
                                src = ada[1][:, :, bass.ds(i * 512 + (k - 2) * 256, 256)]
                            sp.dma_start(raw[:, r, :].rearrange("p (k n) -> p k n", k=8), src).then_inc(raw_in[r], 16)
                    for b in range(2):
                        c = (2 * FFN_IT + b) * 256
                        load(U0["ada1"] + b, K8, ada[1][:, :, c:c + 256])
                    for b in range(DOWN_U):
                        load(U0["down"] + b, K2, wd[:, 2 * b:2 * b + 2, :])
            moe = [w.rearrange("e (k p) n -> e p k n", p=128) for w in (moe_wg, moe_wu, moe_wd)]

            def moe_load(n, e):
                kind, c, b = MOE_ORDER[n]
                w = moe["gud".index(kind)][bass.ds(e, 1)] if not isinstance(e, int) else moe["gud".index(kind)][e:e + 1]
                if kind == "d":
                    src, kk = w[:, :, 4 * c + 2 * b:4 * c + 2 * b + 2, :], 2
                else:
                    src, kk = w[:, :, 4 * b:4 * b + 4, 512 * c:512 * (c + 1)], 4
                sp.dma_start(m_slot(n % NRM).rearrange("p (k n) -> p k n", k=kk),
                             src.rearrange("e p k n -> p (e k) n")).then_inc(mraw_in[n % NRM], 16)

            S_M = S0["moe"]
            for n in range(NRM):
                if n == NR:
                    sp.wait_ge(a_lo[1], HEADS)
                    sp.dma_start(rt[:, 0:64].rearrange("p (k n) -> p k n", k=KT),
                                 router_w.rearrange("(k p) n -> p k n", p=128)).then_inc(rw_in, 16)
                if n < NR:
                    sp.wait_ge(lo_done, S_M - 2 * NR + 2 * n + 2)
                moe_load(n, 0)

            def moe_pass(s0, first_loaded):
                if not first_loaded:
                    for n in range(NRM):
                        sp.wait_ge(lo_done, s0 + 2 * (n - NRM + 1))
                        moe_load(n, 0)
                with sp.Fori(2, NE + 1) as e2:
                    for n in range(NRM, MOE_U + NRM):
                        if MOE_ORDER[n % MOE_U] != ("d", 0, 0):
                            upto = n + (MOE_ORDER[(n + 1) % MOE_U] == ("d", 0, 0))
                            sp.wait_ge(lo_done, e2 * MOE_S + (s0 - 2 * MOE_S + 2 * (upto - NRM + 1)))
                        moe_load(n % MOE_U, e2 + (n // MOE_U - 2))
                for n in range(NRM, MOE_U):
                    sp.wait_ge(lo_done, s0 + (NE - 1) * MOE_S + 2 * (n - NRM + 1))
                    moe_load(n, NE - 1)

            moe_pass(S_M, True)
            sp.wait_ge(route_ready, 1)
            npass = sp.value_load(npass_i[0:1, 0:1], min_val=1, max_val=2)
            with sp.If(npass > 1):
                moe_pass(S_M + NE * MOE_S, False)
            sp.nop()
            sp.wait_ge(out_ev, 4)
            sp.dma_start(out.rearrange("(c p) n -> p c n", p=128), osb).then_inc(out_dma, 16)
            sp.wait_ge(out_dma, 16)

        def unit_of_sub(name, k):
            return U0[name] + k // 2, k % 2

        def phase_subs():
            seq = []
            for l in range(DEPTH):
                for name, n, strided in ((f"pv{l}", 4, 0), (f"f0{l}", 4, 1), (f"q{l}", 4, 1), (f"i{l}", 4, 0),
                                         (f"f1{l}", 4, 1), (f"g{l}", 4, 1), (f"wo{l}", 8, 1)):
                    seq += [(*unit_of_sub(name, k), strided) for k in range(n)]
                if l == 0:
                    for i in range(FFN_IT):
                        seq += [(U0["ffn"] + 4 * i + k % 2, k // 2, 1) for k in range(4)]
                    seq += [(*unit_of_sub("down", k), 0) for k in range(2 * DOWN_U)]
            return seq

        SUBS = phase_subs()
        assert len(SUBS) == S0["moe"]

        def half_of(unit_ap, half, strided):
            if strided:
                return unit_ap.rearrange("p (k n) -> p k n", k=KT)[:, :, half * 128:(half + 1) * 128]
            return unit_ap[:, half * SUB:(half + 1) * SUB]

        def shaped(ap, strided):
            return ap.rearrange("p (k n) -> p k n", k=KT) if strided else ap

        @block.scalar
        def _(act):
            nxt = [0]

            def hi():
                j = nxt[0]
                nxt[0] += 1
                u, half, strided = SUBS[j]
                act.wait_ge(raw_in[u % NR], 16 * (u // NR + 1))
                if j >= NS:
                    act.wait_ge(sub_used, j - NS + 1)
                nc.scalar.activation(shaped(w_hi[:, j % NS, :], strided), half_of(raw[:, u % NR, :], half, strided),
                                     ACT.Copy).then_inc(hi_done, 1)

            def his(n):
                for _ in range(n):
                    if nxt[0] < len(SUBS):
                        hi()

            def norm(n, c0, split, prefetch=0):
                for kt in range(KT):
                    act.wait_ge(h_ready, KT * n + kt + 1)
                    if kt >= 2:
                        act.wait_ge(sq_used, KT * n + kt - 1)
                    nc.scalar.activation(sq[:, kt % 2, c0:NTOK], h[:, kt, c0:NTOK], ACT.Square).then_inc(sq_ready, 1)
                his(prefetch)
                act.wait_ge(inv_ready, n + 1)
                nc.scalar.activation(rstd[:, c0:NTOK], rstd[:, c0:NTOK], ACT.Sqrt).then_inc(rstd_ready, 1)
                if split:
                    for kt in range(KT):
                        act.wait_ge(hn_ready, KT * n + kt + 1)
                        nc.scalar.activation(u_hi[:, kt, :], u32[:, kt % 2, :], ACT.Copy).then_inc(uh_ready, 1)

            act.wait_ge(vec_ready, 1)
            nc.scalar.activation(silu_c[:].rearrange("p k s -> p s k"),
                                 vec[:, V_C:V_C + 16].rearrange("p (s k) -> p s k", s=2), ACT.Silu).then_inc(silu_ready, 1)
            act.wait_ge(d_ready, 1)
            nc.scalar.activation(lbt[:, 0:2, :], lbt[:, 0:2, :], ACT.Exp).then_inc(e_ready, 1)

            def mixer(l):
                n, c0 = MIX[l], c0s[l]
                norm(n, 0, True, prefetch=NS * (l == 0))
                base = S0[f"pv{l}"]
                for j in range(4):
                    if j < 3:
                        act.wait_ge(sub_used, base + j + 1)
                        his(1)
                act.wait_ge(sub_used, base + 4)
                for c in outs_ch[l]:
                    nc.scalar.activation(pv[:, c, :], B[2 + c][:], ACT.Copy).then_inc(pv_ev[l], 1)
                his(1)

                def heads_view(ap, hh, lo):
                    return ap.rearrange("p (c h n) -> p c h n", c=NCH, h=HEADS)[:, lo // 128:, hh, :]

                def proj(kind, name, bank0):
                    for hh in range(HEADS):
                        act.wait_ge(sub_used, S0[name] + hh + 1)
                        bk = B[(bank0 + hh) % 2]
                        if kind == "f0" or kind == "f1":
                            nc.scalar.activation(heads_view(f_t[int(kind[1])], hh, 0),
                                                 bk[:].rearrange("p (c n) -> p c n", c=NCH),
                                                 ACT.Sigmoid).then_inc(proj_ev[l], 1)
                        elif kind == "q":
                            nc.scalar.activation(heads_view(q_t, hh, c0),
                                                 bk[:, c0:].rearrange("p (c n) -> p c n", n=128),
                                                 ACT.Copy, scale=HD ** -0.5).then_inc(proj_ev[l], 1)
                        else:
                            nc.scalar.activation(sg[:, hh, c0:], bk[:, c0:], ACT.Silu).then_inc(proj_ev[l], 1)
                        his(1)

                proj("f0", f"f0{l}", 0)
                proj("q", f"q{l}", 0)
                base = S0[f"i{l}"]
                for j in range(3):
                    act.wait_ge(sub_used, base + j + 1)
                    his(1)
                act.wait_ge(sub_used, base + 4)
                for c in range(NCH):
                    nc.scalar.activation(v_t[:, c, :], B[2 + c][:], ACT.Copy).then_inc(i_ev[l], 1)
                his(1)
                proj("f1", f"f1{l}", 0)
                proj("g", f"g{l}", 0)

                def scan_tail(d):
                    for g in range(3):
                        c = order[d][g]
                        act.wait_ge(kst_tr[l][d], g + 1)
                        nc.scalar.activation(ks[:, c * 512:(c + 1) * 512], B[2 + g][:], ACT.Copy).then_inc(kst_ev[l][d], 1)
                    if d == 0:
                        for n_, c in enumerate(outs_ch[l]):
                            act.wait_ge(o_mm[l][0], n_ + 1)
                            nc.scalar.activation(o_t[:, :, c * 128:(c + 1) * 128],
                                                 B[2 + c][:].rearrange("p (h n) -> p h n", h=HEADS),
                                                 ACT.Copy).then_inc(o_ev[l][0], 1)

                scan_tail(0)
                for g in range(4):
                    act.wait_ge(diff_mm[l], g + 1)
                    if g >= 2:
                        act.wait_ge(pool_mm[l], g - 1)
                    nc.scalar.activation(diff[:, g % 2, c0:], B[2 + g][:, c0:], ACT.Copy).then_inc(diff_ev[l], 1)
                    act.wait_ge(pool_mm[l], g + 1)
                    nc.scalar.activation(u_hi[:, 4 + g, c0:], B[g % 2][:, c0:], ACT.Copy,
                                         scale=vec[:, V_PSC + 4 * l + g:V_PSC + 4 * l + g + 1]).then_inc(pool_hi[l], 1)
                scan_tail(1)
                act.wait_ge(o_ev[l][1], len(outs_ch[l]))
                for hh in range(HEADS):
                    nc.scalar.activation(sq_o[:, hh, c0:], o_t[:, hh, c0:], ACT.Square).then_inc(osq[l], 1)
                act.wait_ge(oinv[l], 4)
                nc.scalar.activation(rr[:, :, c0:], rr[:, :, c0:], ACT.Sqrt).then_inc(orstd[l], 1)
                for hh in range(HEADS):
                    act.wait_ge(a_f[l], hh + 1)
                    nc.scalar.activation(u_hi[:, hh, c0:], a32[:, hh, c0:], ACT.Copy).then_inc(a_hi[l], 1)
                base = S0[f"wo{l}"]
                for j in range(8):
                    act.wait_ge(sub_used, base + j + 1)
                    his(1)

            mixer(0)
            norm(FFN[0], 0, True)

            def ffn_block(i, b):
                t = i * 2 + b
                act.wait_ge(sub_used, i * 4 + (S0["ffn"] + 2 * b + 1))
                if not isinstance(i, int) or t >= 2:
                    act.wait_ge(hid_ready, i * 2 + (b - 1))
                nc.scalar.activation(sil[:, b, :], B[2 * b][:], ACT.Silu).then_inc(sil_ready, 1)

            for b in range(2):
                ffn_block(0, b)
                his(2)
            j0 = nxt[0]
            with act.Fori(1, FFN_IT - 1) as i:
                for b in range(2):
                    ffn_block(i, b)
                    for k in range(2):
                        jj = S0["ffn"] + 4 + 2 * b + k
                        u = U0["ffn"] + 4 + k
                        act.wait_ge(raw_in[u % NR], i * 16 + 16 * (u // NR + 1))
                        act.wait_ge(sub_used, i * 4 + (jj - NS + 1))
                        nc.scalar.activation(shaped(w_hi[:, jj % NS, :], 1), half_of(raw[:, u % NR, :], b, 1),
                                             ACT.Copy).then_inc(hi_done, 1)
            nxt[0] = j0 + 4 * (FFN_IT - 2)
            for b in range(2):
                ffn_block(FFN_IT - 1, b)
                his(2)
            for f in range(22):
                act.wait_ge(hid_ready, f + 1)
                act.wait_ge(sub_used, S0["down"] + max(0, f - KT + 1))
                nc.scalar.activation(u_hi[:, f % KT, :], hid[:, f, :], ACT.Copy).then_inc(hs_hi, 1)
                if f >= KT:
                    his(1)
            for f in range(KT):
                act.wait_ge(sub_used, S0["down"] + 22 - KT + f + 1)
                his(1)
            nxt_down = nxt[0]
            mixer(1)
            norm(FFN[1], CTX, False)

            act.wait_ge(rt_in, 1)
            nc.scalar.activation(r_e, r_d, ACT.Exp).then_inc(e_ready, 1)
            for g in range(4):
                act.wait_ge(vtok_tr, g + 1)
                nc.scalar.activation(vtok[:, g // 2, (g % 2) * 512:(g % 2 + 1) * 512], B[2 + g][:], ACT.Copy).then_inc(vtok_ev, 1)

            act.wait_ge(route_ready, 1)
            npass = act.value_load(npass_i[0:1, 0:1], min_val=1, max_val=2)
            with act.Fori(0, npass) as ps:
                with act.Fori(0, NE) as e:
                    it = ps * NE + e

                    def mhi(s):
                        n = s // 2
                        act.wait_ge(mraw_in[n % NRM], it * (16 * MOE_U // NRM) + 16 * (n // NRM + 1))
                        act.wait_ge(sub_used, it * MOE_S + (S0["moe"] + s - NS + 1))
                        nc.scalar.activation(w_hi[:, (S0["moe"] + s) % NS, :], half_of(m_slot(n % NRM), s % 2, 0),
                                             ACT.Copy).then_inc(hi_done, 1)

                    for s in range(NS):
                        mhi(s)
                    for g in range(2):
                        act.wait_ge(xg_mm, it * 2 + (g + 1))
                        nc.scalar.activation(xg_hi[:, 4 * g:4 * g + 4, :].rearrange("p k n -> p (k n)"), B[4 + g][:],
                                             ACT.Copy).then_inc(xg_h, 1)
                    act.wait_ge(pwt_tr, it + 1)
                    nc.scalar.activation(pwt, B[3][:, 0:256], ACT.Copy).then_inc(pwt_ev, 1)
                    for s in range(MOE_S):
                        ev = M_EVENTS.get(s, ())
                        for what, c in ev:
                            if what == "gate":
                                act.wait_ge(sub_used, it * MOE_S + (S0["moe"] + s + 1))
                                act.wait_ge(mh_ready, it * FC + (c + 1))
                                nc.scalar.activation(msil, B[2 * (c % 2)][:], ACT.Silu).then_inc(msil_ready, 1)
                            elif what == "ht":
                                act.wait_ge(ht_tr, it * FC + (c + 1))
                                nc.scalar.activation(ht_hi[:, c % 2, :], B[4 + c % 2][:], ACT.Copy).then_inc(ht_h, 1)
                        if s + NS < MOE_S:
                            mhi(s + NS)
                    act.wait_ge(sub_used, it * MOE_S + (S0["moe"] + MOE_S))
                    nc.scalar.activation(ybuf[:, 0:512], B[6][:], ACT.Copy).then_inc(y_ev, 1)
            norm(4, CTX, False)
            for g in range(2):
                act.wait_ge(out_tr, 2 * g + 1)
                nc.scalar.activation(osb[:, g, 0:512], B[2 + 2 * g][:], ACT.Copy).then_inc(out_ev, 1)

        @block.vector
        def _(dve):
            link = Steps(dve, dve_step)
            nxt = [0]

            def lo():
                j = nxt[0]
                nxt[0] += 1
                u, half, strided = SUBS[j]
                dve.wait_ge(hi_done, j + 1)
                nc.vector.tensor_tensor(shaped(w_lo[:, j % NS, :], strided), half_of(raw[:, u % NR, :], half, strided),
                                        shaped(w_hi[:, j % NS, :], strided).bitcast(f32), ALU.subtract).then_inc(lo_done, 1)

            def los(n):
                for _ in range(n):
                    if nxt[0] < len(SUBS):
                        lo()

            def tt(out, a, b, op):
                return nc.vector.tensor_tensor(out, a, b, op)

            def bc(ap, m):
                return ap.unsqueeze(len(ap.shape)).broadcast_to((*ap.shape, m))

            def gated(n_next, l, gi, kt, src, c0):
                parts = [(0, 0, CTX)] * (c0 == 0) + [(1, CTX, NTOK)]
                for w, a, b in parts:
                    ins = nc.vector.scalar_tensor_tensor(h[:, kt, a:b], src[:, a - NTOK + src.shape[1]:b - NTOK + src.shape[1]],
                                                         mod[:, l, gi * KT + kt, w:w + 1], h[:, kt, a:b], ALU.mult, ALU.add)
                ins.then_inc(h_ready, 1)

            def norm(n, c0, l=None, w=None, prefetch=0, target=None):
                dve.wait_ge(sq_used, KT * n + KT)
                link(nc.vector.tensor_scalar(rstd[:, c0:], B[6][:, c0:], EPS, None, ALU.add))
                nc.vector.reciprocal(rstd[:, c0:], rstd[:, c0:]).then_inc(inv_ready, 1)
                los(prefetch)
                dve.wait_ge(rstd_ready, n + 1)
                if target is not None:
                    return
                for kt in range(KT + 1):
                    if kt < KT:
                        if kt >= 2:
                            dve.wait_ge(u_ready, KT * n + kt - 1)
                        link(tt(u32[:, kt % 2, :], h[:, kt, :], rstd, ALU.mult))
                        for s_, a, b in ((0, 0, CTX), (1, CTX, NTOK)):
                            ins = nc.vector.tensor_scalar(u32[:, kt % 2, a:b], u32[:, kt % 2, a:b],
                                                          gain[:, l, w, kt, s_:s_ + 1],
                                                          mod[:, l, 3 * w * KT + kt, s_:s_ + 1], ALU.mult, ALU.add)
                            if s_ == 0:
                                link(ins)
                        ins.then_inc(hn_ready, 1)
                    if kt >= 1:
                        k = kt - 1
                        dve.wait_ge(uh_ready, KT * n + k + 1)
                        tt(u_lo[:, k, :], u32[:, k % 2, :], u_hi[:, k, :].bitcast(f32), ALU.subtract).then_inc(u_ready, 1)

            nc.vector.memset(ones[:], 1.0).then_inc(ones_ready, 1)
            nc.vector.memset(ones_d[:], 1.0 / D).then_inc(ones_ready, 1)
            nc.vector.memset(ones_hd[:], 1.0 / HD).then_inc(ones_ready, 1)
            dve.wait_ge(const_in, 32)
            link(nc.vector.tensor_copy(msk[:].rearrange("p a b n -> p (a b n)"), msk_in))
            dve.wait_ge(vec_tr, 2)
            nc.vector.tensor_copy(vec[:], B[6][:, 0:V_ROWS]).then_inc(vec_ready, 1)
            dve.wait_ge(vec_ready, 1)
            r0, r1 = vec[:, V_LB:V_LB + 8], vec[:, V_LB + 8:V_LB + 16]
            link(tt(lbt[:, 2, :], r0, r1, ALU.max))
            link(tt(lbt[:, 0, :], r0, lbt[:, 2, :], ALU.subtract))
            tt(lbt[:, 1, :], r1, lbt[:, 2, :], ALU.subtract).then_inc(d_ready, 1)
            for kt in range(KT):
                dve.wait_ge(x_tr, kt + 1)
                nc.vector.tensor_copy(h[:, kt, :], B[kt % 6][:]).then_inc(h_ready, 1)
            dve.wait_ge(e_ready, 1)
            e0, e1, t0, t1 = (lbt[:, k, :] for k in range(4))
            link(tt(t0, e0, e1, ALU.add))
            link(nc.vector.reciprocal(t1, t0))
            link(tt(e0, e0, t1, ALU.mult))
            link(tt(e1, e1, t1, ALU.mult))
            link(tt(lb[:, 0, :], e0, e0, ALU.subtract))
            link(tt(t0, e0, e1, ALU.add))
            link(tt(lb[:, 1, :], t0, e0, ALU.subtract))
            link(nc.vector.tensor_scalar(lb1[:], lb[:], -1.0, 1.0, ALU.mult, ALU.add))

            def modulation(l):
                dve.wait_ge(direct_used, (24, D0["ada1"] + 2)[l])
                link(tt(mod[:, l], B[7][:, 0:2 * ADA_BLKS].rearrange("p (b s) -> p b s", s=2),
                        bc(vec[:, V_BADA + ADA_BLKS * l:V_BADA + ADA_BLKS * (l + 1)], 2), ALU.add))
                for w in range(2):
                    ins = nc.vector.scalar_tensor_tensor(
                        gain[:, l, w], mod[:, l, (1 + 3 * w) * KT:(2 + 3 * w) * KT, :], 1.0,
                        bc(vec[:, V_NORM + (2 * l + w) * KT:V_NORM + (2 * l + w + 1) * KT], 2), ALU.add, ALU.mult)
                ins.then_inc(mod_ready, 1)
                dve.wait_ge(mod_ready, l + 1)

            modulation(0)

            def mixer(l):
                n, c0 = MIX[l], c0s[l]
                TL = tiles(l)
                t0, nt = TL[0], len(TL)
                norm(n, 0, l, 0, prefetch=NS * (l == 0))
                los(4)

                def gates(d, name):
                    for hh in range(HEADS):
                        first = {"f0": 0, "f1": 8}[name]
                        dve.wait_ge(proj_ev[l], first + hh + 1)
                        fv = f_t[d].rearrange("p (c h n) -> p c h n", c=NCH, h=HEADS)[:, :, hh, :]
                        link(nc.vector.tensor_scalar(fv, fv, lb1[:, l, d * HEADS + hh:d * HEADS + hh + 1],
                                                     lb[:, l, d * HEADS + hh:d * HEADS + hh + 1], ALU.mult, ALU.add))
                        los(1)

                def start(d):
                    link(nc.vector.tensor_scalar(ks, f_t[d], -1.0, 1.0, ALU.mult, ALU.add))
                    tt(qp[:, t0 * 128:], q_t[:, t0 * 128:], f_t[d][:, t0 * 128:], ALU.mult).then_inc(scan_ready[l][d], 1)

                gates(0, "f0")
                los(4)
                los(4)
                dve.wait_ge(proj_ev[l], 8)
                start(0)

                def scan(d, fill):
                    A3 = amat.rearrange("p (t n) -> p t n", n=128)
                    for g in range(nt // 4):
                        dve.wait_ge(diag_mm[l][d], g + 1)
                        tt(A3[:, t0 + 4 * g:t0 + 4 * g + 4, :], B[2 + g][:].rearrange("p (t n) -> p t n", t=4),
                           ident.unsqueeze(1).broadcast_to((128, 4, 128)), ALU.mult).then_inc(diag_ev[l][d], 1)
                    for L in range(LEVELS):
                        m = 1 << L
                        qh, kh = (1, 0) if d == 0 else (0, 1)
                        T = tbuf(d, L)
                        dve.wait_ge(lvl_mm[l][d], (L + 1) * (nt // 8))
                        T2 = T.rearrange("p (s b) -> p s b", b=2)
                        kv = seg(ks, 0, 16, m, kh)
                        tt(kv, kv, bc(T2[:, :, qh], m), ALU.mult)
                        qv = seg(qp, t0, nt, m, qh)
                        tt(qv, qv, bc(T2[:, (t0 * 128) // (2 * m):, kh], m), ALU.mult)
                        tt(tbuf(d, L + 1), T2[:, :, 0], T2[:, :, 1], ALU.mult).then_inc(scan_ready[l][d], 1)
                        if L == 0:
                            dve.wait_ge(diag_ev[l][d], nt // 4)
                        else:
                            dve.wait_ge(lvl_ev[l][d], L * (nt // 8))
                        for g in range(nt // 8):
                            bk = B[2 + 2 * (L % 2) + g]
                            av = A3[:, t0 + 8 * g:t0 + 8 * g + 8, :].rearrange("p t (s b m) -> p t s b m", b=2, m=m)[:, :, :, qh, :]
                            mv = msk[:, d, L, :].unsqueeze(1).broadcast_to((128, 8, 64)).rearrange("p t (s m) -> p t s m", m=m)
                            dv = bk[:].rearrange("p (t s m) -> p t s m", t=8, m=m)
                            nc.vector.copy_predicated(av, mv, dv).then_inc(lvl_ev[l][d], 1)
                        fill(L)

                def fill0(L):
                    if L < 4:
                        gates_one(L)
                    else:
                        los(2 if L == LEVELS - 1 else 1)

                def gates_one(hh):
                    dve.wait_ge(proj_ev[l], 8 + hh + 1)
                    fv = f_t[1].rearrange("p (c h n) -> p c h n", c=NCH, h=HEADS)[:, :, hh, :]
                    nc.vector.tensor_scalar(fv, fv, lb1[:, l, HEADS + hh:HEADS + hh + 1],
                                            lb[:, l, HEADS + hh:HEADS + hh + 1], ALU.mult, ALU.add).then_inc(dve_step, 1)
                    link.n += 1
                    los(1)

                scan(0, fill0)

                def states(d):
                    T = tbuf(d, LEVELS)
                    for g in range(3):
                        dve.wait_ge(st_mm[l][d], g + 1)
                        bk = B[(5, 2, 3)[g]]
                        if g == 0:
                            ins = nc.vector.tensor_copy(s_t[:, 0], bk[:].rearrange("p (h n) -> p h n", h=HEADS))
                        else:
                            c = order[d][g]
                            for hh in range(HEADS):
                                ins = nc.vector.scalar_tensor_tensor(s_t[:, g, hh], s_t[:, g - 1, hh],
                                                                     T[:, c * HEADS + hh:c * HEADS + hh + 1],
                                                                     bk[:, hh * 128:(hh + 1) * 128], ALU.mult, ALU.add)
                        ins.then_inc(st_ev[l][d], 1)
                        dve.wait_ge(st_ev[l][d], g + 1)

                states(0)
                for g in range(4):
                    dve.wait_ge(pool_hi[l], g + 1)
                    nc.vector.scalar_tensor_tensor(u_lo[:, 4 + g, c0:], B[g % 2][:, c0:],
                                                   vec[:, V_PSC + 4 * l + g:V_PSC + 4 * l + g + 1],
                                                   u_hi[:, 4 + g, c0:].bitcast(f32), ALU.mult,
                                                   ALU.subtract).then_inc(pool_lo[l], 1)
                dve.wait_ge(o_mm[l][0], len(outs_ch[l]))
                start(1)
                scan(1, lambda L: None)
                states(1)
                for k, c in enumerate(outs_ch[l]):
                    dve.wait_ge(o_mm[l][1], k + 1)
                    dve.wait_ge(o_ev[l][0], k + 1)
                    ov = o_t[:, :, c * 128:(c + 1) * 128]
                    tt(ov, ov, B[2 + c][:].rearrange("p (h n) -> p h n", h=HEADS), ALU.add).then_inc(o_ev[l][1], 1)
                for hh in range(HEADS):
                    dve.wait_ge(oms[l], hh + 1)
                    link(nc.vector.tensor_scalar(rr[:, hh, c0:], B[2 + hh][:, c0:], EPS, None, ALU.add))
                    nc.vector.reciprocal(rr[:, hh, c0:], rr[:, hh, c0:]).then_inc(oinv[l], 1)
                dve.wait_ge(orstd[l], 1)
                for hh in range(HEADS):
                    w = vec[:, V_HNW + HEADS * l + hh:V_HNW + HEADS * l + hh + 1]
                    link(nc.vector.scalar_tensor_tensor(a32[:, hh, c0:], o_t[:, hh, c0:], w, rr[:, hh, c0:],
                                                        ALU.mult, ALU.mult))
                    tt(a32[:, hh, c0:], a32[:, hh, c0:], sg[:, hh, c0:], ALU.mult).then_inc(a_f[l], 1)
                for hh in range(HEADS):
                    dve.wait_ge(a_hi[l], hh + 1)
                    tt(u_lo[:, hh, c0:], a32[:, hh, c0:], u_hi[:, hh, c0:].bitcast(f32), ALU.subtract).then_inc(a_lo[l], 1)
                for kt in range(KT):
                    dve.wait_ge(sub_used, S0[f"wo{l}"] + kt + 1)
                    gated(FFN[l], l, 2, kt, B[kt % 2][:], c0)
                    los(1)

            mixer(0)
            norm(FFN[0], 0, 0, 1)

            def ffn_block(i, b):
                dve.wait_ge(sil_ready, i * 2 + (b + 1))
                dve.wait_ge(sub_used, i * 4 + (S0["ffn"] + 2 * b + 2))
                dst = hid[:, 2 * i + b, :] if isinstance(i, int) else \
                    hid[:, bass.ds(i * 2 + b, 1), :].rearrange("p f n -> p (f n)")
                tt(dst, sil[:, b, :], B[2 * b + 1][:], ALU.mult).then_inc(hid_ready, 1)

            for b in range(2):
                ffn_block(0, b)
                los(2)
            j0 = nxt[0]
            with dve.Fori(1, FFN_IT - 1) as i:
                for b in range(2):
                    ffn_block(i, b)
                    for k in range(2):
                        jj = S0["ffn"] + 4 + 2 * b + k
                        u = U0["ffn"] + 4 + k
                        dve.wait_ge(hi_done, i * 4 + (jj + 1))
                        tt(shaped(w_lo[:, jj % NS, :], 1), half_of(raw[:, u % NR, :], b, 1),
                           shaped(w_hi[:, jj % NS, :], 1).bitcast(f32), ALU.subtract).then_inc(lo_done, 1)
            nxt[0] = j0 + 4 * (FFN_IT - 2)
            for b in range(2):
                ffn_block(FFN_IT - 1, b)
                los(2)
            modulation(1)
            for f in range(22):
                dve.wait_ge(hs_hi, f + 1)
                tt(u_lo[:, f % KT, :], hid[:, f, :], u_hi[:, f % KT, :].bitcast(f32), ALU.subtract).then_inc(hs_lo, 1)
                if f >= KT:
                    los(1)
            for f in range(KT - 1):
                los(1)
            for kt in range(KT):
                if kt < KT - 1:
                    dve.wait_ge(down_mm, kt + 1)
                else:
                    dve.wait_ge(sub_used, S0["down"] + 22)
                gated(MIX[1], 0, 5, kt, B[kt][:], 0)
            los(1)
            mixer(1)

            norm(FFN[1], CTX, target=True)
            for kt in range(KT):
                link(tt(v32[:, kt, :], h[:, kt, CTX:], rstd[:, CTX:], ALU.mult))
                nc.vector.tensor_scalar(v32[:, kt, :], v32[:, kt, :], gain[:, 1, 1, kt, 1:2],
                                        mod[:, 1, 3 * KT + kt, 1:2], ALU.mult, ALU.add).then_inc(hn_ready, 1)
            for g in range(4):
                nc.vector.memset(yacc[:, 2 * g:2 * g + 2, :], 0.0).then_inc(sc_ev, 1)
            nc.vector.memset(msil, 0.0).then_inc(mh_ready, 1)
            dve.wait_ge(rt_mm, 1)
            link(nc.vector.tensor_copy(r_log, B[0][:, 0:16]))
            for c in range(2):
                link(nc.vector.max(r_top[:, 8 * c:8 * c + 8], r_log[:, 8 * c:8 * c + 8]))
                link(nc.vector.max_index(r_idx[:, 8 * c:8 * c + 8], r_top[:, 8 * c:8 * c + 8], r_log[:, 8 * c:8 * c + 8]))
            link(nc.vector.tensor_copy(r_idf, r_idx))
            for c in range(2):
                ins = tt(r_d[:, c:c + 1], r_top[:, 8 * c + 1:8 * c + 2], r_top[:, 8 * c:8 * c + 1], ALU.subtract)
            ins.then_inc(rt_in, 1)
            for c in range(2):
                for k in range(2):
                    link(nc.vector.tensor_scalar(r_m[:, k, 8 * c:8 * c + 8], e_iota, r_idf[:, 8 * c + k:8 * c + k + 1],
                                                 None, ALU.is_equal))
            tt(r_mask, r_m[:, 0], r_m[:, 1], ALU.add).then_inc(mask_ready, 1)
            dve.wait_ge(e_ready, 2)
            link(nc.vector.tensor_scalar(r_w[:, 0:2], r_e, 1.0, None, ALU.add))
            link(nc.vector.reciprocal(r_w[:, 0:2], r_w[:, 0:2]))
            link(tt(r_w[:, 2:4], r_e, r_w[:, 0:2], ALU.mult))
            for c in range(2):
                s = slice(8 * c, 8 * c + 8)
                link(nc.vector.tensor_scalar(r_comb[:, s], r_m[:, 0, s], r_w[:, c:c + 1], None, ALU.mult))
                link(nc.vector.scalar_tensor_tensor(r_comb[:, s], r_m[:, 1, s], r_w[:, 2 + c:3 + c], r_comb[:, s],
                                                    ALU.mult, ALU.add))
            dve.wait_ge(pos_mm, 1)
            link(nc.vector.scalar_tensor_tensor(r_pos, B[1][:, 0:16], 1.0, r_mask, ALU.add, ALU.mult))
            link(nc.vector.tensor_scalar(r_pos, r_pos, -1.0, None, ALU.add))
            link(nc.vector.tensor_reduce(r_w[:, 0:1], B[1][:, 16:24], AX.X, ALU.max))
            link(nc.vector.tensor_scalar(r_w[:, 1:2], r_w[:, 0:1], SLOTS + 0.5, 1.0, ALU.is_gt, ALU.add))
            nc.vector.tensor_copy(npass_i[:], r_w[:, 1:2]).then_inc(route_ready, 1)
            dve.wait_ge(route_ready, 1)
            npass = dve.value_load(npass_i[0:1, 0:1], min_val=1, max_val=2)
            with dve.Fori(0, npass) as ps:
                with dve.Fori(0, NE) as e:
                    it = ps * NE + e

                    def mlo(s):
                        n = s // 2
                        dve.wait_ge(hi_done, it * MOE_S + (S0["moe"] + s + 1))
                        slot = (S0["moe"] + s) % NS
                        tt(w_lo[:, slot, :], half_of(m_slot(n % NRM), s % 2, 0), w_hi[:, slot, :].bitcast(f32),
                           ALU.subtract).then_inc(lo_done, 1)

                    for c in range(2):
                        at = r_pos[:, bass.ds(e + 8 * c, 1)]
                        nc.vector.tensor_scalar(pbuf[:, c, :], slot_iota, at, None, ALU.is_equal)
                        ins = nc.vector.tensor_scalar(pw[:, c, :], slot_iota, at, r_comb[:, bass.ds(e + 8 * c, 1)],
                                                      ALU.is_equal, ALU.mult)
                    ins.then_inc(p_ready, 1)
                    for s in range(NS):
                        mlo(s)
                    for g in range(2):
                        dve.wait_ge(xg_h, it * 2 + (g + 1))
                        tt(xg_lo[:, 4 * g:4 * g + 4, :].rearrange("p k n -> p (k n)"), B[4 + g][:],
                           xg_hi[:, 4 * g:4 * g + 4, :].rearrange("p k n -> p (k n)").bitcast(f32),
                           ALU.subtract).then_inc(xg_l, 1)
                    for s in range(MOE_S):
                        for what, c in M_EVENTS.get(s, ()):
                            if what == "up":
                                dve.wait_ge(msil_ready, it * FC + (c + 1))
                                dve.wait_ge(sub_used, it * MOE_S + (S0["moe"] + s + 1))
                                tt(mh[:, c % 2, :], msil, B[2 * (c % 2) + 1][:], ALU.mult).then_inc(mh_ready, 1)
                            elif what == "ht":
                                dve.wait_ge(ht_h, it * FC + (c + 1))
                                tt(ht_lo[:, c % 2, :], B[4 + c % 2][:], ht_hi[:, c % 2, :].bitcast(f32),
                                   ALU.subtract).then_inc(ht_l, 1)
                        if s + NS < MOE_S:
                            mlo(s + NS)
                    dve.wait_ge(sub_used, it * MOE_S + (S0["moe"] + MOE_S))
                    nc.vector.tensor_copy(ybuf[:, 512:1024], B[7][:]).then_inc(y_ev, 1)
                    for g in range(4):
                        dve.wait_ge(sc_mm, it * 4 + (g + 1))
                        ya = yacc[:, 2 * g:2 * g + 2, :]
                        tt(ya, ya, B[g][:].rearrange("p (k n) -> p k n", k=2), ALU.add).then_inc(sc_ev, 1)
                nc.vector.tensor_scalar(slot_iota, slot_iota, float(SLOTS), None, ALU.add).then_inc(slot_step, 1)
                dve.wait_ge(slot_step, ps + 1)
            for kt in range(KT):
                gated(4, 1, 5, kt, yacc[:, kt, :], CTX)
            norm(4, CTX, target=True)
            for kt in range(KT):
                nc.vector.scalar_tensor_tensor(v32[:, kt, :], h[:, kt, CTX:], vec[:, V_FIN + kt:V_FIN + kt + 1],
                                               rstd[:, CTX:], ALU.mult, ALU.mult).then_inc(hn_ready, 1)
            for g in range(2):
                dve.wait_ge(out_tr, 2 * g + 2)
                nc.vector.tensor_copy(osb[:, g, 512:1024], B[3 + 2 * g][:]).then_inc(out_ev, 1)

        @block.tensor
        def _(pe):
            nxt = [0]
            mm = nc.tensor.matmul

            def wsub(j):
                return w_hi[:, j % NS, :], w_lo[:, j % NS, :]

            def mm3(out, lh, ll, rh, rl, start, stop):
                mm(out, lh, rh, start=start, stop=False)
                mm(out, lh, rl, start=False, stop=False)
                return mm(out, ll, rh, start=False, stop=stop)

            def norm(n, c0):
                pe.wait_ge(ones_ready, 3)
                for kt in range(KT):
                    pe.wait_ge(sq_ready, KT * n + kt + 1)
                    mm(B[6][:, c0:], ones_d[:], sq[:, kt % 2, c0:], start=(kt == 0), stop=(kt == KT - 1)).then_inc(sq_used, 1)

            pe.wait_ge(vec_in, 32)
            pe.wait_ge(const_in, 32)
            nc.tensor.transpose(B[6][:, 0:96], vrow[0:96, 0, :], ident[0:96, 0:96]).then_inc(vec_tr, 1)
            nc.tensor.transpose(B[6][:, 96:184], vrow[0:88, 1, :], ident[0:88, 0:88]).then_inc(vec_tr, 1)

            def ada_unit(slot, col, dyn):
                w = raw[:, slot, :].rearrange("p (k n) -> p k n", k=KT)
                for b in range(2):
                    o = B[7][:, bass.ds(col + 2 * b, 2)] if dyn else B[7][:, col + 2 * b:col + 2 * b + 2]
                    for kt in range(KT):
                        ins = mm(o, w[:, kt, b * 128:(b + 1) * 128], silu_c[:, kt, :], start=(kt == 0), stop=(kt == KT - 1))
                return ins

            pe.wait_ge(silu_ready, 1)
            for k in range(4):
                pe.wait_ge(raw_in[k], 16)
                ada_unit(k, 4 * k, False).then_inc(direct_used, 1)
            pe.wait_ge(x_in, 32)
            for kt in range(KT):
                if kt >= 6:
                    pe.wait_ge(h_ready, KT * 0 + kt - 5)
                for c in range(NCH):
                    ins = nc.tensor.transpose(B[kt % 6][:, c * 128:(c + 1) * 128], xin[:, c, kt * 128:(kt + 1) * 128], ident)
                ins.then_inc(x_tr, 1)
            with pe.Fori(1, 6) as i:
                for k in range(4):
                    pe.wait_ge(raw_in[k], i * 16 + 16)
                    ada_unit(k, i * 16 + 4 * k, True).then_inc(direct_used, 1)

            def take_sub():
                j = nxt[0]
                nxt[0] += 1
                pe.wait_ge(lo_done, j + 1)
                return j

            def token_major(l, chunks, n):
                for k in range(4):
                    j = take_sub()
                    wh, wl = (w.rearrange("p (k n) -> p k n", k=2) for w in wsub(j))
                    for kk in range(2):
                        kt = 2 * k + kk
                        pe.wait_ge(u_ready, KT * n + kt + 1)
                        for c in chunks:
                            t = slice(c * 128, (c + 1) * 128)
                            ins = mm3(B[2 + c][:], u_hi[:, kt, t], u_lo[:, kt, t], wh[:, kk], wl[:, kk], kt == 0, kt == KT - 1)
                    ins.then_inc(sub_used, 1)

            def block_fm(bank, c0):
                j = take_sub()
                wh, wl = (w.rearrange("p (k n) -> p k n", k=KT) for w in wsub(j))
                for kt in range(KT):
                    mm3_(bank[:, c0:], wh[:, kt], wl[:, kt], kt, c0)
                last[0].then_inc(sub_used, 1)

            last = [None]

            def mm3_(out, wh, wl, kt, c0):
                last[0] = mm3(out, wh, wl, u_hi[:, kt, c0:], u_lo[:, kt, c0:], kt == 0, kt == KT - 1)

            def mixer(l):
                n, c0 = MIX[l], c0s[l]
                TL = tiles(l)
                t0, nt = TL[0], len(TL)
                norm(n, 0)
                token_major(l, outs_ch[l], n)
                blk = [0]

                def proj_block(cc):
                    if blk[0] >= 2:
                        pe.wait_ge(proj_ev[l], blk[0] - 1)
                    block_fm(B[blk[0] % 2], cc)
                    blk[0] += 1

                for _ in range(4):
                    proj_block(0)
                for _ in range(4):
                    proj_block(c0)
                pe.wait_ge(pv_ev[l], len(outs_ch[l]))
                token_major(l, range(NCH), n)

                def scan(d, fill):
                    qh, kh = (1, 0) if d == 0 else (0, 1)
                    pe.wait_ge(scan_ready[l][d], 1)
                    if d == 0:
                        pe.wait_ge(i_ev[l], NCH)
                    for g in range(nt // 4):
                        for t in range(4):
                            ti = TL[4 * g + t]
                            ins = mm(B[2 + g][:, t * 128:(t + 1) * 128], ks[:, ti * 128:(ti + 1) * 128],
                                     q_t[:, ti * 128:(ti + 1) * 128], start=True, stop=True)
                        ins.then_inc(diag_mm[l][d], 1)
                    pe.wait_ge(diag_ev[l][d], nt // 4)
                    for L in range(LEVELS):
                        m = 1 << L
                        pe.wait_ge(scan_ready[l][d], L + 1)
                        if L >= 2:
                            pe.wait_ge(lvl_ev[l][d], (L - 1) * (nt // 8))
                        for g in range(nt // 8):
                            for t in range(8):
                                ti = TL[8 * g + t]
                                ins = mm(B[2 + 2 * (L % 2) + g][:, t * 64:(t + 1) * 64], ks[:, ti * 128:(ti + 1) * 128],
                                         seg(qp, ti, 1, m, qh), start=True, stop=True)
                            ins.then_inc(lvl_mm[l][d], 1)
                        fill(L)
                    pe.wait_ge(scan_ready[l][d], LEVELS + 1)
                    pe.wait_ge(lvl_ev[l][d], LEVELS * (nt // 8))
                    for g in range(3):
                        for hh in range(HEADS):
                            ti = order[d][g] * HEADS + hh
                            ins = nc.tensor.transpose(B[2 + g][:, hh * 128:(hh + 1) * 128], ks[:, ti * 128:(ti + 1) * 128], ident)
                        ins.then_inc(kst_tr[l][d], 1)
                    for g in range(3):
                        c = order[d][g]
                        pe.wait_ge(kst_ev[l][d], g + 1)
                        for hh in range(HEADS):
                            ti = c * HEADS + hh
                            ins = mm(B[(5, 2, 3)[g]][:, hh * 128:(hh + 1) * 128], ks[:, ti * 128:(ti + 1) * 128],
                                     v_t[:, c, hh * 128:(hh + 1) * 128], start=True, stop=True)
                        ins.then_inc(st_mm[l][d], 1)
                    pe.wait_ge(st_ev[l][d], 3)
                    if d == 1:
                        pe.wait_ge(pool_lo[l], 4)
                    for c in outs_ch[l]:
                        pos = order[d].index(c)
                        for hh in range(HEADS):
                            ti = c * HEADS + hh
                            o = B[2 + c][:, hh * 128:(hh + 1) * 128]
                            ins = mm(o, v_t[:, c, hh * 128:(hh + 1) * 128], amat[:, ti * 128:(ti + 1) * 128],
                                     start=True, stop=(pos == 0))
                            if pos:
                                ins = mm(o, s_t[:, pos - 1, hh, :], qp[:, ti * 128:(ti + 1) * 128], start=False, stop=True)
                        ins.then_inc(o_mm[l][d], 1)

                def fill0(L):
                    proj_block(0 if L < 4 else c0)
                    if L == LEVELS - 1:
                        proj_block(c0)

                scan(0, fill0)
                u0 = U0[f"pm{l}"]
                for k in range(2 - l):
                    pe.wait_ge(raw_in[(u0 + k) % NR], 16 * ((u0 + k) // NR + 1))
                pe.wait_ge(wp_in, 16 * (l + 1))
                pe.wait_ge(proj_ev[l], 16)
                pe.wait_ge(o_ev[l][0], len(outs_ch[l]))
                for g in range(4):
                    for side in ([0, 1] if l == 0 else [1]):
                        mat = raw[:, (u0 + side - l) % NR, :].rearrange("p (s g n) -> p s g n", s=2, g=4)
                        for s in range(2):
                            ins = mm(B[2 + g][:, side * 256:(side + 1) * 256], pv[:, 2 * side + s, g * 128:(g + 1) * 128],
                                     mat[:, s, g, :], start=(s == 0), stop=(s == 1))
                    ins.then_inc(diff_mm[l], 1)
                    if g >= 1:
                        pool_block(l, g - 1, c0)
                pool_block(l, 3, c0)
                scan(1, lambda L: None)
                pe.wait_ge(o_ev[l][1], len(outs_ch[l]))
                for hh in range(HEADS):
                    pe.wait_ge(osq[l], hh + 1)
                    mm(B[2 + hh][:, c0:], ones_hd[:], sq_o[:, hh, c0:], start=True, stop=True).then_inc(oms[l], 1)
                pe.wait_ge(a_lo[l], HEADS)
                pe.wait_ge(pool_lo[l], 4)
                for j in range(8):
                    if j >= 2:
                        pe.wait_ge(h_ready, KT * FFN[l] + j - 1)
                    block_fm(B[j % 2], c0)

            def pool_block(l, g, c0):
                pe.wait_ge(diff_ev[l], g + 1)
                if g >= 2:
                    pe.wait_ge(pool_lo[l], g - 1)
                mm(B[g % 2][:, c0:], wp[:, g, :], diff[:, g % 2, c0:], start=True, stop=True).then_inc(pool_mm[l], 1)

            mixer(0)
            norm(FFN[0], 0)
            base = S0["ffn"]

            def ffn_step(i, dyn):
                for b in range(2):
                    for k in range(2):
                        jj = base + 2 * b + k
                        pe.wait_ge(lo_done, i * 4 + (jj + 1))
                        if k == 0 and (dyn or i > 0):
                            pe.wait_ge(hid_ready, i * 2 + (b - 1))
                        wh, wl = (w.rearrange("p (k n) -> p k n", k=KT) for w in wsub(jj))
                        for kt in range(KT):
                            if not dyn and i == 0 and b == 0 and k == 0:
                                pe.wait_ge(u_ready, KT * FFN[0] + kt + 1)
                            mm3_(B[2 * b + k][:], wh[:, kt], wl[:, kt], kt, 0)
                        last[0].then_inc(sub_used, 1)
                for k in range(2):
                    u = U0["ffn"] + 2 + k
                    pe.wait_ge(raw_in[u % NR], i * 16 + 16 * (u // NR + 1))
                    ada_unit(u % NR, i * 8 + 4 * k, dyn).then_inc(direct_used, 1)

            pe.wait_ge(h_ready, KT * FFN[0] + KT)
            ffn_step(0, False)
            with pe.Fori(1, FFN_IT - 1) as i:
                ffn_step(i, True)
            ffn_step(FFN_IT - 1, False)
            nxt[0] = S0["down"]
            for k in range(2):
                u = U0["ada1"] + k
                pe.wait_ge(raw_in[u % NR], 16 * (u // NR + 1))
                ada_unit(u % NR, 8 * FFN_IT + 4 * k, False).then_inc(direct_used, 1)
            pe.wait_ge(hid_ready, 22)
            for f in range(22):
                j = take_sub()
                wh, wl = wsub(j)
                pe.wait_ge(hs_lo, f + 1)
                if f == 0:
                    pe.wait_ge(mod_ready, 2)
                for d in range(KT):
                    dd = slice(d * 128, (d + 1) * 128)
                    ins = mm3(B[d][:], wh[:, dd], wl[:, dd], u_hi[:, f % KT, :], u_lo[:, f % KT, :], f == 0, f == 21)
                    if f == 21 and d < KT - 1:
                        ins.then_inc(down_mm, 1)
                ins.then_inc(sub_used, 1)
            pe.wait_ge(h_ready, KT * MIX[1] + KT)
            mixer(1)
            pe.wait_ge(h_ready, KT * FFN[1] + KT)
            norm(FFN[1], CTX)
            pe.wait_ge(rw_in, 16)
            pe.wait_ge(hn_ready, KT * 3 + KT)
            for c in range(2):
                for kt in range(KT):
                    ins = mm(B[0][:, 8 * c:8 * c + 8], v32[:, kt, c * 128:(c + 1) * 128], rt[:, kt * 8:kt * 8 + 8],
                             start=(kt == 0), stop=(kt == KT - 1))
            ins.then_inc(rt_mm, 1)
            for g in range(4):
                for k in range(4):
                    kt = 4 * (g % 2) + k
                    ins = nc.tensor.transpose(B[2 + g][:, k * 128:(k + 1) * 128], v32[:, kt, (g // 2) * 128:(g // 2 + 1) * 128], ident)
                ins.then_inc(vtok_tr, 1)
            pe.wait_ge(mask_ready, 1)
            mm(B[1][:, 0:8], tri, r_mask[:, 0:8], start=True, stop=True)
            mm(B[1][:, 8:16], tri, r_mask[:, 8:16], start=True, stop=False)
            mm(B[1][:, 8:16], ones[:], r_mask[:, 0:8], start=False, stop=True)
            mm(B[1][:, 16:24], ones[:], r_mask[:, 0:8], start=True, stop=False)
            mm(B[1][:, 16:24], ones[:], r_mask[:, 8:16], start=False, stop=True).then_inc(pos_mm, 1)
            pe.wait_ge(vtok_ev, 4)
            pe.wait_ge(route_ready, 1)
            npass = pe.value_load(npass_i[0:1, 0:1], min_val=1, max_val=2)
            S_M = S0["moe"]
            with pe.Fori(0, npass) as ps:
                with pe.Fori(0, NE) as e:
                    it = ps * NE + e
                    pe.wait_ge(p_ready, it + 1)
                    for g in range(2):
                        for k in range(4):
                            kt = 4 * g + k
                            for c in range(2):
                                ins = mm(B[4 + g][:, k * 128:(k + 1) * 128], vtok[:, c, kt * 128:(kt + 1) * 128],
                                         pbuf[:, c, :], start=(c == 0), stop=(c == 1))
                        ins.then_inc(xg_mm, 1)
                    pe.wait_ge(sc_ev, it * 4 + 4)
                    for c in range(2):
                        ins = nc.tensor.transpose(B[3][:, c * 128:(c + 1) * 128], pw[:, c, :], ident)
                    ins.then_inc(pwt_tr, 1)
                    for g in range(2):
                        pe.wait_ge(xg_l, it * 2 + (g + 1))

                    def hidden_tr(c):
                        pe.wait_ge(mh_ready, it * FC + (c + 2))
                        for k in range(4):
                            ins = nc.tensor.transpose(B[4 + c % 2][:, k * 128:(k + 1) * 128],
                                                      mh[:, c % 2, k * 128:(k + 1) * 128], ident)
                        ins.then_inc(ht_tr, 1)

                    s = 0
                    for n, (kind, c, b) in enumerate(MOE_ORDER):
                        if b == 0 and kind == "u" and c >= 1:
                            hidden_tr(c - 1)
                        if b == 0 and kind == "u" and c == 1:
                            pe.wait_ge(pwt_ev, it + 1)
                        if b == 0 and kind == "d":
                            if c == FC - 1:
                                hidden_tr(c)
                            pe.wait_ge(ht_l, it * FC + (c + 1))
                        for half in range(2):
                            pe.wait_ge(lo_done, it * MOE_S + (S_M + s + 1))
                            wh, wl = wsub(S_M + s)
                            if kind == "d":
                                ft = 2 * b + half
                                lh, ll = (w[:, c % 2, ft * 128:(ft + 1) * 128] for w in (ht_hi, ht_lo))
                                first, final = (c == 0 and ft == 0), (c == FC - 1 and ft == 3)
                                for nb in range(2):
                                    cc = slice(nb * 512, (nb + 1) * 512)
                                    mm(B[6 + nb][:], lh, wh[:, cc], start=first, stop=False)
                                    mm(B[6 + nb][:], lh, wl[:, cc], start=False, stop=False)
                                for nb in range(2):
                                    ins = mm(B[6 + nb][:], ll, wh[:, nb * 512:(nb + 1) * 512], start=False, stop=final)
                            else:
                                bank = B[2 * (c % 2) + (kind == "u")]
                                for kk in range(2):
                                    kt = 4 * b + 2 * half + kk
                                    ins = mm3(bank[:], xg_hi[:, kt, :], xg_lo[:, kt, :], wh[:, kk * 512:(kk + 1) * 512],
                                              wl[:, kk * 512:(kk + 1) * 512], kt == 0, kt == KT - 1)
                            ins.then_inc(sub_used, 1)
                            s += 1
                    pe.wait_ge(y_ev, it * 2 + 2)
                    for g in range(4):
                        for k in range(2):
                            kt = 2 * g + k
                            ins = mm(B[g][:, k * 256:(k + 1) * 256], ybuf[:, kt * 128:(kt + 1) * 128], pwt, start=True, stop=True)
                        ins.then_inc(sc_mm, 1)
            norm(4, CTX)
            pe.wait_ge(hn_ready, KT * 4 + KT)
            for c in range(2):
                for g in range(2):
                    for k in range(4):
                        ins = nc.tensor.transpose(B[2 + 2 * c + g][:, k * 128:(k + 1) * 128],
                                                  v32[:, 4 * g + k, c * 128:(c + 1) * 128], ident)
                    ins.then_inc(out_tr, 1)


def pooling_matrices():
    import numpy as np
    def line(n, k):
        m = np.zeros((n, n))
        for t in range(n):
            lo, hi = max(t - k // 2, 0), min(t + k - 1 - k // 2 + 1, n)
            m[lo:hi, t] = 1.0 / (hi - lo)
        return m
    mats = np.zeros((2, 256, 4, 256))
    for g, k in enumerate((2, 4, 8, 16)):
        mats[0, :, g, :] = line(CTX, k) - np.eye(CTX)
        mats[1, :, g, :] = np.kron(line(LAT // 64, k), line(64, k)) - np.eye(LAT)
    return np.ascontiguousarray(mats.reshape(2, 2, 128, 4, 256).transpose(0, 2, 1, 3, 4), dtype=np.float32)


def level_masks():
    import numpy as np
    out = np.zeros((128, 2, LEVELS, 64), np.float32)
    s = np.arange(128)[:, None]
    t = np.arange(64)[None, :]
    for L in range(LEVELS):
        m = 1 << L
        same = (s // (2 * m)) == (t // m)
        out[:, 0, L] = same & ((s // m) % 2 == 0)
        out[:, 1, L] = same & ((s // m) % 2 == 1)
    return out.reshape(128, -1)


def kernel(**inputs):
    import numpy as np
    import concourse.bacc as bacc
    from concourse.bass_utils import run_bass_kernel_spmd

    a = {k: np.ascontiguousarray(v) for k, v in inputs.items()}
    rows = lambda v: v.reshape(-1, 128)
    vecs = np.concatenate([rows(a["b_ada"]), rows(a["norm_w"]), rows(a["hgrn_lb_raw"]), rows(a["hgrn_norm_w"]),
                           rows(a["pool_scale"]), rows(a["final_norm_w"]), rows(a["c_ctx"]), rows(a["c"])])
    i = np.arange(128)
    cf32 = np.concatenate([np.eye(128), (i[:, None] < i[None, :]), np.tile(i, (128, 1)),
                           np.tile(np.arange(8), (128, 1))], axis=1).astype(np.float32)
    ins = [("x", a["x"][0]), ("ctx_in", a["ctx"][0]), ("vecs", vecs), ("w_ada", a["w_ada"]), ("w_in", a["w_in"]),
           ("w_pool", a["w_pool"]), ("w_out", a["w_out"]), ("ffn_wg", a["ffn_wg"][0]), ("ffn_wu", a["ffn_wu"][0]),
           ("ffn_wd", a["ffn_wd"][0]), ("router_w", a["router_w"][0]), ("moe_wg", a["moe_wg"][0]),
           ("moe_wu", a["moe_wu"][0]), ("moe_wd", a["moe_wd"][0]), ("cf32", cf32),
           ("pool_mats", pooling_matrices()), ("masks", level_masks())]
    nc = bacc.Bacc("TRN2", target_bir_lowering=False, num_devices=1)
    arrays, aps = {}, []
    for name, v in ins:
        arrays[f"in_{name}"] = v
        aps.append(nc.dram_tensor(f"in_{name}", v.shape, mybir.dt.from_np(v.dtype), kind="ExternalInput").ap())
    o = nc.dram_tensor("out_lat", (LAT, D), mybir.dt.float32, kind="ExternalOutput").ap()
    bass_hybrid_trunk(nc, *aps, o)
    r = run_bass_kernel_spmd(nc, [arrays], core_ids=[0])
    return r.results[0]["out_lat"].reshape(1, LAT, D)
```

```python
import concourse.bass as bass
from concourse import mybir
from contextlib import ExitStack

D = 1024
KT = D // 128
CTX = LAT = 256
NTOK = CTX + LAT
HEADS = 4
HD = 128
NCH = NTOK // 128
LEVELS = 7
NADA = 6
ADA_BLKS = NADA * KT
F_DENSE = 2816
F_EXP = 3584
NE = 8
DEPTH = 2
EPS = 1e-6
UNIT = 2048
SUB = UNIT // 2
NR = 4
NRM = 6
NS = 4
ADA_G = NADA * D // 512
FFN_SUBS = [(0, 0), (0, 1), (1, 0), (2, 0), (3, 0), (3, 1), (1, 1), (2, 1)]
FFN_FREE = [max(k for k, (u_, _) in enumerate(FFN_SUBS) if u_ == u) + 1 for u in range(4)]
FFN_IT = F_DENSE // 256
DOWN_U = F_DENSE // 256
FC = F_EXP // 512
SLOTS = 128
V_BADA, V_NORM, V_LB, V_HNW, V_PSC, V_FIN, V_C = 0, 96, 128, 144, 152, 160, 168
V_ROWS = 184


MOE_ORDER = [("g", 0, 0), ("g", 0, 1), ("u", 0, 0), ("u", 0, 1)]
for _c in range(1, FC):
    MOE_ORDER += [("g", _c, 0), ("g", _c, 1), ("u", _c, 0), ("u", _c, 1), ("d", _c - 1, 0), ("d", _c - 1, 1)]
MOE_ORDER += [("d", FC - 1, 0), ("d", FC - 1, 1)]
MOE_U = len(MOE_ORDER)
MOE_S = 2 * MOE_U
assert MOE_U % NRM == 0 and MOE_S % NS == 0


def plan():
    seq = [("ada0", 2 * ADA_G, "s")]
    for l in range(DEPTH):
        seq += [(f"pv{l}", 2, "s"), (f"f0{l}", 2, "s"), (f"q{l}", 2, "s"), (f"i{l}", 2, "s"),
                (f"f1{l}", 2, "s"), (f"g{l}", 2, "s"), (f"pm{l}", 2 - l, f"p{l}"), (f"wo{l}", 4, "s")]
        if l == 0:
            seq += [("ada1", 2, "s"), ("ffn", 4 * FFN_IT, "m"), ("down", DOWN_U, "s")]
    unit, sub, free = {}, {}, []
    u = s = 0
    for name, n, kind in seq:
        unit[name], sub[name] = u, s
        for i in range(n):
            if kind[0] == "p":
                free.append((kind, HEADS))
            elif kind == "m":
                free.append(("s", s + 8 * (i // 4) + FFN_FREE[i % 4]))
            else:
                free.append(("s", s + 2 * (i + 1)))
        s += 0 if kind[0] == "p" else 2 * n
        u += n
    unit["moe"], sub["moe"] = u, s
    return unit, sub, free


def bass_hybrid_trunk(nc, x, ctx_in, vecs, w_ada, w_in, w_pool, w_out, ffn_wg, ffn_wu, ffn_wd, router_w,
                      moe_wg, moe_wu, moe_wd, cf32, pool_mats, masks, out):
    f32, f32r, i32, ui32, u8 = (mybir.dt.float32, mybir.dt.float32r, mybir.dt.int32, mybir.dt.uint32,
                               mybir.dt.uint8)
    ACT = mybir.ActivationFunctionType
    ALU = mybir.AluOpType
    AX = mybir.AxisListType
    U0, S0, FREE = plan()

    st = ExitStack()
    with st:
        def sb(name, shape, dt=f32):
            return st.enter_context(nc.sbuf_tensor(name, shape, dt))

        def sem(name):
            return st.enter_context(nc.semaphore(name))

        h = sb("h", [128, KT, NTOK])
        raw = sb("raw", [128, NR, UNIT])
        w_hi = sb("w_hi", [128, NS, SUB], f32r)
        w_lo = sb("w_lo", [128, NS, SUB], f32r)
        u_hi = sb("u_hi", [128, KT, NTOK], f32r)
        u_lo = sb("u_lo", [128, KT, NTOK], f32r)
        cst = sb("cst", [128, 3 * 128 + 8])
        ident, tri, slot_iota, e_iota = cst[:, 0:128], cst[:, 128:256], cst[:, 256:384], cst[:, 384:392]
        ones = sb("ones", [128, 128])
        ones_d = sb("ones_d", [128, 128])
        ones_hd = sb("ones_hd", [128, 128])
        msk = sb("msk", [128, 2, LEVELS, 64], u8)
        vec = sb("vec", [128, V_ROWS])
        silu_c = sb("silu_c", [128, KT, 2])
        c4 = sb("c4", [128, KT, 128], f32r)
        sel = sb("sel", [4, 2])
        stat = sb("stat", [128, NCH * HEADS])
        mod = sb("mod", [128, 2, ADA_BLKS, 2])
        gain = sb("gain", [128, 2, 2, KT, 2])
        lb = sb("lb", [128, 2, 2 * HEADS])
        lb1 = sb("lb1", [128, 2, 2 * HEADS])
        lbt = sb("lbt", [128, 4, 8])
        wp = sb("wp", [128, 4, 128])
        eps_t = sb("eps_t", [128, 1])
        ARENA = 20992
        arena = sb("arena", [128, ARENA])
        top = [0]

        def take(n, at=None):
            if at is None:
                at = top[0]
                top[0] += n
            assert at + n <= ARENA
            return at

        a_q, a_f0, a_f1, a_t2 = take(2048), take(2048), take(2048), take(1024)
        a_qp, a_ks, a_a, a_v = take(2048), take(2048), take(2048), take(2048)
        a_sg, a_pv, a_s = take(2048), take(2048), take(1536)

        def ar(at, n):
            return arena[:, at:at + n]

        q_t = ar(a_q, 2048)
        f_t = [ar(a_f0, 2048), ar(a_f1, 2048)]
        t2 = ar(a_t2, 1024)
        qp, ks, amat = ar(a_qp, 2048), ar(a_ks, 2048), ar(a_a, 2048)
        v_t = ar(a_v, 2048).rearrange("p (c n) -> p c n", c=NCH)
        sg = ar(a_sg, 2048).rearrange("p (h n) -> p h n", h=HEADS)
        pv = ar(a_pv, 2048).rearrange("p (c n) -> p c n", c=NCH)
        s_t = ar(a_s, 1536).rearrange("p (c h n) -> p c h n", c=3, h=HEADS)
        o_t = ar(a_f0, 2048).rearrange("p (h n) -> p h n", h=HEADS)
        diff = ar(a_t2, 1024).rearrange("p (b n) -> p b n", b=2)
        odiag = ar(a_qp, 2048).rearrange("p (h c n) -> p h c n", h=HEADS, n=128)
        sq_o = ar(a_ks, 2048).rearrange("p (h n) -> p h n", h=HEADS)
        a32 = ar(a_a, 2048).rearrange("p (h n) -> p h n", h=HEADS)
        sq = ar(a_sg, 1024).rearrange("p (b n) -> p b n", b=2)
        u32 = ar(a_pv, 2048).rearrange("p (b n) -> p b n", b=4)
        ndiag = ar(a_v, 512).rearrange("p (c n) -> p c n", n=128)
        row = ar(a_s, 1024).rearrange("p (b n) -> p b n", b=2)
        vrow = ar(a_q, 256).rearrange("p (b n) -> p b n", b=2)
        xin = ar(a_qp, 4096).rearrange("p (c n) -> p c n", c=NCH)
        msk_in = ar(a_sg, 2 * LEVELS * 64)
        a_hid = 0
        hid = ar(a_hid, 22 * NTOK).rearrange("p (f n) -> p f n", f=22)
        sil = ar(22 * NTOK, 1024).rearrange("p (b n) -> p b n", b=2)
        assert 22 * NTOK + 1024 <= a_v
        mraw = ar(0, 2 * UNIT).rearrange("p (b n) -> p b n", b=2)
        m0 = 2 * UNIT
        v32 = ar(m0, 2048).rearrange("p (k n) -> p k n", k=KT)
        vtok = ar(m0 + 2048, 2048).rearrange("p (c n) -> p c n", c=2)
        yacc = ar(m0 + 4096, 2048).rearrange("p (k n) -> p k n", k=KT)
        ybuf = ar(m0 + 6144, 1024)
        assert m0 + 7168 <= a_v
        m1 = a_v + 512
        msil = ar(m1, 512)
        mh = ar(m1 + 512, 1024).rearrange("p (b n) -> p b n", b=2)
        assert m1 + 1536 <= a_sg
        m2 = a_sg + 1024
        pbuf = ar(m2, 256).rearrange("p (c n) -> p c n", c=2)
        pw = ar(m2 + 256, 256).rearrange("p (c n) -> p c n", c=2)
        pwt = ar(m2 + 512, 256)
        rt = ar(m2 + 768, 256)
        assert m2 + 1024 <= a_pv
        xg_hi = u_hi[:, 0:2, :].rearrange("p k n -> p (k n)").rearrange("p (k n) -> p k n", k=KT)
        xg_lo = u_lo[:, 0:2, :].rearrange("p k n -> p (k n)").rearrange("p (k n) -> p k n", k=KT)
        ht_hi, ht_lo = u_hi[:, 2:4, :], u_lo[:, 2:4, :]
        npass_i = sb("npass_i", [128, 1], i32)
        r_log, r_top, r_idf = rt[:, 64:80], rt[:, 80:96], rt[:, 112:128]
        r_idx = rt[:, 96:112].bitcast(ui32)
        r_d, r_e, r_w = rt[:, 128:130], rt[:, 130:132], rt[:, 132:136]
        r_m = rt[:, 136:168].rearrange("p (k n) -> p k n", k=2)
        r_mask, r_comb, r_pos = rt[:, 168:184], rt[:, 184:200], rt[:, 200:216]
        M_EVENTS = {}
        for n_, (kind, c_, b_) in enumerate(MOE_ORDER):
            if b_ == 1:
                ev = M_EVENTS.setdefault(2 * n_ + 1, [])
                if kind == "g":
                    ev += [("gate", c_)] + [("ht", c_ - 1)] * (c_ > 0)
                elif kind == "u":
                    ev += [("up", c_)]
                elif c_ == FC - 2:
                    ev += [("ht", FC - 1)]
        osb = ar(0, 2048).rearrange("p (c n) -> p c n", c=2)

        B = [st.enter_context(nc.psum_tensor(f"bank{i}", [128, 512], f32)) for i in range(8)]

        vec_in, const_in, x_in = sem("vec_in"), sem("const_in"), sem("x_in")
        raw_in = [sem(f"raw_in{i}") for i in range(NR)]
        hi_done, lo_done, sub_used = sem("hi_done"), sem("lo_done"), sem("sub_used")
        row_ev, row_used = sem("row_ev"), sem("row_used")
        dve_step = sem("dve_step")
        vec_tr, x_tr, vec_ready, silu_ready = sem("vec_tr"), sem("x_tr"), sem("vec_ready"), sem("silu_ready")
        c_zero, c_hi, c_lo = sem("c_zero"), sem("c_hi"), sem("c_lo")
        mod_ready, ones_ready = sem("mod_ready"), sem("ones_ready")
        h_ready = sem("h_ready")
        sq_ready = sem("sq_ready")
        sq_used = sem("sq_used")
        inv_ready = sem("inv_ready")
        rstd_ready = sem("rstd_ready")
        diag_ready = sem("diag_ready")
        bcast_mm = sem("bcast_mm")
        hn_ready = sem("hn_ready")
        uh_ready = sem("uh_ready")
        u_ready = sem("u_ready")
        per_layer = lambda name: [sem(f"{name}{l}") for l in range(DEPTH)]
        proj_ev, pv_ev, i_ev = per_layer("proj_ev"), per_layer("pv_ev"), per_layer("i_ev")
        scan_ready = [[sem(f"scan_ready{l}{d}") for d in range(2)] for l in range(DEPTH)]
        diag_mm = [[sem(f"diag_mm{l}{d}") for d in range(2)] for l in range(DEPTH)]
        diag_ev = [[sem(f"diag_ev{l}{d}") for d in range(2)] for l in range(DEPTH)]
        lvl_mm = [[sem(f"lvl_mm{l}{d}") for d in range(2)] for l in range(DEPTH)]
        lvl_ev = [[sem(f"lvl_ev{l}{d}") for d in range(2)] for l in range(DEPTH)]
        kst_tr = [[sem(f"kst_tr{l}{d}") for d in range(2)] for l in range(DEPTH)]
        kst_ev = [[sem(f"kst_ev{l}{d}") for d in range(2)] for l in range(DEPTH)]
        st_mm = [[sem(f"st_mm{l}{d}") for d in range(2)] for l in range(DEPTH)]
        st_ev = [[sem(f"st_ev{l}{d}") for d in range(2)] for l in range(DEPTH)]
        o_mm = [[sem(f"o_mm{l}{d}") for d in range(2)] for l in range(DEPTH)]
        o_ev = [[sem(f"o_ev{l}{d}") for d in range(2)] for l in range(DEPTH)]
        diff_mm, diff_ev, pool_mm = per_layer("diff_mm"), per_layer("diff_ev"), per_layer("pool_mm")
        pool_hi, pool_lo = per_layer("pool_hi"), per_layer("pool_lo")
        osq, oms, oinv, orstd, odg, obc, a_f = (per_layer("osq"), per_layer("oms"), per_layer("oinv"),
                                                per_layer("orstd"), per_layer("odg"), per_layer("obc"), per_layer("a_f"))
        a_hi, a_lo = per_layer("a_hi"), per_layer("a_lo")
        sil_ready, hid_ready, ffn_tail = sem("sil_ready"), sem("hid_ready"), sem("ffn_tail")
        hs_hi, hs_lo, hs_used, down_mm = sem("hs_hi"), sem("hs_lo"), sem("hs_used"), sem("down_mm")
        rt_mm, vtok_tr, vtok_ev, mask_ready, pos_mm, route_ready = (
            sem("rt_mm"), sem("vtok_tr"), sem("vtok_ev"), sem("mask_ready"), sem("pos_mm"), sem("route_ready"))
        d_ready, e_ready, rt_in = sem("d_ready"), sem("e_ready"), sem("rt_in")
        p_ready, xg_mm, xg_h, xg_l = sem("p_ready"), sem("xg_mm"), sem("xg_h"), sem("xg_l")
        msil_ready, mh_ready, ht_tr, ht_h, ht_l = (sem("msil_ready"), sem("mh_ready"), sem("ht_tr"), sem("ht_h"),
                                                   sem("ht_l"))
        y_ev, pwt_tr, pwt_ev, sc_mm, sc_ev = sem("y_ev"), sem("pwt_tr"), sem("pwt_ev"), sem("sc_mm"), sem("sc_ev")
        out_tr, out_ev, out_dma = sem("out_tr"), sem("out_ev"), sem("out_dma")
        rw_in, wp_in = sem("rw_in"), sem("wp_in")
        mraw_in = [sem(f"mraw_in{i}") for i in range(NRM)]
        slot_step = sem("slot_step")

        def m_slot(r):
            return raw[:, (U0["moe"] + r) % NR, :] if r < NR else mraw[:, r - NR, :]

        block = st.enter_context(nc.Block())

        class Steps:
            def __init__(self, eng, s):
                self.eng, self.s, self.n = eng, s, 0

            def __call__(self, ins):
                self.n += 1
                ins.then_inc(self.s, 1)
                self.eng.wait_ge(self.s, self.n)

        def sub_hi(j, shape=None):
            s = w_hi[:, j % NS, :]
            return s

        MIX, FFN = [0, 2], [1, 3]
        c0s = [0, CTX]
        outs_ch = [[0, 1, 2, 3], [2, 3]]
        order = [[0, 1, 2, 3], [1, 0, 3, 2]]

        def tiles(l):
            return [c * HEADS + hh for c in outs_ch[l] for hh in range(HEADS)]

        def seg(ap, lo_tile, n_tiles, m, half):
            return ap[:, lo_tile * 128:(lo_tile + n_tiles) * 128].rearrange(
                "p (s b m) -> p s b m", b=2, m=m)[:, :, half, :]

        def tbuf(d, L):
            src = f_t[d] if L % 2 == 0 else t2
            return src[:, 0:2048 >> L]

        @block.sync
        def _(sp):
            sp.dma_start(vrow[0:96, 0, :], vecs[0:96, :]).then_inc(vec_in, 16)
            sp.dma_start(vrow[0:88, 1, :], vecs[96:184, :]).then_inc(vec_in, 16)
            sp.dma_start(cst[:], cf32).then_inc(const_in, 16)
            sp.dma_start(msk_in, masks).then_inc(const_in, 16)

            def slot_free(u):
                if u >= NR:
                    kind, n = FREE[u - NR]
                    if kind == "s":
                        sp.wait_ge(lo_done, n)
                    else:
                        sp.wait_ge(pool_mm[int(kind[1])], n)

            def load(u, dst_shape, src):
                slot_free(u)
                pat, kw = dst_shape
                sp.dma_start(raw[:, u % NR, :].rearrange(pat, **kw), src).then_inc(raw_in[u % NR], 16)

            K8 = ("p (k n) -> p k n", dict(k=8))
            K4 = ("p (k n) -> p k n", dict(k=4))
            K2 = ("p (k n) -> p k n", dict(k=2))
            ada = [w_ada[l].rearrange("(k p) n -> p k n", p=128) for l in range(2)]
            win = [w_in[l].rearrange("(k p) n -> p k n", p=128) for l in range(2)]
            wo = [w_out[l].rearrange("(k p) n -> p k n", p=128) for l in range(2)]
            for i in range(4):
                load(i, K4, ada[0][:, 4 * (i % 2):4 * (i % 2) + 4, 512 * (i // 2):512 * (i // 2 + 1)])
            sp.dma_start(xin[:, 0:2, :], ctx_in.rearrange("(c p) n -> p c n", p=128)).then_inc(x_in, 16)
            sp.dma_start(xin[:, 2:4, :], x.rearrange("(c p) n -> p c n", p=128)).then_inc(x_in, 16)
            with sp.Fori(1, 6) as i:
                for k in range(4):
                    sp.wait_ge(lo_done, i * 8 + (2 * k - 6))
                    sp.dma_start(raw[:, k, :].rearrange("p (k n) -> p k n", k=4),
                                 ada[0][:, 4 * (k % 2):4 * (k % 2) + 4,
                                        bass.ds(i * 1024 + 512 * (k // 2), 512)]).then_inc(raw_in[k], 16)
            for l in range(2):
                def tok_major(name, col):
                    for b in range(2):
                        load(U0[name] + b, K4, win[l][:, 4 * b:4 * b + 4, col:col + 512])

                def feat_major(name, col):
                    for b in range(2):
                        load(U0[name] + b, K8, win[l][:, :, col + 256 * b:col + 256 * (b + 1)])

                tok_major(f"pv{l}", 5 * 512)
                feat_major(f"f0{l}", 2 * 512)
                feat_major(f"q{l}", 0)
                tok_major(f"i{l}", 512)
                feat_major(f"f1{l}", 3 * 512)
                feat_major(f"g{l}", 4 * 512)
                for b in range(2 - l):
                    load(U0[f"pm{l}"] + b, ("p (s g n) -> p s g n", dict(s=2, g=4)), pool_mats[1 - (1 - l) * (1 - b)])
                if l == 1:
                    sp.wait_ge(pool_mm[0], 4)
                sp.dma_start(wp[:], w_pool[l].rearrange("g c d -> c g d")).then_inc(wp_in, 16)
                for b in range(4):
                    load(U0[f"wo{l}"] + b, K8, wo[l][:, :, 256 * b:256 * (b + 1)])
                if l == 0:
                    wg = ffn_wg.rearrange("(k p) n -> p k n", p=128)
                    wu = ffn_wu.rearrange("(k p) n -> p k n", p=128)
                    wd = ffn_wd.rearrange("(f p) n -> p f n", p=128)
                    for b in range(2):
                        load(U0["ada1"] + b, K4, ada[1][:, 4 * b:4 * b + 4, 0:512])
                    base = U0["ffn"]
                    for k, (pat, src) in enumerate([(K4, ada[1][:, 0:4, 512:1024]), (K8, wg[:, :, 0:256]),
                                                    (K8, wu[:, :, 0:256]), (K4, ada[1][:, 4:8, 512:1024])]):
                        load(base + k, pat, src)
                    with sp.Fori(1, FFN_IT) as i:
                        for k in range(4):
                            r = (base + k) % NR
                            sp.wait_ge(lo_done, i * 8 + (S0["ffn"] + FFN_FREE[k] - 8))
                            if k in (1, 2):
                                kk, src = 8, (wg, wu)[k - 1][:, :, bass.ds(i * 256, 256)]
                            else:
                                kk, src = 4, ada[1][:, 4 * (k // 3):4 * (k // 3) + 4, bass.ds(i * 512 + 512, 512)]
                            sp.dma_start(raw[:, r, :].rearrange("p (k n) -> p k n", k=kk), src).then_inc(raw_in[r], 16)
                    for b in range(DOWN_U):
                        load(U0["down"] + b, K2, wd[:, 2 * b:2 * b + 2, :])
            moe = [w.rearrange("e (k p) n -> e p k n", p=128) for w in (moe_wg, moe_wu, moe_wd)]

            def moe_load(n, e):
                kind, c, b = MOE_ORDER[n]
                w = moe["gud".index(kind)][bass.ds(e, 1)] if not isinstance(e, int) else moe["gud".index(kind)][e:e + 1]
                if kind == "d":
                    src, kk = w[:, :, 4 * c + 2 * b:4 * c + 2 * b + 2, :], 2
                else:
                    src, kk = w[:, :, 4 * b:4 * b + 4, 512 * c:512 * (c + 1)], 4
                sp.dma_start(m_slot(n % NRM).rearrange("p (k n) -> p k n", k=kk),
                             src.rearrange("e p k n -> p (e k) n")).then_inc(mraw_in[n % NRM], 16)

            S_M = S0["moe"]
            for n in range(NRM):
                if n == NR:
                    sp.wait_ge(a_lo[1], HEADS)
                    sp.dma_start(rt[:, 0:64].rearrange("p (k n) -> p k n", k=KT),
                                 router_w.rearrange("(k p) n -> p k n", p=128)).then_inc(rw_in, 16)
                if n < NR:
                    sp.wait_ge(lo_done, S_M - 2 * NR + 2 * n + 2)
                moe_load(n, 0)

            def moe_pass(s0, first_loaded):
                if not first_loaded:
                    for n in range(NRM):
                        sp.wait_ge(lo_done, s0 + 2 * (n - NRM + 1))
                        moe_load(n, 0)
                with sp.Fori(2, NE + 1) as e2:
                    for n in range(NRM, MOE_U + NRM):
                        if MOE_ORDER[n % MOE_U] != ("d", 0, 0):
                            upto = n + (MOE_ORDER[(n + 1) % MOE_U] == ("d", 0, 0))
                            sp.wait_ge(lo_done, e2 * MOE_S + (s0 - 2 * MOE_S + 2 * (upto - NRM + 1)))
                        moe_load(n % MOE_U, e2 + (n // MOE_U - 2))
                for n in range(NRM, MOE_U):
                    sp.wait_ge(lo_done, s0 + (NE - 1) * MOE_S + 2 * (n - NRM + 1))
                    moe_load(n, NE - 1)

            moe_pass(S_M, True)
            sp.wait_ge(route_ready, 1)
            npass = sp.value_load(npass_i[0:1, 0:1], min_val=1, max_val=2)
            with sp.If(npass > 1):
                moe_pass(S_M + NE * MOE_S, False)
            sp.nop()
            sp.wait_ge(out_ev, 4)
            sp.dma_start(out.rearrange("(c p) n -> p c n", p=128), osb).then_inc(out_dma, 16)
            sp.wait_ge(out_dma, 16)

        def unit_of_sub(name, k):
            return U0[name] + k // 2, k % 2

        def phase_subs():
            seq = [(*unit_of_sub("ada0", k), 0) for k in range(4 * ADA_G)]
            for l in range(DEPTH):
                for name, n, strided in ((f"pv{l}", 4, 0), (f"f0{l}", 4, 1), (f"q{l}", 4, 1), (f"i{l}", 4, 0),
                                         (f"f1{l}", 4, 1), (f"g{l}", 4, 1), (f"wo{l}", 8, 1)):
                    seq += [(*unit_of_sub(name, k), strided) for k in range(n)]
                if l == 0:
                    seq += [(*unit_of_sub("ada1", k), 0) for k in range(4)]
                    for i in range(FFN_IT):
                        seq += [(U0["ffn"] + 4 * i + u_, half, int(u_ in (1, 2))) for u_, half in FFN_SUBS]
                    seq += [(*unit_of_sub("down", k), 0) for k in range(2 * DOWN_U)]
            return seq

        SUBS = phase_subs()
        assert len(SUBS) == S0["moe"]

        def half_of(unit_ap, half, strided):
            if strided:
                return unit_ap.rearrange("p (k n) -> p k n", k=KT)[:, :, half * 128:(half + 1) * 128]
            return unit_ap[:, half * SUB:(half + 1) * SUB]

        def shaped(ap, strided):
            return ap.rearrange("p (k n) -> p k n", k=KT) if strided else ap

        @block.scalar
        def _(act):
            nxt = [0]

            def hi(i=0):
                j = nxt[0]
                nxt[0] += 1
                u, half, strided = SUBS[j]
                act.wait_ge(raw_in[u % NR], i * 16 + 16 * (u // NR + 1))
                if j >= NS:
                    act.wait_ge(sub_used, i * 8 + (j - NS + 1))
                nc.scalar.activation(shaped(w_hi[:, j % NS, :], strided), half_of(raw[:, u % NR, :], half, strided),
                                     ACT.Copy).then_inc(hi_done, 1)

            def his(n):
                for _ in range(n):
                    if nxt[0] < len(SUBS):
                        hi()

            def rows(g, i=0, single=False):
                b = 0 if single else g % 2
                last_sub = S0["ada0"] + 4 * g if g < ADA_G else S0["ada1"] if g == ADA_G else S0["ffn"] + 8 * (g - ADA_G - 1) + 2
                act.wait_ge(sub_used, (i * 4 if not single else i * 8) + (last_sub + 4))
                if single and g > ADA_G or g >= 2:
                    act.wait_ge(row_used, i + (g if single else g - 1))
                nc.scalar.activation(row[0:4, b, :], B[4 + b][0:4, :], ACT.Copy).then_inc(row_ev, 1)

            def stats(n, c0):
                for kt in range(KT):
                    act.wait_ge(h_ready, KT * n + kt + 1)
                    if kt >= 2:
                        act.wait_ge(sq_used, KT * n + kt - 1)
                    nc.scalar.activation(sq[:, kt % 2, c0:NTOK], h[:, kt, c0:NTOK], ACT.Square).then_inc(sq_ready, 1)
                act.wait_ge(inv_ready, n + 1)
                nc.scalar.activation(stat[:, c0 // 128:NCH], stat[:, c0 // 128:NCH], ACT.Sqrt).then_inc(rstd_ready, 1)

            def modulated(n, l, w):
                for kt in range(KT):
                    act.wait_ge(hn_ready, KT * n + kt + 1)
                    for s_, a, b in ((0, 0, CTX), (1, CTX, NTOK)):
                        ins = nc.scalar.activation(u_hi[:, kt, a:b], u32[:, kt % 4, a:b], ACT.Identity,
                                                   bias=mod[:, l, 3 * w * KT + kt, s_:s_ + 1])
                    ins.then_inc(uh_ready, 1)

            act.wait_ge(vec_ready, 1)
            nc.scalar.activation(silu_c[:].rearrange("p k s -> p s k"),
                                 vec[:, V_C:V_C + 16].rearrange("p (s k) -> p s k", s=2), ACT.Silu).then_inc(silu_ready, 1)
            act.wait_ge(silu_ready, 1)
            act.wait_ge(c_zero, 1)
            nc.scalar.activation(c4[:, :, 0:2], silu_c[:], ACT.Copy).then_inc(c_hi, 1)
            act.wait_ge(d_ready, 1)
            nc.scalar.activation(lbt[:, 0:2, :], lbt[:, 0:2, :], ACT.Exp).then_inc(e_ready, 1)

            his(NS)
            for g in range(2):
                his(3)
                rows(g)
                his(1)
            stats(0, 0)
            j0 = nxt[0]
            with act.Fori(0, ADA_G // 2 - 2) as i:
                for g in range(2):
                    for _ in range(3):
                        hi(i)
                    rows(2 + g, i * 2)
                    hi(i)
            nxt[0] = j0 + 4 * ADA_G - 16
            for g in range(ADA_G - 2, ADA_G):
                his(3)
                rows(g)
                his(1)

            def mixer(l):
                n, c0 = MIX[l], c0s[l]
                if l:
                    stats(n, 0)
                modulated(n, l, 0)
                base = S0[f"pv{l}"]
                for j in range(4):
                    if j < 3:
                        act.wait_ge(sub_used, base + j + 1)
                        his(1)
                act.wait_ge(sub_used, base + 4)
                for c in outs_ch[l]:
                    nc.scalar.activation(pv[:, c, :], B[2 + c][:], ACT.Copy).then_inc(pv_ev[l], 1)
                his(1)

                def heads_view(ap, hh, lo):
                    return ap.rearrange("p (c h n) -> p c h n", c=NCH, h=HEADS)[:, lo // 128:, hh, :]

                def proj(kind, name, bank0):
                    for hh in range(HEADS):
                        act.wait_ge(sub_used, S0[name] + hh + 1)
                        bk = B[(bank0 + hh) % 2]
                        if kind == "f0" or kind == "f1":
                            nc.scalar.activation(heads_view(f_t[int(kind[1])], hh, 0),
                                                 bk[:].rearrange("p (c n) -> p c n", c=NCH),
                                                 ACT.Sigmoid).then_inc(proj_ev[l], 1)
                        elif kind == "q":
                            nc.scalar.activation(heads_view(q_t, hh, c0),
                                                 bk[:, c0:].rearrange("p (c n) -> p c n", n=128),
                                                 ACT.Copy, scale=HD ** -0.5).then_inc(proj_ev[l], 1)
                        else:
                            nc.scalar.activation(sg[:, hh, c0:], bk[:, c0:], ACT.Silu).then_inc(proj_ev[l], 1)
                        his(1)

                proj("f0", f"f0{l}", 0)
                proj("q", f"q{l}", 0)
                base = S0[f"i{l}"]
                for j in range(3):
                    act.wait_ge(sub_used, base + j + 1)
                    his(1)
                act.wait_ge(sub_used, base + 4)
                for c in range(NCH):
                    nc.scalar.activation(v_t[:, c, :], B[2 + c][:], ACT.Copy).then_inc(i_ev[l], 1)
                his(1)
                proj("f1", f"f1{l}", 0)
                proj("g", f"g{l}", 0)

                def scan_tail(d):
                    for g in range(3):
                        c = order[d][g]
                        act.wait_ge(kst_tr[l][d], g + 1)
                        nc.scalar.activation(ks[:, c * 512:(c + 1) * 512], B[2 + g][:], ACT.Copy).then_inc(kst_ev[l][d], 1)
                    if d == 0:
                        for n_, c in enumerate(outs_ch[l]):
                            act.wait_ge(o_mm[l][0], n_ + 1)
                            nc.scalar.activation(o_t[:, :, c * 128:(c + 1) * 128],
                                                 B[2 + c][:].rearrange("p (h n) -> p h n", h=HEADS),
                                                 ACT.Copy).then_inc(o_ev[l][0], 1)

                scan_tail(0)
                for g in range(4):
                    act.wait_ge(diff_mm[l], g + 1)
                    if g >= 2:
                        act.wait_ge(pool_mm[l], g - 1)
                    nc.scalar.activation(diff[:, g % 2, c0:], B[2 + g][:, c0:], ACT.Copy).then_inc(diff_ev[l], 1)
                    act.wait_ge(pool_mm[l], g + 1)
                    nc.scalar.activation(u_hi[:, 4 + g, c0:], B[g % 2][:, c0:], ACT.Copy,
                                         scale=vec[:, V_PSC + 4 * l + g:V_PSC + 4 * l + g + 1]).then_inc(pool_hi[l], 1)
                scan_tail(1)
                act.wait_ge(o_ev[l][1], len(outs_ch[l]))
                for hh in range(HEADS):
                    nc.scalar.activation(sq_o[:, hh, c0:], o_t[:, hh, c0:], ACT.Square).then_inc(osq[l], 1)
                act.wait_ge(oinv[l], 1)
                nc.scalar.activation(stat[:], stat[:], ACT.Sqrt).then_inc(orstd[l], 1)
                for hh in range(HEADS):
                    act.wait_ge(a_f[l], hh + 1)
                    nc.scalar.activation(u_hi[:, hh, c0:], a32[:, hh, c0:], ACT.Copy).then_inc(a_hi[l], 1)
                base = S0[f"wo{l}"]
                for j in range(8):
                    act.wait_ge(sub_used, base + j + 1)
                    his(1)

            mixer(0)
            stats(FFN[0], 0)
            rows(ADA_G, single=True)
            his(4)
            modulated(FFN[0], 0, 1)

            def ffn_step(i, loop=False):
                def block_silu(b):
                    act.wait_ge(sub_used, i * 8 + (S0["ffn"] + (2, 6)[b] + 1))
                    if loop or i:
                        act.wait_ge(hid_ready, i * 2 + (b - 1))
                    nc.scalar.activation(sil[:, b, :], B[2 * b][:], ACT.Silu).then_inc(sil_ready, 1)

                one = (lambda: hi(i - 1)) if loop else (lambda: his(1))
                one(), one()
                block_silu(0)
                one(), one(), one()
                rows(ADA_G + 1, i, single=True)
                one()
                block_silu(1)
                one(), one()

            ffn_step(0)
            j0 = nxt[0]
            with act.Fori(1, FFN_IT - 1) as i:
                ffn_step(i, True)
            nxt[0] = j0 + 8 * (FFN_IT - 2)
            ffn_step(FFN_IT - 1)
            for f in range(22):
                act.wait_ge(hid_ready, f + 1)
                act.wait_ge(sub_used, S0["down"] + max(0, f - KT + 1))
                nc.scalar.activation(u_hi[:, f % KT, :], hid[:, f, :], ACT.Copy).then_inc(hs_hi, 1)
                if f >= KT:
                    his(1)
            for f in range(KT):
                act.wait_ge(sub_used, S0["down"] + 22 - KT + f + 1)
                his(1)
            mixer(1)
            stats(FFN[1], CTX)
            for kt in range(KT):
                act.wait_ge(hn_ready, KT * FFN[1] + kt + 1)
                nc.scalar.activation(v32[:, kt, :], v32[:, kt, :], ACT.Identity,
                                     bias=mod[:, 1, 3 * KT + kt, 1:2]).then_inc(uh_ready, 1)

            act.wait_ge(rt_in, 1)
            nc.scalar.activation(r_e, r_d, ACT.Exp).then_inc(e_ready, 1)
            for g in range(4):
                act.wait_ge(vtok_tr, g + 1)
                nc.scalar.activation(vtok[:, g // 2, (g % 2) * 512:(g % 2 + 1) * 512], B[2 + g][:], ACT.Copy).then_inc(vtok_ev, 1)

            act.wait_ge(route_ready, 1)
            npass = act.value_load(npass_i[0:1, 0:1], min_val=1, max_val=2)
            with act.Fori(0, npass) as ps:
                with act.Fori(0, NE) as e:
                    it = ps * NE + e

                    def mhi(s):
                        n = s // 2
                        act.wait_ge(mraw_in[n % NRM], it * (16 * MOE_U // NRM) + 16 * (n // NRM + 1))
                        act.wait_ge(sub_used, it * MOE_S + (S0["moe"] + s - NS + 1))
                        nc.scalar.activation(w_hi[:, (S0["moe"] + s) % NS, :], half_of(m_slot(n % NRM), s % 2, 0),
                                             ACT.Copy).then_inc(hi_done, 1)

                    for s in range(NS):
                        mhi(s)
                    for g in range(2):
                        act.wait_ge(xg_mm, it * 2 + (g + 1))
                        nc.scalar.activation(xg_hi[:, 4 * g:4 * g + 4, :].rearrange("p k n -> p (k n)"), B[4 + g][:],
                                             ACT.Copy).then_inc(xg_h, 1)
                    act.wait_ge(pwt_tr, it + 1)
                    nc.scalar.activation(pwt, B[3][:, 0:256], ACT.Copy).then_inc(pwt_ev, 1)
                    for s in range(MOE_S):
                        ev = M_EVENTS.get(s, ())
                        for what, c in ev:
                            if what == "gate":
                                act.wait_ge(sub_used, it * MOE_S + (S0["moe"] + s + 1))
                                act.wait_ge(mh_ready, it * FC + (c + 1))
                                nc.scalar.activation(msil, B[2 * (c % 2)][:], ACT.Silu).then_inc(msil_ready, 1)
                            elif what == "ht":
                                act.wait_ge(ht_tr, it * FC + (c + 1))
                                nc.scalar.activation(ht_hi[:, c % 2, :], B[4 + c % 2][:], ACT.Copy).then_inc(ht_h, 1)
                        if s + NS < MOE_S:
                            mhi(s + NS)
                    act.wait_ge(sub_used, it * MOE_S + (S0["moe"] + MOE_S))
                    nc.scalar.activation(ybuf[:, 0:512], B[6][:], ACT.Copy).then_inc(y_ev, 1)
            stats(4, CTX)
            for g in range(2):
                act.wait_ge(out_tr, 2 * g + 1)
                nc.scalar.activation(osb[:, g, 0:512], B[2 + 2 * g][:], ACT.Copy).then_inc(out_ev, 1)

        @block.vector
        def _(dve):
            link = Steps(dve, dve_step)
            nxt = [0]

            def lo(i=0):
                j = nxt[0]
                nxt[0] += 1
                u, half, strided = SUBS[j]
                dve.wait_ge(hi_done, i * 8 + (j + 1))
                nc.vector.tensor_tensor(shaped(w_lo[:, j % NS, :], strided), half_of(raw[:, u % NR, :], half, strided),
                                        shaped(w_hi[:, j % NS, :], strided).bitcast(f32), ALU.subtract).then_inc(lo_done, 1)

            def los(n):
                for _ in range(n):
                    if nxt[0] < len(SUBS):
                        lo()

            def tt(out, a, b, op):
                return nc.vector.tensor_tensor(out, a, b, op)

            def bc(ap, m):
                return ap.unsqueeze(len(ap.shape)).broadcast_to((*ap.shape, m))

            def gated(n_next, l, gi, kt, src, c0):
                parts = [(0, 0, CTX)] * (c0 == 0) + [(1, CTX, NTOK)]
                for w, a, b in parts:
                    ins = nc.vector.scalar_tensor_tensor(h[:, kt, a:b], src[:, a - NTOK + src.shape[1]:b - NTOK + src.shape[1]],
                                                         mod[:, l, gi * KT + kt, w:w + 1], h[:, kt, a:b], ALU.mult, ALU.add)
                ins.then_inc(h_ready, 1)

            def stats(n, c0):
                ch = slice(c0 // 128, NCH)
                dve.wait_ge(sq_used, KT * n + KT)
                link(nc.vector.tensor_scalar(stat[:, ch], B[6][:, ch], EPS, None, ALU.add))
                nc.vector.reciprocal(stat[:, ch], stat[:, ch]).then_inc(inv_ready, 1)
                dve.wait_ge(rstd_ready, n + 1)
                tt(ndiag[:, ch], ident.unsqueeze(1).broadcast_to((128, NCH - c0 // 128, 128)), bc(stat[:, ch], 128),
                   ALU.mult).then_inc(diag_ready, 1)

            def modulated(n, l, w):
                dve.wait_ge(bcast_mm, n + 1)
                for kt in range(KT + 2):
                    if kt < KT:
                        if kt >= 4:
                            dve.wait_ge(u_ready, KT * n + kt - 3)
                        for s_, a, b in ((0, 0, CTX), (1, CTX, NTOK)):
                            ins = nc.vector.scalar_tensor_tensor(u32[:, kt % 4, a:b], h[:, kt, a:b],
                                                                 gain[:, l, w, kt, s_:s_ + 1], B[6][:, a:b],
                                                                 ALU.mult, ALU.mult)
                        ins.then_inc(hn_ready, 1)
                    if kt >= 2:
                        k = kt - 2
                        dve.wait_ge(uh_ready, KT * n + k + 1)
                        for s_, a, b in ((0, 0, CTX), (1, CTX, NTOK)):
                            ins = nc.vector.scalar_tensor_tensor(u_lo[:, k, a:b], u32[:, k % 4, a:b],
                                                                 mod[:, l, 3 * w * KT + k, s_:s_ + 1],
                                                                 u_hi[:, k, a:b].bitcast(f32), ALU.add, ALU.subtract)
                        ins.then_inc(u_ready, 1)

            nc.vector.memset(ones[:], 1.0).then_inc(ones_ready, 1)
            nc.vector.memset(ones_d[:], 1.0 / D).then_inc(ones_ready, 1)
            nc.vector.memset(ones_hd[:], 1.0 / HD).then_inc(ones_ready, 1)
            dve.wait_ge(const_in, 32)
            link(nc.vector.tensor_copy(msk[:].rearrange("p a b n -> p (a b n)"), msk_in))
            nc.vector.memset(c4[:].bitcast(f32), 0.0).then_inc(c_zero, 1)
            tt(sel[:], ident[0:4, 0:2], ident[0:4, 2:4], ALU.add).then_inc(ones_ready, 1)
            dve.wait_ge(vec_tr, 2)
            nc.vector.tensor_copy(vec[:], B[6][:, 0:V_ROWS]).then_inc(vec_ready, 1)
            dve.wait_ge(vec_ready, 1)
            r0, r1 = vec[:, V_LB:V_LB + 8], vec[:, V_LB + 8:V_LB + 16]
            link(tt(lbt[:, 2, :], r0, r1, ALU.max))
            link(tt(lbt[:, 0, :], r0, lbt[:, 2, :], ALU.subtract))
            tt(lbt[:, 1, :], r1, lbt[:, 2, :], ALU.subtract).then_inc(d_ready, 1)
            dve.wait_ge(c_hi, 1)
            tt(c4[:, :, 2:4], silu_c[:], c4[:, :, 0:2].bitcast(f32), ALU.subtract).then_inc(c_lo, 1)
            los(12)
            for kt in range(KT):
                dve.wait_ge(x_tr, kt + 1)
                nc.vector.tensor_copy(h[:, kt, :], B[kt % 4][:]).then_inc(h_ready, 1)
            dve.wait_ge(e_ready, 1)
            e0, e1, t0, t1 = (lbt[:, k, :] for k in range(4))
            link(tt(t0, e0, e1, ALU.add))
            link(nc.vector.reciprocal(t1, t0))
            link(tt(e0, e0, t1, ALU.mult))
            link(tt(e1, e1, t1, ALU.mult))
            link(tt(lb[:, 0, :], e0, e0, ALU.subtract))
            link(tt(t0, e0, e1, ALU.add))
            link(tt(lb[:, 1, :], t0, e0, ALU.subtract))
            link(nc.vector.tensor_scalar(lb1[:], lb[:], -1.0, 1.0, ALU.mult, ALU.add))

            def modulation(l):
                dve.wait_ge(row_used, ADA_G * (l + 1))
                link(tt(mod[:, l], B[7][:, 0:2 * ADA_BLKS].rearrange("p (b s) -> p b s", s=2),
                        bc(vec[:, V_BADA + ADA_BLKS * l:V_BADA + ADA_BLKS * (l + 1)], 2), ALU.add))
                for w in range(2):
                    ins = nc.vector.scalar_tensor_tensor(
                        gain[:, l, w], mod[:, l, (1 + 3 * w) * KT:(2 + 3 * w) * KT, :], 1.0,
                        bc(vec[:, V_NORM + (2 * l + w) * KT:V_NORM + (2 * l + w + 1) * KT], 2), ALU.add, ALU.mult)
                ins.then_inc(mod_ready, 1)
                dve.wait_ge(mod_ready, l + 1)

            stats(0, 0)
            j0 = nxt[0]
            with dve.Fori(0, ADA_G // 2 - 2) as i:
                for _ in range(8):
                    lo(i)
            nxt[0] = j0 + 4 * ADA_G - 16
            los(8)
            modulation(0)

            def mixer(l):
                n, c0 = MIX[l], c0s[l]
                TL = tiles(l)
                t0, nt = TL[0], len(TL)
                if l:
                    stats(n, 0)
                modulated(n, l, 0)
                los(4)

                def gates(d, name):
                    for hh in range(HEADS):
                        first = {"f0": 0, "f1": 8}[name]
                        dve.wait_ge(proj_ev[l], first + hh + 1)
                        fv = f_t[d].rearrange("p (c h n) -> p c h n", c=NCH, h=HEADS)[:, :, hh, :]
                        link(nc.vector.tensor_scalar(fv, fv, lb1[:, l, d * HEADS + hh:d * HEADS + hh + 1],
                                                     lb[:, l, d * HEADS + hh:d * HEADS + hh + 1], ALU.mult, ALU.add))
                        los(1)

                def start(d):
                    link(nc.vector.tensor_scalar(ks, f_t[d], -1.0, 1.0, ALU.mult, ALU.add))
                    tt(qp[:, t0 * 128:], q_t[:, t0 * 128:], f_t[d][:, t0 * 128:], ALU.mult).then_inc(scan_ready[l][d], 1)

                gates(0, "f0")
                los(4)
                los(4)
                dve.wait_ge(proj_ev[l], 8)
                start(0)

                def scan(d, fill):
                    A3 = amat.rearrange("p (t n) -> p t n", n=128)
                    for g in range(nt // 4):
                        dve.wait_ge(diag_mm[l][d], g + 1)
                        tt(A3[:, t0 + 4 * g:t0 + 4 * g + 4, :], B[2 + g][:].rearrange("p (t n) -> p t n", t=4),
                           ident.unsqueeze(1).broadcast_to((128, 4, 128)), ALU.mult).then_inc(diag_ev[l][d], 1)
                    for L in range(LEVELS):
                        m = 1 << L
                        qh, kh = (1, 0) if d == 0 else (0, 1)
                        T = tbuf(d, L)
                        dve.wait_ge(lvl_mm[l][d], (L + 1) * (nt // 8))
                        T2 = T.rearrange("p (s b) -> p s b", b=2)
                        kv = seg(ks, 0, 16, m, kh)
                        tt(kv, kv, bc(T2[:, :, qh], m), ALU.mult)
                        qv = seg(qp, t0, nt, m, qh)
                        tt(qv, qv, bc(T2[:, (t0 * 128) // (2 * m):, kh], m), ALU.mult)
                        tt(tbuf(d, L + 1), T2[:, :, 0], T2[:, :, 1], ALU.mult).then_inc(scan_ready[l][d], 1)
                        if L == 0:
                            dve.wait_ge(diag_ev[l][d], nt // 4)
                        else:
                            dve.wait_ge(lvl_ev[l][d], L * (nt // 8))
                        for g in range(nt // 8):
                            bk = B[2 + 2 * (L % 2) + g]
                            av = A3[:, t0 + 8 * g:t0 + 8 * g + 8, :].rearrange("p t (s b m) -> p t s b m", b=2, m=m)[:, :, :, qh, :]
                            mv = msk[:, d, L, :].unsqueeze(1).broadcast_to((128, 8, 64)).rearrange("p t (s m) -> p t s m", m=m)
                            dv = bk[:].rearrange("p (t s m) -> p t s m", t=8, m=m)
                            nc.vector.copy_predicated(av, mv, dv).then_inc(lvl_ev[l][d], 1)
                        fill(L)

                def fill0(L):
                    if L < 4:
                        gates_one(L)
                    else:
                        los(2 if L == LEVELS - 1 else 1)

                def gates_one(hh):
                    dve.wait_ge(proj_ev[l], 8 + hh + 1)
                    fv = f_t[1].rearrange("p (c h n) -> p c h n", c=NCH, h=HEADS)[:, :, hh, :]
                    nc.vector.tensor_scalar(fv, fv, lb1[:, l, HEADS + hh:HEADS + hh + 1],
                                            lb[:, l, HEADS + hh:HEADS + hh + 1], ALU.mult, ALU.add).then_inc(dve_step, 1)
                    link.n += 1
                    los(1)

                scan(0, fill0)

                def states(d):
                    T = tbuf(d, LEVELS)
                    for g in range(3):
                        dve.wait_ge(st_mm[l][d], g + 1)
                        bk = B[(5, 2, 3)[g]]
                        if g == 0:
                            ins = nc.vector.tensor_copy(s_t[:, 0], bk[:].rearrange("p (h n) -> p h n", h=HEADS))
                        else:
                            c = order[d][g]
                            for hh in range(HEADS):
                                ins = nc.vector.scalar_tensor_tensor(s_t[:, g, hh], s_t[:, g - 1, hh],
                                                                     T[:, c * HEADS + hh:c * HEADS + hh + 1],
                                                                     bk[:, hh * 128:(hh + 1) * 128], ALU.mult, ALU.add)
                        ins.then_inc(st_ev[l][d], 1)
                        dve.wait_ge(st_ev[l][d], g + 1)

                states(0)
                for g in range(4):
                    dve.wait_ge(pool_hi[l], g + 1)
                    nc.vector.scalar_tensor_tensor(u_lo[:, 4 + g, c0:], B[g % 2][:, c0:],
                                                   vec[:, V_PSC + 4 * l + g:V_PSC + 4 * l + g + 1],
                                                   u_hi[:, 4 + g, c0:].bitcast(f32), ALU.mult,
                                                   ALU.subtract).then_inc(pool_lo[l], 1)
                dve.wait_ge(o_mm[l][0], len(outs_ch[l]))
                start(1)
                scan(1, lambda L: None)
                states(1)
                for k, c in enumerate(outs_ch[l]):
                    dve.wait_ge(o_mm[l][1], k + 1)
                    dve.wait_ge(o_ev[l][0], k + 1)
                    ov = o_t[:, :, c * 128:(c + 1) * 128]
                    tt(ov, ov, B[2 + c][:].rearrange("p (h n) -> p h n", h=HEADS), ALU.add).then_inc(o_ev[l][1], 1)
                ch = slice(c0 // 128, NCH)
                sv = stat[:].rearrange("p (h c) -> p h c", h=HEADS)
                dve.wait_ge(oms[l], HEADS)
                link(nc.vector.tensor_scalar(sv[:, :, ch], B[6][:, 0:HEADS * NCH].rearrange("p (h c) -> p h c", h=HEADS)[:, :, ch],
                                             EPS, None, ALU.add))
                nc.vector.reciprocal(stat[:], stat[:]).then_inc(oinv[l], 1)
                dve.wait_ge(orstd[l], 1)
                for hh in range(HEADS):
                    tt(odiag[:, hh, ch], ident.unsqueeze(1).broadcast_to((128, NCH - c0 // 128, 128)), bc(sv[:, hh, ch], 128),
                       ALU.mult).then_inc(odg[l], 1)
                for hh in range(HEADS):
                    dve.wait_ge(obc[l], hh + 1)
                    w = vec[:, V_HNW + HEADS * l + hh:V_HNW + HEADS * l + hh + 1]
                    link(nc.vector.scalar_tensor_tensor(a32[:, hh, c0:], o_t[:, hh, c0:], w, B[2 + hh][:, c0:],
                                                        ALU.mult, ALU.mult))
                    tt(a32[:, hh, c0:], a32[:, hh, c0:], sg[:, hh, c0:], ALU.mult).then_inc(a_f[l], 1)
                for hh in range(HEADS):
                    dve.wait_ge(a_hi[l], hh + 1)
                    tt(u_lo[:, hh, c0:], a32[:, hh, c0:], u_hi[:, hh, c0:].bitcast(f32), ALU.subtract).then_inc(a_lo[l], 1)
                for kt in range(KT):
                    dve.wait_ge(sub_used, S0[f"wo{l}"] + kt + 1)
                    gated(FFN[l], l, 2, kt, B[kt % 2][:], c0)
                    los(1)

            mixer(0)
            stats(FFN[0], 0)
            los(4)
            modulated(FFN[0], 0, 1)

            def ffn_step(i, loop=False):
                def hidden(b):
                    dve.wait_ge(sil_ready, i * 2 + (b + 1))
                    dve.wait_ge(sub_used, i * 8 + (S0["ffn"] + (3, 7)[b] + 1))
                    dst = hid[:, bass.ds(i * 2 + b, 1), :].rearrange("p f n -> p (f n)") if loop else hid[:, 2 * i + b, :]
                    tt(dst, sil[:, b, :], B[2 * b + 1][:], ALU.mult).then_inc(hid_ready, 1)

                one = (lambda: lo(i - 1)) if loop else (lambda: los(1))
                for _ in range(3):
                    one()
                hidden(0)
                for _ in range(4):
                    one()
                if not loop and i == FFN_IT - 1:
                    modulation(1)
                hidden(1)
                one()

            ffn_step(0)
            j0 = nxt[0]
            with dve.Fori(1, FFN_IT - 1) as i:
                ffn_step(i, True)
            nxt[0] = j0 + 8 * (FFN_IT - 2)
            ffn_step(FFN_IT - 1)
            for f in range(22):
                dve.wait_ge(hs_hi, f + 1)
                tt(u_lo[:, f % KT, :], hid[:, f, :], u_hi[:, f % KT, :].bitcast(f32), ALU.subtract).then_inc(hs_lo, 1)
                if f >= KT:
                    los(1)
            for f in range(KT - 1):
                los(1)
            for kt in range(KT):
                if kt < KT - 1:
                    dve.wait_ge(down_mm, kt + 1)
                else:
                    dve.wait_ge(sub_used, S0["down"] + 22)
                gated(MIX[1], 0, 5, kt, B[kt][:], 0)
            los(1)
            mixer(1)

            stats(FFN[1], CTX)
            dve.wait_ge(bcast_mm, FFN[1] + 1)
            for kt in range(KT):
                nc.vector.scalar_tensor_tensor(v32[:, kt, :], h[:, kt, CTX:], gain[:, 1, 1, kt, 1:2], B[6][:, CTX:],
                                               ALU.mult, ALU.mult).then_inc(hn_ready, 1)
            for g in range(4):
                nc.vector.memset(yacc[:, 2 * g:2 * g + 2, :], 0.0).then_inc(sc_ev, 1)
            nc.vector.memset(msil, 0.0).then_inc(mh_ready, 1)
            dve.wait_ge(rt_mm, 1)
            link(nc.vector.tensor_copy(r_log, B[0][:, 0:16]))
            for c in range(2):
                link(nc.vector.max(r_top[:, 8 * c:8 * c + 8], r_log[:, 8 * c:8 * c + 8]))
                link(nc.vector.max_index(r_idx[:, 8 * c:8 * c + 8], r_top[:, 8 * c:8 * c + 8], r_log[:, 8 * c:8 * c + 8]))
            link(nc.vector.tensor_copy(r_idf, r_idx))
            for c in range(2):
                ins = tt(r_d[:, c:c + 1], r_top[:, 8 * c + 1:8 * c + 2], r_top[:, 8 * c:8 * c + 1], ALU.subtract)
            ins.then_inc(rt_in, 1)
            for c in range(2):
                for k in range(2):
                    link(nc.vector.tensor_scalar(r_m[:, k, 8 * c:8 * c + 8], e_iota, r_idf[:, 8 * c + k:8 * c + k + 1],
                                                 None, ALU.is_equal))
            tt(r_mask, r_m[:, 0], r_m[:, 1], ALU.add).then_inc(mask_ready, 1)
            dve.wait_ge(e_ready, 2)
            link(nc.vector.tensor_scalar(r_w[:, 0:2], r_e, 1.0, None, ALU.add))
            link(nc.vector.reciprocal(r_w[:, 0:2], r_w[:, 0:2]))
            link(tt(r_w[:, 2:4], r_e, r_w[:, 0:2], ALU.mult))
            for c in range(2):
                s = slice(8 * c, 8 * c + 8)
                link(nc.vector.tensor_scalar(r_comb[:, s], r_m[:, 0, s], r_w[:, c:c + 1], None, ALU.mult))
                link(nc.vector.scalar_tensor_tensor(r_comb[:, s], r_m[:, 1, s], r_w[:, 2 + c:3 + c], r_comb[:, s],
                                                    ALU.mult, ALU.add))
            dve.wait_ge(pos_mm, 1)
            link(nc.vector.scalar_tensor_tensor(r_pos, B[1][:, 0:16], 1.0, r_mask, ALU.add, ALU.mult))
            link(nc.vector.tensor_scalar(r_pos, r_pos, -1.0, None, ALU.add))
            link(nc.vector.tensor_reduce(r_w[:, 0:1], B[1][:, 16:24], AX.X, ALU.max))
            link(nc.vector.tensor_scalar(r_w[:, 1:2], r_w[:, 0:1], SLOTS + 0.5, 1.0, ALU.is_gt, ALU.add))
            nc.vector.tensor_copy(npass_i[:], r_w[:, 1:2]).then_inc(route_ready, 1)
            dve.wait_ge(route_ready, 1)
            npass = dve.value_load(npass_i[0:1, 0:1], min_val=1, max_val=2)
            with dve.Fori(0, npass) as ps:
                with dve.Fori(0, NE) as e:
                    it = ps * NE + e

                    def mlo(s):
                        n = s // 2
                        dve.wait_ge(hi_done, it * MOE_S + (S0["moe"] + s + 1))
                        slot = (S0["moe"] + s) % NS
                        tt(w_lo[:, slot, :], half_of(m_slot(n % NRM), s % 2, 0), w_hi[:, slot, :].bitcast(f32),
                           ALU.subtract).then_inc(lo_done, 1)

                    for c in range(2):
                        at = r_pos[:, bass.ds(e + 8 * c, 1)]
                        nc.vector.tensor_scalar(pbuf[:, c, :], slot_iota, at, None, ALU.is_equal)
                        ins = nc.vector.tensor_scalar(pw[:, c, :], slot_iota, at, r_comb[:, bass.ds(e + 8 * c, 1)],
                                                      ALU.is_equal, ALU.mult)
                    ins.then_inc(p_ready, 1)
                    for s in range(NS):
                        mlo(s)
                    for g in range(2):
                        dve.wait_ge(xg_h, it * 2 + (g + 1))
                        tt(xg_lo[:, 4 * g:4 * g + 4, :].rearrange("p k n -> p (k n)"), B[4 + g][:],
                           xg_hi[:, 4 * g:4 * g + 4, :].rearrange("p k n -> p (k n)").bitcast(f32),
                           ALU.subtract).then_inc(xg_l, 1)
                    for s in range(MOE_S):
                        for what, c in M_EVENTS.get(s, ()):
                            if what == "up":
                                dve.wait_ge(msil_ready, it * FC + (c + 1))
                                dve.wait_ge(sub_used, it * MOE_S + (S0["moe"] + s + 1))
                                tt(mh[:, c % 2, :], msil, B[2 * (c % 2) + 1][:], ALU.mult).then_inc(mh_ready, 1)
                            elif what == "ht":
                                dve.wait_ge(ht_h, it * FC + (c + 1))
                                tt(ht_lo[:, c % 2, :], B[4 + c % 2][:], ht_hi[:, c % 2, :].bitcast(f32),
                                   ALU.subtract).then_inc(ht_l, 1)
                        if s + NS < MOE_S:
                            mlo(s + NS)
                    dve.wait_ge(sub_used, it * MOE_S + (S0["moe"] + MOE_S))
                    nc.vector.tensor_copy(ybuf[:, 512:1024], B[7][:]).then_inc(y_ev, 1)
                    for g in range(4):
                        dve.wait_ge(sc_mm, it * 4 + (g + 1))
                        ya = yacc[:, 2 * g:2 * g + 2, :]
                        tt(ya, ya, B[g][:].rearrange("p (k n) -> p k n", k=2), ALU.add).then_inc(sc_ev, 1)
                nc.vector.tensor_scalar(slot_iota, slot_iota, float(SLOTS), None, ALU.add).then_inc(slot_step, 1)
                dve.wait_ge(slot_step, ps + 1)
            for kt in range(KT):
                gated(4, 1, 5, kt, yacc[:, kt, :], CTX)
            stats(4, CTX)
            dve.wait_ge(bcast_mm, 5)
            for kt in range(KT):
                nc.vector.scalar_tensor_tensor(v32[:, kt, :], h[:, kt, CTX:], vec[:, V_FIN + kt:V_FIN + kt + 1],
                                               B[6][:, CTX:], ALU.mult, ALU.mult).then_inc(hn_ready, 1)
            for g in range(2):
                dve.wait_ge(out_tr, 2 * g + 2)
                nc.vector.tensor_copy(osb[:, g, 512:1024], B[3 + 2 * g][:]).then_inc(out_ev, 1)

        @block.tensor
        def _(pe):
            nxt = [0]
            mm = nc.tensor.matmul

            def wsub(j):
                return w_hi[:, j % NS, :], w_lo[:, j % NS, :]

            def mm3(out, lh, ll, rh, rl, start, stop):
                mm(out, lh, rh, start=start, stop=False)
                mm(out, lh, rl, start=False, stop=False)
                return mm(out, ll, rh, start=False, stop=stop)

            def stats(n, c0):
                for kt in range(KT):
                    pe.wait_ge(sq_ready, KT * n + kt + 1)
                    for c in range(c0 // 128, NCH):
                        ins = mm(B[6][:, c:c + 1], sq[:, kt % 2, c * 128:(c + 1) * 128], ones_d[:, 0:1],
                                 start=(kt == 0 and c == c0 // 128), stop=(kt == KT - 1), skip_group_check=True)
                    ins.then_inc(sq_used, 1)

            def spread(n, c0):
                pe.wait_ge(diag_ready, n + 1)
                mm(B[6][:, c0:], ones[:], ndiag[:, c0 // 128:NCH].rearrange("p c n -> p (c n)"),
                   start=True, stop=True).then_inc(bcast_mm, 1)

            pe.wait_ge(vec_in, 32)
            pe.wait_ge(const_in, 32)
            nc.tensor.transpose(B[6][:, 0:96], vrow[0:96, 0, :], ident[0:96, 0:96]).then_inc(vec_tr, 1)
            nc.tensor.transpose(B[6][:, 96:184], vrow[0:88, 1, :], ident[0:88, 0:88]).then_inc(vec_tr, 1)

            def ada_sub(j, k, bank, i=0):
                pe.wait_ge(lo_done, i * 8 + (j + 1))
                wh, wl = (w.rearrange("p (k n) -> p k n", k=2) for w in wsub(j))
                for kk in range(2):
                    kt = 2 * k + kk
                    mm(bank[:], c4[:, kt, :], wh[:, kk], start=(kt == 0), stop=False)
                    ins = mm(bank[:], c4[:, kt, :], wl[:, kk], start=False, stop=(kt == KT - 1))
                ins.then_inc(sub_used, 1)

            def ada_cols(g, b, i=0, step=1):
                pe.wait_ge(row_ev, i * step + (g + 1))
                for k in range(4):
                    if isinstance(i, int):
                        o = B[7][:, 8 * (g % ADA_G) + 2 * k:8 * (g % ADA_G) + 2 * k + 2]
                    else:
                        o = B[7][:, bass.ds(i * (8 * step) + (8 * (g % ADA_G) + 2 * k), 2)]
                    ins = mm(o, row[0:4, b, k * 128:(k + 1) * 128], sel[:], start=True, stop=True)
                ins.then_inc(row_used, 1)

            pe.wait_ge(c_lo, 1)
            pe.wait_ge(ones_ready, 4)
            for g in range(2):
                for k in range(4):
                    ada_sub(4 * g + k, k, B[4 + g])
                    if g == 1 and k == 1:
                        ada_cols(0, 0)
            pe.wait_ge(x_in, 32)
            for kt in range(KT):
                if kt >= 4:
                    pe.wait_ge(h_ready, KT * 0 + kt - 3)
                for c in range(NCH):
                    ins = nc.tensor.transpose(B[kt % 4][:, c * 128:(c + 1) * 128], xin[:, c, kt * 128:(kt + 1) * 128], ident)
                ins.then_inc(x_tr, 1)
            stats(0, 0)
            with pe.Fori(0, ADA_G // 2 - 1) as i:
                for g in range(2):
                    for k in range(4):
                        ada_sub(8 + 4 * g + k, k, B[4 + g], i)
                        if k == 1:
                            ada_cols(1 + g, (1 + g) % 2, i, 2)
            ada_cols(ADA_G - 1, 1)
            spread(0, 0)
            nxt[0] = 4 * ADA_G

            def take_sub():
                j = nxt[0]
                nxt[0] += 1
                pe.wait_ge(lo_done, j + 1)
                return j

            def token_major(l, chunks, n):
                for k in range(4):
                    j = take_sub()
                    wh, wl = (w.rearrange("p (k n) -> p k n", k=2) for w in wsub(j))
                    for kk in range(2):
                        kt = 2 * k + kk
                        pe.wait_ge(u_ready, KT * n + kt + 1)
                        for c in chunks:
                            t = slice(c * 128, (c + 1) * 128)
                            ins = mm3(B[2 + c][:], u_hi[:, kt, t], u_lo[:, kt, t], wh[:, kk], wl[:, kk], kt == 0, kt == KT - 1)
                    ins.then_inc(sub_used, 1)

            def block_fm(bank, c0):
                j = take_sub()
                wh, wl = (w.rearrange("p (k n) -> p k n", k=KT) for w in wsub(j))
                for kt in range(KT):
                    mm3_(bank[:, c0:], wh[:, kt], wl[:, kt], kt, c0)
                last[0].then_inc(sub_used, 1)

            last = [None]

            def mm3_(out, wh, wl, kt, c0):
                last[0] = mm3(out, wh, wl, u_hi[:, kt, c0:], u_lo[:, kt, c0:], kt == 0, kt == KT - 1)

            def mixer(l):
                n, c0 = MIX[l], c0s[l]
                TL = tiles(l)
                t0, nt = TL[0], len(TL)
                if l:
                    stats(n, 0)
                    spread(n, 0)
                token_major(l, outs_ch[l], n)
                blk = [0]

                def proj_block(cc):
                    if blk[0] >= 2:
                        pe.wait_ge(proj_ev[l], blk[0] - 1)
                    block_fm(B[blk[0] % 2], cc)
                    blk[0] += 1

                for _ in range(4):
                    proj_block(0)
                for _ in range(4):
                    proj_block(c0)
                pe.wait_ge(pv_ev[l], len(outs_ch[l]))
                token_major(l, range(NCH), n)

                def scan(d, fill):
                    qh, kh = (1, 0) if d == 0 else (0, 1)
                    pe.wait_ge(scan_ready[l][d], 1)
                    if d == 0:
                        pe.wait_ge(i_ev[l], NCH)
                    for g in range(nt // 4):
                        for t in range(4):
                            ti = TL[4 * g + t]
                            ins = mm(B[2 + g][:, t * 128:(t + 1) * 128], ks[:, ti * 128:(ti + 1) * 128],
                                     q_t[:, ti * 128:(ti + 1) * 128], start=True, stop=True)
                        ins.then_inc(diag_mm[l][d], 1)
                    pe.wait_ge(diag_ev[l][d], nt // 4)
                    for L in range(LEVELS):
                        m = 1 << L
                        pe.wait_ge(scan_ready[l][d], L + 1)
                        if L >= 2:
                            pe.wait_ge(lvl_ev[l][d], (L - 1) * (nt // 8))
                        for g in range(nt // 8):
                            for t in range(8):
                                ti = TL[8 * g + t]
                                ins = mm(B[2 + 2 * (L % 2) + g][:, t * 64:(t + 1) * 64], ks[:, ti * 128:(ti + 1) * 128],
                                         seg(qp, ti, 1, m, qh), start=True, stop=True)
                            ins.then_inc(lvl_mm[l][d], 1)
                        fill(L)
                    pe.wait_ge(scan_ready[l][d], LEVELS + 1)
                    pe.wait_ge(lvl_ev[l][d], LEVELS * (nt // 8))
                    for g in range(3):
                        for hh in range(HEADS):
                            ti = order[d][g] * HEADS + hh
                            ins = nc.tensor.transpose(B[2 + g][:, hh * 128:(hh + 1) * 128], ks[:, ti * 128:(ti + 1) * 128], ident)
                        ins.then_inc(kst_tr[l][d], 1)
                    for g in range(3):
                        c = order[d][g]
                        pe.wait_ge(kst_ev[l][d], g + 1)
                        for hh in range(HEADS):
                            ti = c * HEADS + hh
                            ins = mm(B[(5, 2, 3)[g]][:, hh * 128:(hh + 1) * 128], ks[:, ti * 128:(ti + 1) * 128],
                                     v_t[:, c, hh * 128:(hh + 1) * 128], start=True, stop=True)
                        ins.then_inc(st_mm[l][d], 1)
                    pe.wait_ge(st_ev[l][d], 3)
                    if d == 1:
                        pe.wait_ge(pool_lo[l], 4)
                    for c in outs_ch[l]:
                        pos = order[d].index(c)
                        for hh in range(HEADS):
                            ti = c * HEADS + hh
                            o = B[2 + c][:, hh * 128:(hh + 1) * 128]
                            ins = mm(o, v_t[:, c, hh * 128:(hh + 1) * 128], amat[:, ti * 128:(ti + 1) * 128],
                                     start=True, stop=(pos == 0))
                            if pos:
                                ins = mm(o, s_t[:, pos - 1, hh, :], qp[:, ti * 128:(ti + 1) * 128], start=False, stop=True)
                        ins.then_inc(o_mm[l][d], 1)

                def fill0(L):
                    proj_block(0 if L < 4 else c0)
                    if L == LEVELS - 1:
                        proj_block(c0)

                scan(0, fill0)
                u0 = U0[f"pm{l}"]
                for k in range(2 - l):
                    pe.wait_ge(raw_in[(u0 + k) % NR], 16 * ((u0 + k) // NR + 1))
                pe.wait_ge(wp_in, 16 * (l + 1))
                pe.wait_ge(proj_ev[l], 16)
                pe.wait_ge(o_ev[l][0], len(outs_ch[l]))
                for g in range(4):
                    for side in ([0, 1] if l == 0 else [1]):
                        mat = raw[:, (u0 + side - l) % NR, :].rearrange("p (s g n) -> p s g n", s=2, g=4)
                        for s in range(2):
                            ins = mm(B[2 + g][:, side * 256:(side + 1) * 256], pv[:, 2 * side + s, g * 128:(g + 1) * 128],
                                     mat[:, s, g, :], start=(s == 0), stop=(s == 1))
                    ins.then_inc(diff_mm[l], 1)
                    if g >= 1:
                        pool_block(l, g - 1, c0)
                pool_block(l, 3, c0)
                scan(1, lambda L: None)
                pe.wait_ge(o_ev[l][1], len(outs_ch[l]))
                for hh in range(HEADS):
                    pe.wait_ge(osq[l], hh + 1)
                    for c in outs_ch[l]:
                        ins = mm(B[6][:, NCH * hh + c:NCH * hh + c + 1], sq_o[:, hh, c * 128:(c + 1) * 128], ones_hd[:, 0:1],
                                 start=True, stop=True)
                    ins.then_inc(oms[l], 1)
                for hh in range(HEADS):
                    pe.wait_ge(odg[l], hh + 1)
                    mm(B[2 + hh][:, c0:], ones[:], odiag[:, hh, c0 // 128:].rearrange("p c n -> p (c n)"),
                       start=True, stop=True).then_inc(obc[l], 1)
                pe.wait_ge(a_lo[l], HEADS)
                pe.wait_ge(pool_lo[l], 4)
                for j in range(8):
                    if j >= 2:
                        pe.wait_ge(h_ready, KT * FFN[l] + j - 1)
                    block_fm(B[j % 2], c0)

            def pool_block(l, g, c0):
                pe.wait_ge(diff_ev[l], g + 1)
                if g >= 2:
                    pe.wait_ge(pool_lo[l], g - 1)
                mm(B[g % 2][:, c0:], wp[:, g, :], diff[:, g % 2, c0:], start=True, stop=True).then_inc(pool_mm[l], 1)

            mixer(0)
            for k in range(4):
                ada_sub(S0["ada1"] + k, k, B[4])
            stats(FFN[0], 0)
            ada_cols(ADA_G, 0)
            spread(FFN[0], 0)
            base = S0["ffn"]

            def ffn_step(i, dyn):
                def block(s, b, k):
                    jj = base + s
                    pe.wait_ge(lo_done, i * 8 + (jj + 1))
                    if k == 0 and (dyn or i > 0):
                        pe.wait_ge(hid_ready, i * 2 + (b - 1))
                    wh, wl = (w.rearrange("p (k n) -> p k n", k=KT) for w in wsub(jj))
                    for kt in range(KT):
                        if not dyn and i == 0 and b == 0 and k == 0:
                            pe.wait_ge(u_ready, KT * FFN[0] + kt + 1)
                        mm3_(B[2 * b + k][:], wh[:, kt], wl[:, kt], kt, 0)
                    last[0].then_inc(sub_used, 1)

                for k in range(2):
                    ada_sub(base + k, k, B[4], i)
                block(2, 0, 0)
                block(3, 0, 1)
                for k in range(2):
                    ada_sub(base + 4 + k, 2 + k, B[4], i)
                block(6, 1, 0)
                ada_cols(ADA_G + 1, 0, i) if dyn else ada_cols(ADA_G + 1 + i, 0)
                block(7, 1, 1)

            ffn_step(0, False)
            with pe.Fori(1, FFN_IT - 1) as i:
                ffn_step(i, True)
            ffn_step(FFN_IT - 1, False)
            nxt[0] = S0["down"]
            pe.wait_ge(hid_ready, 22)
            for f in range(22):
                j = take_sub()
                wh, wl = wsub(j)
                pe.wait_ge(hs_lo, f + 1)
                if f == 0:
                    pe.wait_ge(mod_ready, 2)
                for d in range(KT):
                    dd = slice(d * 128, (d + 1) * 128)
                    ins = mm3(B[d][:], wh[:, dd], wl[:, dd], u_hi[:, f % KT, :], u_lo[:, f % KT, :], f == 0, f == 21)
                    if f == 21 and d < KT - 1:
                        ins.then_inc(down_mm, 1)
                ins.then_inc(sub_used, 1)
            pe.wait_ge(h_ready, KT * MIX[1] + KT)
            mixer(1)
            pe.wait_ge(h_ready, KT * FFN[1] + KT)
            stats(FFN[1], CTX)
            spread(FFN[1], CTX)
            pe.wait_ge(rw_in, 16)
            pe.wait_ge(uh_ready, KT * 3 + KT)
            for c in range(2):
                for kt in range(KT):
                    ins = mm(B[0][:, 8 * c:8 * c + 8], v32[:, kt, c * 128:(c + 1) * 128], rt[:, kt * 8:kt * 8 + 8],
                             start=(kt == 0), stop=(kt == KT - 1))
            ins.then_inc(rt_mm, 1)
            for g in range(4):
                for k in range(4):
                    kt = 4 * (g % 2) + k
                    ins = nc.tensor.transpose(B[2 + g][:, k * 128:(k + 1) * 128], v32[:, kt, (g // 2) * 128:(g // 2 + 1) * 128], ident)
                ins.then_inc(vtok_tr, 1)
            pe.wait_ge(mask_ready, 1)
            mm(B[1][:, 0:8], tri, r_mask[:, 0:8], start=True, stop=True)
            mm(B[1][:, 8:16], tri, r_mask[:, 8:16], start=True, stop=False)
            mm(B[1][:, 8:16], ones[:], r_mask[:, 0:8], start=False, stop=True)
            mm(B[1][:, 16:24], ones[:], r_mask[:, 0:8], start=True, stop=False)
            mm(B[1][:, 16:24], ones[:], r_mask[:, 8:16], start=False, stop=True).then_inc(pos_mm, 1)
            pe.wait_ge(vtok_ev, 4)
            pe.wait_ge(route_ready, 1)
            npass = pe.value_load(npass_i[0:1, 0:1], min_val=1, max_val=2)
            S_M = S0["moe"]
            with pe.Fori(0, npass) as ps:
                with pe.Fori(0, NE) as e:
                    it = ps * NE + e
                    pe.wait_ge(p_ready, it + 1)
                    for g in range(2):
                        for k in range(4):
                            kt = 4 * g + k
                            for c in range(2):
                                ins = mm(B[4 + g][:, k * 128:(k + 1) * 128], vtok[:, c, kt * 128:(kt + 1) * 128],
                                         pbuf[:, c, :], start=(c == 0), stop=(c == 1))
                        ins.then_inc(xg_mm, 1)
                    pe.wait_ge(sc_ev, it * 4 + 4)
                    for c in range(2):
                        ins = nc.tensor.transpose(B[3][:, c * 128:(c + 1) * 128], pw[:, c, :], ident)
                    ins.then_inc(pwt_tr, 1)
                    for g in range(2):
                        pe.wait_ge(xg_l, it * 2 + (g + 1))

                    def hidden_tr(c):
                        pe.wait_ge(mh_ready, it * FC + (c + 2))
                        for k in range(4):
                            ins = nc.tensor.transpose(B[4 + c % 2][:, k * 128:(k + 1) * 128],
                                                      mh[:, c % 2, k * 128:(k + 1) * 128], ident)
                        ins.then_inc(ht_tr, 1)

                    s = 0
                    for n, (kind, c, b) in enumerate(MOE_ORDER):
                        if b == 0 and kind == "u" and c >= 1:
                            hidden_tr(c - 1)
                        if b == 0 and kind == "u" and c == 1:
                            pe.wait_ge(pwt_ev, it + 1)
                        if b == 0 and kind == "d":
                            if c == FC - 1:
                                hidden_tr(c)
                            pe.wait_ge(ht_l, it * FC + (c + 1))
                        for half in range(2):
                            pe.wait_ge(lo_done, it * MOE_S + (S_M + s + 1))
                            wh, wl = wsub(S_M + s)
                            if kind == "d":
                                ft = 2 * b + half
                                lh, ll = (w[:, c % 2, ft * 128:(ft + 1) * 128] for w in (ht_hi, ht_lo))
                                first, final = (c == 0 and ft == 0), (c == FC - 1 and ft == 3)
                                for nb in range(2):
                                    cc = slice(nb * 512, (nb + 1) * 512)
                                    mm(B[6 + nb][:], lh, wh[:, cc], start=first, stop=False)
                                    mm(B[6 + nb][:], lh, wl[:, cc], start=False, stop=False)
                                for nb in range(2):
                                    ins = mm(B[6 + nb][:], ll, wh[:, nb * 512:(nb + 1) * 512], start=False, stop=final)
                            else:
                                bank = B[2 * (c % 2) + (kind == "u")]
                                for kk in range(2):
                                    kt = 4 * b + 2 * half + kk
                                    ins = mm3(bank[:], xg_hi[:, kt, :], xg_lo[:, kt, :], wh[:, kk * 512:(kk + 1) * 512],
                                              wl[:, kk * 512:(kk + 1) * 512], kt == 0, kt == KT - 1)
                            ins.then_inc(sub_used, 1)
                            s += 1
                    pe.wait_ge(y_ev, it * 2 + 2)
                    for g in range(4):
                        for k in range(2):
                            kt = 2 * g + k
                            ins = mm(B[g][:, k * 256:(k + 1) * 256], ybuf[:, kt * 128:(kt + 1) * 128], pwt, start=True, stop=True)
                        ins.then_inc(sc_mm, 1)
            stats(4, CTX)
            spread(4, CTX)
            pe.wait_ge(hn_ready, KT * 4 + KT)
            for c in range(2):
                for g in range(2):
                    for k in range(4):
                        ins = nc.tensor.transpose(B[2 + 2 * c + g][:, k * 128:(k + 1) * 128],
                                                  v32[:, 4 * g + k, c * 128:(c + 1) * 128], ident)
                    ins.then_inc(out_tr, 1)


def pooling_matrices():
    import numpy as np
    def line(n, k):
        m = np.zeros((n, n))
        for t in range(n):
            lo, hi = max(t - k // 2, 0), min(t + k - 1 - k // 2 + 1, n)
            m[lo:hi, t] = 1.0 / (hi - lo)
        return m
    mats = np.zeros((2, 256, 4, 256))
    for g, k in enumerate((2, 4, 8, 16)):
        mats[0, :, g, :] = line(CTX, k) - np.eye(CTX)
        mats[1, :, g, :] = np.kron(line(LAT // 64, k), line(64, k)) - np.eye(LAT)
    return np.ascontiguousarray(mats.reshape(2, 2, 128, 4, 256).transpose(0, 2, 1, 3, 4), dtype=np.float32)


def level_masks():
    import numpy as np
    out = np.zeros((128, 2, LEVELS, 64), np.float32)
    s = np.arange(128)[:, None]
    t = np.arange(64)[None, :]
    for L in range(LEVELS):
        m = 1 << L
        same = (s // (2 * m)) == (t // m)
        out[:, 0, L] = same & ((s // m) % 2 == 0)
        out[:, 1, L] = same & ((s // m) % 2 == 1)
    return out.reshape(128, -1)


def kernel(**inputs):
    import numpy as np
    import concourse.bacc as bacc
    from concourse.bass_utils import run_bass_kernel_spmd

    a = {k: np.ascontiguousarray(v) for k, v in inputs.items()}
    rows = lambda v: v.reshape(-1, 128)
    vecs = np.concatenate([rows(a["b_ada"]), rows(a["norm_w"]), rows(a["hgrn_lb_raw"]), rows(a["hgrn_norm_w"]),
                           rows(a["pool_scale"]), rows(a["final_norm_w"]), rows(a["c_ctx"]), rows(a["c"])])
    i = np.arange(128)
    cf32 = np.concatenate([np.eye(128), (i[:, None] < i[None, :]), np.tile(i, (128, 1)),
                           np.tile(np.arange(8), (128, 1))], axis=1).astype(np.float32)
    ins = [("x", a["x"][0]), ("ctx_in", a["ctx"][0]), ("vecs", vecs), ("w_ada", a["w_ada"]), ("w_in", a["w_in"]),
           ("w_pool", a["w_pool"]), ("w_out", a["w_out"]), ("ffn_wg", a["ffn_wg"][0]), ("ffn_wu", a["ffn_wu"][0]),
           ("ffn_wd", a["ffn_wd"][0]), ("router_w", a["router_w"][0]), ("moe_wg", a["moe_wg"][0]),
           ("moe_wu", a["moe_wu"][0]), ("moe_wd", a["moe_wd"][0]), ("cf32", cf32),
           ("pool_mats", pooling_matrices()), ("masks", level_masks())]
    nc = bacc.Bacc("TRN2", target_bir_lowering=False, num_devices=1)
    arrays, aps = {}, []
    for name, v in ins:
        arrays[f"in_{name}"] = v
        aps.append(nc.dram_tensor(f"in_{name}", v.shape, mybir.dt.from_np(v.dtype), kind="ExternalInput").ap())
    o = nc.dram_tensor("out_lat", (LAT, D), mybir.dt.float32, kind="ExternalOutput").ap()
    bass_hybrid_trunk(nc, *aps, o)
    r = run_bass_kernel_spmd(nc, [arrays], core_ids=[0])
    return r.results[0]["out_lat"].reshape(1, LAT, D)
```

```python
import concourse.bass as bass
from concourse import mybir
from contextlib import ExitStack

D = 1024
KT = D // 128
CTX = LAT = 256
NTOK = CTX + LAT
HEADS = 4
HD = 128
NCH = NTOK // 128
LEVELS = 7
NADA = 6
ADA_BLKS = NADA * KT
F_DENSE = 2816
F_EXP = 3584
NE = 8
DEPTH = 2
EPS = 1e-6
UNIT = 2048
SUB = UNIT // 2
NR = 4
NRM = 6
NS = 4
ADA_G = NADA * D // 512
FFN_SUBS = [(0, 0), (0, 1), (1, 0), (2, 0), (3, 0), (3, 1), (1, 1), (2, 1)]
FFN_FREE = [max(k for k, (u_, _) in enumerate(FFN_SUBS) if u_ == u) + 1 for u in range(4)]
FFN_IT = F_DENSE // 256
LAST_F = 3
DOWN_U = F_DENSE // 256
FC = F_EXP // 512
SLOTS = 128
V_BADA, V_NORM, V_LB, V_HNW, V_PSC, V_FIN, V_C = 0, 96, 128, 144, 152, 160, 168
V_ROWS = 184


MOE_ORDER = [("g", 0, 0), ("g", 0, 1), ("u", 0, 0), ("u", 0, 1)]
for _c in range(1, FC):
    MOE_ORDER += [("g", _c, 0), ("g", _c, 1), ("u", _c, 0), ("u", _c, 1), ("d", _c - 1, 0), ("d", _c - 1, 1)]
MOE_ORDER += [("d", FC - 1, 0), ("d", FC - 1, 1)]
MOE_U = len(MOE_ORDER)
MOE_S = 2 * MOE_U
assert MOE_U % NRM == 0 and MOE_S % NS == 0


FIRST = [("a", g) for g in range(6)] + [("p", 0), ("p", 1)]
for _g in range(6, ADA_G):
    FIRST += [("a", _g), ("p", _g - 4)]
assert FIRST[-1] == ("p", 2 * HEADS - 1)
FIRST_UNITS, FIRST_SUBS, FIRST_POS = [], [], {}
for _kind, _n in FIRST:
    FIRST_POS[_kind, _n] = len(FIRST_SUBS)
    for _k in range(4 if _kind == "a" else 1):
        _unit = ("a", _n, _k // 2) if _kind == "a" else ("p", _n // 2, 0)
        if _unit not in FIRST_UNITS:
            FIRST_UNITS.append(_unit)
        FIRST_SUBS.append((FIRST_UNITS.index(_unit), _k % 2 if _kind == "a" else _n % 2, int(_kind == "p")))
SHIFT_SCALE_G = 2 * D // 512


def plan():
    seq = [("first", len(FIRST_UNITS), "f")]
    for l in range(DEPTH):
        if l:
            seq += [(f"f0{l}", 2, "s"), (f"q{l}", 2, "s")]
        seq += [(f"i{l}", 2, "s"), (f"f1{l}", 2, "s"), (f"pv{l}", 2, "s"), (f"g{l}", 2, "s"),
                (f"pm{l}", 2 - l, f"p{l}"), (f"wo{l}", 4, "s")]
        if l == 0:
            seq += [("ada1", 2, "s"), ("ffn", 4 * FFN_IT, "m"), ("down", DOWN_U, "s")]
    unit, sub, free = {}, {}, []
    u = s = 0
    for name, n, kind in seq:
        unit[name], sub[name] = u, s
        for i in range(n):
            if kind[0] == "p":
                free.append((kind, HEADS))
            elif kind == "f":
                free.append(("s", max(k for k, (u_, _, _) in enumerate(FIRST_SUBS) if u_ == i) + 1))
            elif kind == "m":
                free.append(("s", s + 8 * (i // 4) + FFN_FREE[i % 4]))
            else:
                free.append(("s", s + 2 * (i + 1)))
        s += 0 if kind[0] == "p" else 2 * n
        u += n
    unit["moe"], sub["moe"] = u, s
    return unit, sub, free


def bass_hybrid_trunk(nc, x, ctx_in, vecs, w_ada, w_in, w_pool, w_out, ffn_wg, ffn_wu, ffn_wd, router_w,
                      moe_wg, moe_wu, moe_wd, cf32, pool_mats, masks, out):
    f32, f32r, i32, ui32, u8 = (mybir.dt.float32, mybir.dt.float32r, mybir.dt.int32, mybir.dt.uint32,
                               mybir.dt.uint8)
    ACT = mybir.ActivationFunctionType
    ALU = mybir.AluOpType
    AX = mybir.AxisListType
    U0, S0, FREE = plan()

    st = ExitStack()
    with st:
        def sb(name, shape, dt=f32):
            return st.enter_context(nc.sbuf_tensor(name, shape, dt))

        def sem(name):
            return st.enter_context(nc.semaphore(name))

        h = sb("h", [128, KT, NTOK])
        raw = sb("raw", [128, NR, UNIT])
        w_hi = sb("w_hi", [128, NS, SUB], f32r)
        w_lo = sb("w_lo", [128, NS, SUB], f32r)
        u_hi = sb("u_hi", [128, KT, NTOK], f32r)
        u_lo = sb("u_lo", [128, KT, NTOK], f32r)
        cst = sb("cst", [128, 3 * 128 + 8])
        ident, tri, slot_iota, e_iota = cst[:, 0:128], cst[:, 128:256], cst[:, 256:384], cst[:, 384:392]
        ones = sb("ones", [128, 128])
        ones_d = sb("ones_d", [128, 128])
        ones_hd = sb("ones_hd", [128, 128])
        msk = sb("msk", [128, 2, LEVELS, 64], u8)
        vec = sb("vec", [128, V_ROWS])
        silu_c = sb("silu_c", [128, KT, 2])
        c4 = sb("c4", [128, KT, 128], f32r)
        sel = sb("sel", [4, 2])
        stat = sb("stat", [128, NCH * HEADS])
        mod = sb("mod", [128, 2, ADA_BLKS, 2])
        gain = sb("gain", [128, 2, 2, KT, 2])
        lb = sb("lb", [128, 2, 2 * HEADS])
        lb1 = sb("lb1", [128, 2, 2 * HEADS])
        lbt = sb("lbt", [128, 4, 8])
        wp = sb("wp", [128, 4, 128])
        eps_t = sb("eps_t", [128, 1])
        ARENA = 20992
        arena = sb("arena", [128, ARENA])
        top = [0]

        def take(n, at=None):
            if at is None:
                at = top[0]
                top[0] += n
            assert at + n <= ARENA
            return at

        a_q, a_f0, a_f1, a_t2 = take(2048), take(2048), take(2048), take(1024)
        a_qp, a_ks, a_a, a_v = take(2048), take(2048), take(2048), take(2048)
        a_sg, a_pv, a_s = take(2048), take(2048), take(1536)

        def ar(at, n):
            return arena[:, at:at + n]

        q_t = ar(a_q, 2048)
        f_t = [ar(a_f0, 2048), ar(a_f1, 2048)]
        t2 = ar(a_t2, 1024)
        qp, ks, amat = ar(a_qp, 2048), ar(a_ks, 2048), ar(a_a, 2048)
        v_t = ar(a_v, 2048).rearrange("p (c n) -> p c n", c=NCH)
        sg = ar(a_sg, 2048).rearrange("p (h n) -> p h n", h=HEADS)
        pv = ar(a_pv, 2048).rearrange("p (c n) -> p c n", c=NCH)
        s_t = ar(a_s, 1536).rearrange("p (c h n) -> p c h n", c=3, h=HEADS)
        o_t = ar(a_f0, 2048).rearrange("p (h n) -> p h n", h=HEADS)
        diff = ar(a_q, 2048).rearrange("p (g n) -> p g n", g=4)
        odiag = ar(a_qp, 2048).rearrange("p (h c n) -> p h c n", h=HEADS, n=128)
        sq_o = ar(a_ks, 2048).rearrange("p (h n) -> p h n", h=HEADS)
        a32 = ar(a_a, 2048).rearrange("p (h n) -> p h n", h=HEADS)
        sq = ar(a_sg, 1024).rearrange("p (b n) -> p b n", b=2)
        u32 = ar(a_pv, 2048).rearrange("p (b n) -> p b n", b=4)
        ndiag = ar(a_v, 512).rearrange("p (c n) -> p c n", n=128)
        sq_sum = ar(a_v + 512, 512)
        row = ar(a_s, 1024).rearrange("p (b n) -> p b n", b=2)
        vrow = ar(a_q, 256).rearrange("p (b n) -> p b n", b=2)
        xin = ar(a_qp, 4096).rearrange("p (c n) -> p c n", c=NCH)
        msk_in = ar(a_t2, 2 * LEVELS * 64)
        a_hid = 0
        hid = ar(a_hid, 22 * NTOK).rearrange("p (f n) -> p f n", f=22)
        sil = ar(22 * NTOK, 1024).rearrange("p (b n) -> p b n", b=2)
        assert 22 * NTOK + 1024 <= a_v
        mraw = ar(0, 2 * UNIT).rearrange("p (b n) -> p b n", b=2)
        m0 = 2 * UNIT
        v32 = ar(m0, 2048).rearrange("p (k n) -> p k n", k=KT)
        vtok = ar(m0 + 2048, 2048).rearrange("p (c n) -> p c n", c=2)
        yacc = ar(m0 + 4096, 2048).rearrange("p (k n) -> p k n", k=KT)
        ybuf = ar(m0 + 6144, 1024)
        assert m0 + 7168 <= a_v
        m1 = a_v + 512
        msil = ar(m1, 512)
        mh = ar(m1 + 512, 1024).rearrange("p (b n) -> p b n", b=2)
        assert m1 + 1536 <= a_sg
        m2 = a_sg + 1024
        pbuf = ar(m2, 256).rearrange("p (c n) -> p c n", c=2)
        pw = ar(m2 + 256, 256).rearrange("p (c n) -> p c n", c=2)
        pwt = ar(m2 + 512, 256)
        rt = ar(m2 + 768, 256)
        assert m2 + 1024 <= a_pv
        xg_hi = u_hi[:, 0:2, :].rearrange("p k n -> p (k n)").rearrange("p (k n) -> p k n", k=KT)
        xg_lo = u_lo[:, 0:2, :].rearrange("p k n -> p (k n)").rearrange("p (k n) -> p k n", k=KT)
        ht_hi, ht_lo = u_hi[:, 2:4, :], u_lo[:, 2:4, :]
        npass_i = sb("npass_i", [128, 1], i32)
        r_log, r_top, r_idf = rt[:, 64:80], rt[:, 80:96], rt[:, 112:128]
        r_idx = rt[:, 96:112].bitcast(ui32)
        r_d, r_e, r_w = rt[:, 128:130], rt[:, 130:132], rt[:, 132:136]
        r_m = rt[:, 136:168].rearrange("p (k n) -> p k n", k=2)
        r_mask, r_comb = rt[:, 168:184], rt[:, 184:200]
        r_pos = rt[:, 200:200 + 2 * (NE + 1)].rearrange("p (c e) -> p c e", c=2)
        M_EVENTS = {3: [("gate", 0), ("scatter", 0)], 4: [("scatter", 1)], 5: [("slots", 0)], 7: [("up", 0), ("weights", 0)]}
        for n_, (kind, c_, b_) in enumerate(MOE_ORDER):
            if b_ == 1 and n_ > 3:
                ev = M_EVENTS.setdefault(2 * n_ + 1, [])
                if kind == "g":
                    ev += [("gate", c_), ("ht", c_ - 1)]
                elif kind == "u":
                    ev += [("up", c_)] + [("gather", 0)] * (c_ == FC - 1)
                elif c_ == FC - 2:
                    ev += [("ht", FC - 1)]
        osb = ar(0, 2048).rearrange("p (c n) -> p c n", c=2)

        B = [st.enter_context(nc.psum_tensor(f"bank{i}", [128, 512], f32)) for i in range(8)]

        SB = [B[0], B[1], B[6], B[7]]

        vec_in, const_in, mask_in, x_in = sem("vec_in"), sem("const_in"), sem("mask_in"), sem("x_in")
        raw_in = [sem(f"raw_in{i}") for i in range(NR)]
        hi_done, lo_done, sub_used = sem("hi_done"), sem("lo_done"), sem("sub_used")
        row_ev, row_used = sem("row_ev"), sem("row_used")
        dve_step = sem("dve_step")
        vec_tr, x_tr, vec_ready, silu_ready = sem("vec_tr"), sem("x_tr"), sem("vec_ready"), sem("silu_ready")
        c_zero, c_hi, c_lo = sem("c_zero"), sem("c_hi"), sem("c_lo")
        mod_ready, ones_ready = sem("mod_ready"), sem("ones_ready")
        h_ready = sem("h_ready")
        sq_ready = sem("sq_ready")
        sq_used = sem("sq_used")
        sq_summed = sem("sq_summed")
        mean_sq = sem("mean_sq")
        inv_ready = sem("inv_ready")
        rstd_ready = sem("rstd_ready")
        diag_ready = sem("diag_ready")
        bcast_mm = sem("bcast_mm")
        hn_ready = sem("hn_ready")
        uh_ready = sem("uh_ready")
        u_ready = sem("u_ready")
        per_layer = lambda name: [sem(f"{name}{l}") for l in range(DEPTH)]
        proj_ev, pv_ev, i_ev = per_layer("proj_ev"), per_layer("pv_ev"), per_layer("i_ev")
        scan_ready = [[sem(f"scan_ready{l}{d}") for d in range(2)] for l in range(DEPTH)]
        diag_mm = [[sem(f"diag_mm{l}{d}") for d in range(2)] for l in range(DEPTH)]
        diag_ev = [[sem(f"diag_ev{l}{d}") for d in range(2)] for l in range(DEPTH)]
        lvl_mm = [[sem(f"lvl_mm{l}{d}") for d in range(2)] for l in range(DEPTH)]
        lvl_ev = [[sem(f"lvl_ev{l}{d}") for d in range(2)] for l in range(DEPTH)]
        kst_tr = [[sem(f"kst_tr{l}{d}") for d in range(2)] for l in range(DEPTH)]
        kst_ev = [[sem(f"kst_ev{l}{d}") for d in range(2)] for l in range(DEPTH)]
        st_mm = [[sem(f"st_mm{l}{d}") for d in range(2)] for l in range(DEPTH)]
        st_ev = [[sem(f"st_ev{l}{d}") for d in range(2)] for l in range(DEPTH)]
        o_mm = [[sem(f"o_mm{l}{d}") for d in range(2)] for l in range(DEPTH)]
        o_ev = [[sem(f"o_ev{l}{d}") for d in range(2)] for l in range(DEPTH)]
        diff_mm, diff_ev, pool_mm = per_layer("diff_mm"), per_layer("diff_ev"), per_layer("pool_mm")
        pool_hi, pool_lo = per_layer("pool_hi"), per_layer("pool_lo")
        osq, oms, oinv, orstd, odg, obc, a_f = (per_layer("osq"), per_layer("oms"), per_layer("oinv"),
                                                per_layer("orstd"), per_layer("odg"), per_layer("obc"), per_layer("a_f"))
        a_hi, a_lo = per_layer("a_hi"), per_layer("a_lo")
        sil_ready, hid_ready = sem("sil_ready"), sem("hid_ready")
        hs_hi, hs_lo, down_mm = sem("hs_hi"), sem("hs_lo"), sem("down_mm")
        rt_mm, vtok_tr, vtok_ev, mask_ready, pos_mm, route_ready = (
            sem("rt_mm"), sem("vtok_tr"), sem("vtok_ev"), sem("mask_ready"), sem("pos_mm"), sem("route_ready"))
        d_ready, e_ready, rt_in = sem("d_ready"), sem("e_ready"), sem("rt_in")
        p_ready, pw_ready, xg_mm, xg_h, xg_l = sem("p_ready"), sem("pw_ready"), sem("xg_mm"), sem("xg_h"), sem("xg_l")
        msil_ready, mh_ready, ht_tr, ht_h, ht_l = (sem("msil_ready"), sem("mh_ready"), sem("ht_tr"), sem("ht_h"),
                                                   sem("ht_l"))
        y_ev, pwt_tr, pwt_ev, sc_mm, sc_ev = sem("y_ev"), sem("pwt_tr"), sem("pwt_ev"), sem("sc_mm"), sem("sc_ev")
        out_tr, out_ev, out_dma = sem("out_tr"), [sem("out_ev_act"), sem("out_ev_dve")], sem("out_dma")
        rw_in, wp_in = sem("rw_in"), sem("wp_in")
        mraw_in = [sem(f"mraw_in{i}") for i in range(NRM)]
        slot_step = sem("slot_step")

        def m_slot(r):
            return raw[:, (U0["moe"] + r) % NR, :] if r < NR else mraw[:, r - NR, :]

        block = st.enter_context(nc.Block())

        class Steps:
            def __init__(self, eng, s):
                self.eng, self.s, self.n = eng, s, 0

            def __call__(self, ins):
                self.n += 1
                ins.then_inc(self.s, 1)
                self.eng.wait_ge(self.s, self.n)

        MIX, FFN = [0, 2], [1, 3]
        c0s = [0, CTX]
        outs_ch = [[0, 1, 2, 3], [2, 3]]
        order = [[0, 1, 2, 3], [1, 0, 3, 2]]

        def tiles(l):
            return [c * HEADS + hh for c in outs_ch[l] for hh in range(HEADS)]

        def seg(ap, lo_tile, n_tiles, m, half):
            return ap[:, lo_tile * 128:(lo_tile + n_tiles) * 128].rearrange(
                "p (s b m) -> p s b m", b=2, m=m)[:, :, half, :]

        def tbuf(d, L):
            src = f_t[d] if L % 2 == 0 else t2
            return src[:, 0:2048 >> L]

        @block.sync
        def _(sp):
            sp.dma_start(vrow[0:96, 0, :], vecs[0:96, :]).then_inc(vec_in, 16)
            sp.dma_start(vrow[0:88, 1, :], vecs[96:184, :]).then_inc(vec_in, 16)
            sp.dma_start(cst[:], cf32).then_inc(const_in, 16)
            sp.dma_start(xin[:, 0:2, :], ctx_in.rearrange("(c p) n -> p c n", p=128)).then_inc(x_in, 16)
            sp.dma_start(xin[:, 2:4, :], x.rearrange("(c p) n -> p c n", p=128)).then_inc(x_in, 16)

            def slot_free(u):
                if u >= NR:
                    kind, n = FREE[u - NR]
                    if kind == "s":
                        sp.wait_ge(lo_done, n)
                    else:
                        sp.wait_ge(diff_mm[int(kind[1])], n)

            def load(u, dst_shape, src):
                slot_free(u)
                pat, kw = dst_shape
                sp.dma_start(raw[:, u % NR, :].rearrange(pat, **kw), src).then_inc(raw_in[u % NR], 16)

            K8 = ("p (k n) -> p k n", dict(k=8))
            K4 = ("p (k n) -> p k n", dict(k=4))
            K2 = ("p (k n) -> p k n", dict(k=2))
            ada = [w_ada[l].rearrange("(k p) n -> p k n", p=128) for l in range(2)]
            win = [w_in[l].rearrange("(k p) n -> p k n", p=128) for l in range(2)]
            wo = [w_out[l].rearrange("(k p) n -> p k n", p=128) for l in range(2)]
            for u, (kind, n, b) in enumerate(FIRST_UNITS):
                if kind == "a":
                    load(u, K4, ada[0][:, 4 * b:4 * b + 4, 512 * n:512 * (n + 1)])
                else:
                    col = (2 * 512 if n < 2 else 0) + 256 * (n % 2)
                    load(u, K8, win[0][:, :, col:col + 256])
                if u == NR - 1:
                    sp.dma_start(msk_in, masks).then_inc(mask_in, 16)
            for l in range(2):
                def tok_major(name, col):
                    for b in range(2):
                        load(U0[name] + b, K4, win[l][:, 4 * b:4 * b + 4, col:col + 512])

                def feat_major(name, col):
                    for b in range(2):
                        load(U0[name] + b, K8, win[l][:, :, col + 256 * b:col + 256 * (b + 1)])

                if l:
                    feat_major(f"f0{l}", 2 * 512)
                    feat_major(f"q{l}", 0)
                tok_major(f"i{l}", 512)
                feat_major(f"f1{l}", 3 * 512)
                tok_major(f"pv{l}", 5 * 512)
                feat_major(f"g{l}", 4 * 512)
                for b in range(2 - l):
                    load(U0[f"pm{l}"] + b, ("p (s g n) -> p s g n", dict(s=2, g=4)), pool_mats[1 - (1 - l) * (1 - b)])
                if l == 1:
                    sp.wait_ge(pool_mm[0], 4)
                sp.dma_start(wp[:], w_pool[l].rearrange("g c d -> c g d")).then_inc(wp_in, 16)
                for b in range(4):
                    load(U0[f"wo{l}"] + b, K8, wo[l][:, :, 256 * b:256 * (b + 1)])
                if l == 0:
                    wg = ffn_wg.rearrange("(k p) n -> p k n", p=128)
                    wu = ffn_wu.rearrange("(k p) n -> p k n", p=128)
                    wd = ffn_wd.rearrange("(f p) n -> p f n", p=128)
                    for b in range(2):
                        load(U0["ada1"] + b, K4, ada[1][:, 4 * b:4 * b + 4, 0:512])
                    base = U0["ffn"]
                    for k, (pat, src) in enumerate([(K4, ada[1][:, 0:4, 512:1024]), (K8, wg[:, :, 0:256]),
                                                    (K8, wu[:, :, 0:256]), (K4, ada[1][:, 4:8, 512:1024])]):
                        load(base + k, pat, src)
                    with sp.Fori(1, FFN_IT) as i:
                        for k in range(4):
                            r = (base + k) % NR
                            sp.wait_ge(lo_done, i * 8 + (S0["ffn"] + FFN_FREE[k] - 8))
                            if k in (1, 2):
                                kk, src = 8, (wg, wu)[k - 1][:, :, bass.ds(i * 256, 256)]
                            else:
                                kk, src = 4, ada[1][:, 4 * (k // 3):4 * (k // 3) + 4, bass.ds(i * 512 + 512, 512)]
                            sp.dma_start(raw[:, r, :].rearrange("p (k n) -> p k n", k=kk), src).then_inc(raw_in[r], 16)
                    for b in range(DOWN_U):
                        load(U0["down"] + b, K2, wd[:, 2 * b:2 * b + 2, :])
            moe = [w.rearrange("e (k p) n -> e p k n", p=128) for w in (moe_wg, moe_wu, moe_wd)]

            def moe_load(n, e):
                kind, c, b = MOE_ORDER[n]
                w = moe["gud".index(kind)][bass.ds(e, 1)] if not isinstance(e, int) else moe["gud".index(kind)][e:e + 1]
                if kind == "d":
                    src, kk = w[:, :, 4 * c + 2 * b:4 * c + 2 * b + 2, :], 2
                else:
                    src, kk = w[:, :, 4 * b:4 * b + 4, 512 * c:512 * (c + 1)], 4
                sp.dma_start(m_slot(n % NRM).rearrange("p (k n) -> p k n", k=kk),
                             src.rearrange("e p k n -> p (e k) n")).then_inc(mraw_in[n % NRM], 16)

            S_M = S0["moe"]
            for n in range(NRM):
                if n == NR:
                    sp.wait_ge(a_lo[1], HEADS)
                    sp.dma_start(rt[:, 0:64].rearrange("p (k n) -> p k n", k=KT),
                                 router_w.rearrange("(k p) n -> p k n", p=128)).then_inc(rw_in, 16)
                if n < NR:
                    sp.wait_ge(lo_done, S_M - 2 * NR + 2 * n + 2)
                moe_load(n, 0)

            def moe_pass(s0, first):
                for n in range(first, NRM):
                    sp.wait_ge(lo_done, s0 + 2 * (n - NRM + 1))
                    moe_load(n, 0)
                with sp.Fori(2, NE + 1) as e2:
                    for n in range(NRM, MOE_U + NRM):
                        if MOE_ORDER[n % MOE_U] != ("d", 0, 0):
                            upto = n + (MOE_ORDER[(n + 1) % MOE_U] == ("d", 0, 0))
                            sp.wait_ge(lo_done, e2 * MOE_S + (s0 - 2 * MOE_S + 2 * (upto - NRM + 1)))
                        moe_load(n % MOE_U, e2 + (n // MOE_U - 2))
                for n in range(NRM, MOE_U + AHEAD):
                    sp.wait_ge(lo_done, s0 + (NE - 1) * MOE_S + 2 * (n - NRM + 1))
                    moe_load(n % MOE_U, NE - 1 if n < MOE_U else 0)

            AHEAD = NS // 2
            moe_pass(S_M, NRM)
            sp.wait_ge(route_ready, 1)
            npass = sp.value_load(npass_i[0:1, 0:1], min_val=1, max_val=2)
            with sp.If(npass > 1):
                moe_pass(S_M + NE * MOE_S, AHEAD)
            sp.nop()
            for c in range(2):
                for e in range(2):
                    sp.wait_ge(out_ev[e], c + 1)
                sp.dma_start(out[128 * c:128 * (c + 1), :], osb[:, c, :]).then_inc(out_dma, 16)
            sp.wait_ge(out_dma, 32)

        def unit_of_sub(name, k):
            return U0[name] + k // 2, k % 2

        def phase_subs():
            seq = list(FIRST_SUBS)
            for l in range(DEPTH):
                for name, n, strided in ((f"f0{l}", 4 * l, 1), (f"q{l}", 4 * l, 1), (f"i{l}", 4, 0), (f"f1{l}", 4, 1),
                                         (f"pv{l}", 4, 0), (f"g{l}", 4, 1), (f"wo{l}", 8, 1)):
                    if not n:
                        continue
                    seq += [(*unit_of_sub(name, k), strided) for k in range(n)]
                if l == 0:
                    seq += [(*unit_of_sub("ada1", k), 0) for k in range(4)]
                    for i in range(FFN_IT):
                        seq += [(U0["ffn"] + 4 * i + u_, half, int(u_ in (1, 2))) for u_, half in FFN_SUBS]
                    seq += [(*unit_of_sub("down", k), 0) for k in range(2 * DOWN_U)]
            return seq

        SUBS = phase_subs()
        assert len(SUBS) == S0["moe"]

        def half_of(unit_ap, half, strided):
            if strided:
                return unit_ap.rearrange("p (k n) -> p k n", k=KT)[:, :, half * 128:(half + 1) * 128]
            return unit_ap[:, half * SUB:(half + 1) * SUB]

        def shaped(ap, strided):
            return ap.rearrange("p (k n) -> p k n", k=KT) if strided else ap

        @block.scalar
        def _(act):
            nxt = [0]

            def hi(i=0):
                j = nxt[0]
                nxt[0] += 1
                u, half, strided = SUBS[j]
                act.wait_ge(raw_in[u % NR], i * 16 + 16 * (u // NR + 1))
                if j >= NS:
                    act.wait_ge(sub_used, i * 8 + (j - NS + 1))
                nc.scalar.activation(shaped(w_hi[:, j % NS, :], strided), half_of(raw[:, u % NR, :], half, strided),
                                     ACT.Copy).then_inc(hi_done, 1)

            def his(n):
                for _ in range(n):
                    if nxt[0] < len(SUBS):
                        hi()

            def rows(g, i=0, single=False):
                b = 0 if single else g % 2
                last_sub = FIRST_POS["a", g] if g < ADA_G else S0["ada1"] if g == ADA_G else S0["ffn"] + 8 * (g - ADA_G - 1) + 2
                act.wait_ge(sub_used, i * 8 + (last_sub + 4))
                if single and g > ADA_G or g >= 2:
                    act.wait_ge(row_used, i + (g if single else g - 1))
                nc.scalar.activation(row[0:4, b, :], B[4 + b][0:4, :], ACT.Copy).then_inc(row_ev, 1)

            def mhi(s, it=0):
                n = s // 2
                act.wait_ge(mraw_in[n % NRM], it * (16 * MOE_U // NRM) + 16 * (n // NRM + 1))
                act.wait_ge(sub_used, it * MOE_S + (S0["moe"] + s - NS + 1))
                nc.scalar.activation(w_hi[:, (S0["moe"] + s) % NS, :], half_of(m_slot(n % NRM), s % 2, 0),
                                     ACT.Copy).then_inc(hi_done, 1)

            def square(n, c0, kt):
                act.wait_ge(h_ready, KT * n + kt + 1)
                if kt >= 2:
                    act.wait_ge(sq_used, KT * n + kt - 1)
                nc.scalar.activation(sq[:, kt % 2, c0:NTOK], h[:, kt, c0:NTOK], ACT.Square).then_inc(sq_ready, 1)

            def root(n, c0):
                act.wait_ge(inv_ready, n + 1)
                nc.scalar.activation(stat[:, c0 // 128:NCH], stat[:, c0 // 128:NCH], ACT.Sqrt).then_inc(rstd_ready, 1)

            def modulated(n, l, w):
                for kt in range(KT):
                    act.wait_ge(hn_ready, KT * n + kt + 1)
                    for s_, a, b in ((0, 0, CTX), (1, CTX, NTOK)):
                        ins = nc.scalar.activation(u_hi[:, kt, a:b], u32[:, kt % 4, a:b], ACT.Identity,
                                                   bias=mod[:, l, 3 * w * KT + kt, s_:s_ + 1])
                    ins.then_inc(uh_ready, 1)

            act.wait_ge(vec_ready, 1)
            nc.scalar.activation(silu_c[:].rearrange("p k s -> p s k"),
                                 vec[:, V_C:V_C + 16].rearrange("p (s k) -> p s k", s=2), ACT.Silu).then_inc(silu_ready, 1)
            act.wait_ge(silu_ready, 1)
            act.wait_ge(c_zero, 1)
            nc.scalar.activation(c4[:, :, 0:2], silu_c[:], ACT.Copy).then_inc(c_hi, 1)
            act.wait_ge(d_ready, 1)
            nc.scalar.activation(lbt[:, 0:2, :], lbt[:, 0:2, :], ACT.Exp).then_inc(e_ready, 1)

            for kt in range(KT):
                square(0, 0, kt)
                if kt % 2:
                    his(1)

            def first():
                for kind, n in FIRST:
                    if kind == "p":
                        mixer_proj(0, "f0" if n < 4 else "q", n % 4, FIRST_POS[kind, n])
                        continue
                    for k in range(4):
                        if k == 3:
                            rows(n)
                        his(1)
                        if n == SHIFT_SCALE_G + 1 and k == 1:
                            modulated(0, 0, 0)
                    if n == 0:
                        root(0, 0)

            def mixer_proj(l, kind, hh, j):
                c0 = c0s[l]
                act.wait_ge(sub_used, j + 1)
                bk = B[2 + hh % 2]
                if kind == "f0" or kind == "f1":
                    nc.scalar.activation(heads_view(f_t[int(kind[1])], hh, 0), bk[:].rearrange("p (c n) -> p c n", c=NCH),
                                         ACT.Sigmoid).then_inc(proj_ev[l], 1)
                elif kind == "q":
                    nc.scalar.activation(heads_view(q_t, hh, c0), bk[:, c0:].rearrange("p (c n) -> p c n", n=128),
                                         ACT.Copy, scale=HD ** -0.5).then_inc(proj_ev[l], 1)
                else:
                    nc.scalar.activation(sg[:, hh, c0:], bk[:, c0:], ACT.Silu).then_inc(proj_ev[l], 1)
                his(1)

            def heads_view(ap, hh, lo):
                return ap.rearrange("p (c h n) -> p c h n", c=NCH, h=HEADS)[:, lo // 128:, hh, :]

            def mixer(l):
                n, c0 = MIX[l], c0s[l]
                if l:
                    root(n, 0)
                    his(LAST_F)
                    modulated(n, l, 0)

                def proj(kind):
                    for hh in range(HEADS):
                        mixer_proj(l, kind, hh, S0[f"{kind}{l}"] + hh)

                def token_major(name, dst, chunks, ev, ks_):
                    for k in ks_:
                        act.wait_ge(sub_used, S0[name] + k + 1)
                        if k == 3:
                            for c in chunks:
                                nc.scalar.activation(dst[:, c, :], B[2 + c][:], ACT.Copy).then_inc(ev, 1)
                        his(1)

                if l:
                    proj("f0")
                    proj("q")
                else:
                    first()
                token_major(f"i{l}", v_t, range(NCH), i_ev[l], range(4))
                proj("f1")

                def keys_tm(d):
                    for g in range(3):
                        c = order[d][g]
                        act.wait_ge(kst_tr[l][d], g + 1)
                        nc.scalar.activation(ks[:, c * 512:(c + 1) * 512], SB[g][:], ACT.Copy).then_inc(kst_ev[l][d], 1)

                def pool_out(g):
                    act.wait_ge(pool_mm[l], g + 1)
                    nc.scalar.activation(u_hi[:, 4 + g, c0:], B[2 + g][:, c0:], ACT.Copy,
                                         scale=vec[:, V_PSC + 4 * l + g:V_PSC + 4 * l + g + 1]).then_inc(pool_hi[l], 1)

                keys_tm(0)
                token_major(f"pv{l}", pv, outs_ch[l], pv_ev[l], range(2))
                for n_, c in enumerate(outs_ch[l]):
                    act.wait_ge(o_mm[l][0], n_ + 1)
                    nc.scalar.activation(o_t[:, :, c * 128:(c + 1) * 128],
                                         SB[c][:].rearrange("p (h n) -> p h n", h=HEADS),
                                         ACT.Copy).then_inc(o_ev[l][0], 1)
                token_major(f"pv{l}", pv, outs_ch[l], pv_ev[l], range(2, 4))
                proj("g")
                for g in range(4):
                    act.wait_ge(diff_mm[l], g + 1)
                    nc.scalar.activation(diff[:, g, c0:], B[2 + g][:, c0:], ACT.Copy).then_inc(diff_ev[l], 1)
                pool_out(0)
                pool_out(1)
                keys_tm(1)
                pool_out(2)
                pool_out(3)
                act.wait_ge(o_ev[l][1], len(outs_ch[l]))
                for hh in range(HEADS):
                    nc.scalar.activation(sq_o[:, hh, c0:], o_t[:, hh, c0:], ACT.Square).then_inc(osq[l], 1)
                act.wait_ge(oinv[l], 1)
                nc.scalar.activation(stat[:], stat[:], ACT.Sqrt).then_inc(orstd[l], 1)
                for hh in range(HEADS):
                    act.wait_ge(a_f[l], hh + 1)
                    nc.scalar.activation(u_hi[:, hh, c0:], a32[:, hh, c0:], ACT.Copy).then_inc(a_hi[l], 1)
                base = S0[f"wo{l}"]
                for j in range(8):
                    act.wait_ge(sub_used, base + j + 1)
                    if l and j >= NS:
                        mhi(j - NS)
                    his(1)
                    square(FFN[l], c0, j)

            mixer(0)
            root(FFN[0], 0)
            rows(ADA_G, single=True)
            his(4)
            modulated(FFN[0], 0, 1)

            def ffn_step(i, loop=False):
                def block_silu(b):
                    act.wait_ge(sub_used, i * 8 + (S0["ffn"] + (2, 6)[b] + 1))
                    if loop or i:
                        act.wait_ge(hid_ready, i * 2 + (b - 1))
                    nc.scalar.activation(sil[:, b, :], B[2 * b][:], ACT.Silu).then_inc(sil_ready, 1)

                one = (lambda: hi(i - 1)) if loop else (lambda: his(1))
                one(), one()
                block_silu(0)
                one(), one(), one()
                rows(ADA_G + 1, i, single=True)
                one()
                block_silu(1)
                one(), one()

            ffn_step(0)
            j0 = nxt[0]
            with act.Fori(1, FFN_IT - 1) as i:
                ffn_step(i, True)
            nxt[0] = j0 + 8 * (FFN_IT - 2)
            ffn_step(FFN_IT - 1)
            for f in range(22):
                act.wait_ge(hid_ready, f + 1)
                act.wait_ge(sub_used, S0["down"] + max(0, f - KT + 1))
                nc.scalar.activation(u_hi[:, f % KT, :], hid[:, f, :], ACT.Copy).then_inc(hs_hi, 1)
                if f >= KT:
                    his(1)
            for f in range(KT - LAST_F):
                act.wait_ge(sub_used, S0["down"] + 22 - KT + f + 1)
                his(1)
            for kt in range(KT):
                square(MIX[1], 0, kt)
            mixer(1)
            root(FFN[1], CTX)
            for kt in range(KT):
                act.wait_ge(hn_ready, KT * FFN[1] + kt + 1)
                nc.scalar.activation(v32[:, kt, :], v32[:, kt, :], ACT.Identity,
                                     bias=mod[:, 1, 3 * KT + kt, 1:2]).then_inc(uh_ready, 1)

            act.wait_ge(rt_in, 1)
            nc.scalar.activation(r_e, r_d, ACT.Exp).then_inc(e_ready, 1)
            for g in range(4):
                act.wait_ge(vtok_tr, g + 1)
                nc.scalar.activation(vtok[:, g // 2, (g % 2) * 512:(g % 2 + 1) * 512], B[2 + g][:], ACT.Copy).then_inc(vtok_ev, 1)

            act.wait_ge(route_ready, 1)
            npass = act.value_load(npass_i[0:1, 0:1], min_val=1, max_val=2)

            def gathered(n):
                for g in range(2):
                    act.wait_ge(xg_mm, n * 2 + (g + 1))
                    nc.scalar.activation(xg_hi[:, 4 * g:4 * g + 4, :].rearrange("p k n -> p (k n)"), B[2 + g][:],
                                         ACT.Copy).then_inc(xg_h, 1)

            gathered(0)
            with act.Fori(0, npass) as ps:
                with act.Fori(0, NE) as e:
                    it = ps * NE + e
                    for s in range(MOE_S):
                        for what, c in M_EVENTS.get(s, ()):
                            if what == "gate":
                                act.wait_ge(sub_used, it * MOE_S + (S0["moe"] + s + 1))
                                act.wait_ge(mh_ready, it * FC + (c + 1))
                                nc.scalar.activation(msil, B[2 * (c % 2)][:], ACT.Silu).then_inc(msil_ready, 1)
                            elif what == "ht":
                                act.wait_ge(ht_tr, it * FC + (c + 1))
                                nc.scalar.activation(ht_hi[:, c % 2, :], B[4 + c % 2][:], ACT.Copy).then_inc(ht_h, 1)
                            elif what == "weights":
                                act.wait_ge(pwt_tr, it + 1)
                                nc.scalar.activation(pwt, B[6][:, 0:256], ACT.Copy).then_inc(pwt_ev, 1)
                            elif what == "gather":
                                gathered(it + 1)
                        if s == MOE_S - 1:
                            act.wait_ge(sub_used, it * MOE_S + (S0["moe"] + MOE_S))
                            nc.scalar.activation(ybuf[:, 0:512], B[6][:], ACT.Copy).then_inc(y_ev, 1)
                        mhi(s + NS, it)
            for kt in range(KT):
                square(4, CTX, kt)
            root(4, CTX)
            for g in range(2):
                act.wait_ge(out_tr, 2 * g + 1)
                nc.scalar.activation(osb[:, g, 0:512], B[2 + 2 * g][:], ACT.Copy).then_inc(out_ev[0], 1)

        @block.vector
        def _(dve):
            link = Steps(dve, dve_step)
            nxt = [0]

            def lo(i=0):
                j = nxt[0]
                nxt[0] += 1
                u, half, strided = SUBS[j]
                dve.wait_ge(hi_done, i * 8 + (j + 1))
                nc.vector.tensor_tensor(shaped(w_lo[:, j % NS, :], strided), half_of(raw[:, u % NR, :], half, strided),
                                        shaped(w_hi[:, j % NS, :], strided).bitcast(f32), ALU.subtract).then_inc(lo_done, 1)

            def los(n):
                for _ in range(n):
                    if nxt[0] < len(SUBS):
                        lo()

            def tt(out, a, b, op):
                return nc.vector.tensor_tensor(out, a, b, op)

            def bc(ap, m):
                return ap.unsqueeze(len(ap.shape)).broadcast_to((*ap.shape, m))

            def mlo(s, it=0):
                dve.wait_ge(hi_done, it * MOE_S + (S0["moe"] + s + 1))
                slot = (S0["moe"] + s) % NS
                tt(w_lo[:, slot, :], half_of(m_slot(s // 2 % NRM), s % 2, 0), w_hi[:, slot, :].bitcast(f32),
                   ALU.subtract).then_inc(lo_done, 1)

            def clear_experts(k):
                if k < 4:
                    nc.vector.memset(yacc[:, 2 * k:2 * k + 2, :], 0.0).then_inc(sc_ev, 1)
                elif k < 6:
                    nc.vector.memset(ybuf[:, 512 * (k - 4):512 * (k - 3)], 0.0).then_inc(y_ev, 1)
                elif k == 6:
                    nc.vector.memset(pwt, 0.0).then_inc(pwt_ev, 1)

            def gated(n_next, l, gi, kt, src, c0):
                parts = [(0, 0, CTX)] * (c0 == 0) + [(1, CTX, NTOK)]
                for w, a, b in parts:
                    ins = nc.vector.scalar_tensor_tensor(h[:, kt, a:b], src[:, a - NTOK + src.shape[1]:b - NTOK + src.shape[1]],
                                                         mod[:, l, gi * KT + kt, w:w + 1], h[:, kt, a:b], ALU.mult, ALU.add)
                ins.then_inc(h_ready, 1)

            def stats(n, c0):
                ch = slice(c0 // 128, NCH)
                dve.wait_ge(mean_sq, n + 1)
                link(nc.vector.tensor_scalar(stat[:, ch], B[6][:, ch], EPS, None, ALU.add))
                nc.vector.reciprocal(stat[:, ch], stat[:, ch]).then_inc(inv_ready, 1)
                dve.wait_ge(rstd_ready, n + 1)
                tt(ndiag[:, ch], ident.unsqueeze(1).broadcast_to((128, NCH - c0 // 128, 128)), bc(stat[:, ch], 128),
                   ALU.mult).then_inc(diag_ready, 1)

            def modulated(n, l, w):
                dve.wait_ge(bcast_mm, n + 1)
                for kt in range(KT + 2):
                    if kt < KT:
                        if kt >= 4:
                            dve.wait_ge(u_ready, KT * n + kt - 3)
                        for s_, a, b in ((0, 0, CTX), (1, CTX, NTOK)):
                            ins = nc.vector.scalar_tensor_tensor(u32[:, kt % 4, a:b], h[:, kt, a:b],
                                                                 gain[:, l, w, kt, s_:s_ + 1], B[6][:, a:b],
                                                                 ALU.mult, ALU.mult)
                        ins.then_inc(hn_ready, 1)
                    if kt >= 2:
                        k = kt - 2
                        dve.wait_ge(uh_ready, KT * n + k + 1)
                        for s_, a, b in ((0, 0, CTX), (1, CTX, NTOK)):
                            ins = nc.vector.scalar_tensor_tensor(u_lo[:, k, a:b], u32[:, k % 4, a:b],
                                                                 mod[:, l, 3 * w * KT + k, s_:s_ + 1],
                                                                 u_hi[:, k, a:b].bitcast(f32), ALU.add, ALU.subtract)
                        ins.then_inc(u_ready, 1)

            nc.vector.memset(ones[:], 1.0).then_inc(ones_ready, 1)
            nc.vector.memset(ones_d[:], 1.0 / D).then_inc(ones_ready, 1)
            nc.vector.memset(ones_hd[:], 1.0 / HD).then_inc(ones_ready, 1)
            dve.wait_ge(const_in, 16)
            nc.vector.memset(c4[:].bitcast(f32), 0.0).then_inc(c_zero, 1)
            tt(sel[:], ident[0:4, 0:2], ident[0:4, 2:4], ALU.add).then_inc(ones_ready, 1)
            dve.wait_ge(vec_tr, 2)
            nc.vector.tensor_copy(vec[:], B[6][:, 0:V_ROWS]).then_inc(vec_ready, 1)
            dve.wait_ge(vec_ready, 1)
            r0, r1 = vec[:, V_LB:V_LB + 8], vec[:, V_LB + 8:V_LB + 16]
            link(tt(lbt[:, 2, :], r0, r1, ALU.max))
            link(tt(lbt[:, 0, :], r0, lbt[:, 2, :], ALU.subtract))
            tt(lbt[:, 1, :], r1, lbt[:, 2, :], ALU.subtract).then_inc(d_ready, 1)
            dve.wait_ge(c_hi, 1)
            tt(c4[:, :, 2:4], silu_c[:], c4[:, :, 0:2].bitcast(f32), ALU.subtract).then_inc(c_lo, 1)
            for kt in range(KT):
                dve.wait_ge(x_tr, kt + 1)
                nc.vector.tensor_copy(h[:, kt, :], B[kt % 4][:]).then_inc(h_ready, 1)
            los(NS)
            mods = [0]

            def modulation(l, groups, ws):
                g0, g1 = groups
                b0, b1 = g0 * ADA_BLKS // ADA_G, g1 * ADA_BLKS // ADA_G
                dve.wait_ge(row_used, ADA_G * l + g1)
                link(tt(mod[:, l, b0:b1], B[7][:, 2 * b0:2 * b1].rearrange("p (b s) -> p b s", s=2),
                        bc(vec[:, V_BADA + ADA_BLKS * l + b0:V_BADA + ADA_BLKS * l + b1], 2), ALU.add))
                for w in ws:
                    ins = nc.vector.scalar_tensor_tensor(
                        gain[:, l, w], mod[:, l, (1 + 3 * w) * KT:(2 + 3 * w) * KT, :], 1.0,
                        bc(vec[:, V_NORM + (2 * l + w) * KT:V_NORM + (2 * l + w + 1) * KT], 2), ALU.add, ALU.mult)
                ins.then_inc(mod_ready, 1)
                mods[0] += 1
                dve.wait_ge(mod_ready, mods[0])

            def gate(l, d, hh):
                dve.wait_ge(proj_ev[l], 8 * d + hh + 1)
                fv = f_t[d].rearrange("p (c h n) -> p c h n", c=NCH, h=HEADS)[:, :, hh, :]
                ins = nc.vector.tensor_scalar(fv, fv, lb1[:, l, d * HEADS + hh:d * HEADS + hh + 1],
                                              lb[:, l, d * HEADS + hh:d * HEADS + hh + 1], ALU.mult, ALU.add)
                ins.then_inc(dve_step, 1)
                link.n += 1
                los(1)

            def first_stats():
                stats(0, 0)
                dve.wait_ge(e_ready, 1)
                e0, e1, t0, t1 = (lbt[:, k, :] for k in range(4))
                link(tt(t0, e0, e1, ALU.add))
                link(nc.vector.reciprocal(t1, t0))
                link(tt(e0, e0, t1, ALU.mult))
                link(tt(e1, e1, t1, ALU.mult))
                link(tt(lb[:, 0, :], e0, e0, ALU.subtract))
                link(tt(t0, e0, e1, ALU.add))
                link(tt(lb[:, 1, :], t0, e0, ALU.subtract))
                link(nc.vector.tensor_scalar(lb1[:], lb[:], -1.0, 1.0, ALU.mult, ALU.add))

                dve.wait_ge(mask_in, 16)
                link(nc.vector.tensor_copy(msk[:].rearrange("p a b n -> p (a b n)"), msk_in))

            def first():
                for kind, n in FIRST:
                    if kind == "p":
                        if n < 4:
                            gate(0, 0, n)
                        elif n < 7:
                            los(1)
                        continue
                    for k in range(4):
                        los(1)
                        if n == SHIFT_SCALE_G and k == 2:
                            modulation(0, (0, SHIFT_SCALE_G), [0])
                        if n == SHIFT_SCALE_G + 1 and k == 1:
                            modulated(0, 0, 0)
                    if n == 0:
                        first_stats()
                modulation(0, (SHIFT_SCALE_G, ADA_G), [1])

            def mixer(l):
                n, c0 = MIX[l], c0s[l]
                TL = tiles(l)
                t0, nt = TL[0], len(TL)
                def start(d):
                    link(nc.vector.tensor_scalar(ks, f_t[d], -1.0, 1.0, ALU.mult, ALU.add))
                    tt(qp[:, t0 * 128:], q_t[:, t0 * 128:], f_t[d][:, t0 * 128:], ALU.mult).then_inc(scan_ready[l][d], 1)

                if l:
                    stats(n, 0)
                    los(1)
                    modulated(n, l, 0)
                    los(LAST_F - 1)
                    for hh in range(HEADS):
                        gate(l, 0, hh)
                    los(3)
                else:
                    first()
                dve.wait_ge(dve_step, link.n)
                dve.wait_ge(proj_ev[l], 8)
                start(0)
                los(1)

                def scan(d, fill):
                    A3 = amat.rearrange("p (t n) -> p t n", n=128)
                    for g in range(nt // 4):
                        dve.wait_ge(diag_mm[l][d], g + 1)
                        tt(A3[:, t0 + 4 * g:t0 + 4 * g + 4, :], SB[g][:].rearrange("p (t n) -> p t n", t=4),
                           ident.unsqueeze(1).broadcast_to((128, 4, 128)), ALU.mult).then_inc(diag_ev[l][d], 1)
                    for L in range(LEVELS):
                        m = 1 << L
                        qh, kh = (1, 0) if d == 0 else (0, 1)
                        T = tbuf(d, L)
                        dve.wait_ge(lvl_mm[l][d], (L + 1) * (nt // 8))
                        T2 = T.rearrange("p (s b) -> p s b", b=2)
                        kv = seg(ks, 0, 16, m, kh)
                        tt(kv, kv, bc(T2[:, :, qh], m), ALU.mult)
                        qv = seg(qp, t0, nt, m, qh)
                        tt(qv, qv, bc(T2[:, (t0 * 128) // (2 * m):, kh], m), ALU.mult)
                        tt(tbuf(d, L + 1), T2[:, :, 0], T2[:, :, 1], ALU.mult).then_inc(scan_ready[l][d], 1)
                        fill(L)
                        if L == 0:
                            dve.wait_ge(diag_ev[l][d], nt // 4)
                        else:
                            dve.wait_ge(lvl_ev[l][d], L * (nt // 8))
                        for g in range(nt // 8):
                            bk = SB[2 * (L % 2) + g]
                            av = A3[:, t0 + 8 * g:t0 + 8 * g + 8, :].rearrange("p t (s b m) -> p t s b m", b=2, m=m)[:, :, :, qh, :]
                            mv = msk[:, d, L, :].unsqueeze(1).broadcast_to((128, 8, 64)).rearrange("p t (s m) -> p t s m", m=m)
                            dv = bk[:].rearrange("p (t s m) -> p t s m", t=8, m=m)
                            nc.vector.copy_predicated(av, mv, dv).then_inc(lvl_ev[l][d], 1)

                def fill0(L):
                    if L < 4:
                        los(1)
                    else:
                        gate(l, 1, L - 4)

                scan(0, fill0)
                gate(l, 1, 3)

                def states(d):
                    T = tbuf(d, LEVELS)
                    for g in range(3):
                        dve.wait_ge(st_mm[l][d], g + 1)
                        bk = SB[(3, 0, 1)[g]]
                        if g == 0:
                            ins = nc.vector.tensor_copy(s_t[:, 0], bk[:].rearrange("p (h n) -> p h n", h=HEADS))
                        else:
                            c = order[d][g]
                            for hh in range(HEADS):
                                ins = nc.vector.scalar_tensor_tensor(s_t[:, g, hh], s_t[:, g - 1, hh],
                                                                     T[:, c * HEADS + hh:c * HEADS + hh + 1],
                                                                     bk[:, hh * 128:(hh + 1) * 128], ALU.mult, ALU.add)
                        ins.then_inc(st_ev[l][d], 1)
                        dve.wait_ge(st_ev[l][d], g + 1)

                def pool_out(g):
                    dve.wait_ge(pool_hi[l], g + 1)
                    nc.vector.scalar_tensor_tensor(u_lo[:, 4 + g, c0:], B[2 + g][:, c0:],
                                                   vec[:, V_PSC + 4 * l + g:V_PSC + 4 * l + g + 1],
                                                   u_hi[:, 4 + g, c0:].bitcast(f32), ALU.mult,
                                                   ALU.subtract).then_inc(pool_lo[l], 1)

                states(0)
                los(1)
                dve.wait_ge(o_mm[l][0], len(outs_ch[l]))
                dve.wait_ge(dve_step, link.n)
                start(1)
                los(1)
                scan(1, lambda L: los(1 if L < 6 else 0))
                pool_out(0)
                pool_out(1)
                states(1)
                pool_out(2)
                pool_out(3)
                for k, c in enumerate(outs_ch[l]):
                    dve.wait_ge(o_mm[l][1], k + 1)
                    dve.wait_ge(o_ev[l][0], k + 1)
                    ov = o_t[:, :, c * 128:(c + 1) * 128]
                    tt(ov, ov, SB[c][:].rearrange("p (h n) -> p h n", h=HEADS), ALU.add).then_inc(o_ev[l][1], 1)
                def a_low(hh):
                    dve.wait_ge(a_hi[l], hh + 1)
                    tt(u_lo[:, hh, c0:], a32[:, hh, c0:], u_hi[:, hh, c0:].bitcast(f32), ALU.subtract).then_inc(a_lo[l], 1)

                ch = slice(c0 // 128, NCH)
                sv = stat[:].rearrange("p (h c) -> p h c", h=HEADS)
                dve.wait_ge(oms[l], HEADS)
                link(nc.vector.tensor_scalar(sv[:, :, ch], B[6][:, 0:HEADS * NCH].rearrange("p (h c) -> p h c", h=HEADS)[:, :, ch],
                                             EPS, None, ALU.add))
                nc.vector.reciprocal(stat[:], stat[:]).then_inc(oinv[l], 1)
                dve.wait_ge(orstd[l], 1)
                for hh in range(HEADS):
                    tt(odiag[:, hh, ch], ident.unsqueeze(1).broadcast_to((128, NCH - c0 // 128, 128)), bc(sv[:, hh, ch], 128),
                       ALU.mult).then_inc(odg[l], 1)
                for hh in range(HEADS):
                    dve.wait_ge(obc[l], hh + 1)
                    w = vec[:, V_HNW + HEADS * l + hh:V_HNW + HEADS * l + hh + 1]
                    link(nc.vector.scalar_tensor_tensor(a32[:, hh, c0:], o_t[:, hh, c0:], w, B[2 + hh][:, c0:],
                                                        ALU.mult, ALU.mult))
                    tt(a32[:, hh, c0:], a32[:, hh, c0:], sg[:, hh, c0:], ALU.mult).then_inc(a_f[l], 1)
                    if hh >= 1:
                        a_low(hh - 1)
                a_low(HEADS - 1)
                for kt in range(KT):
                    dve.wait_ge(sub_used, S0[f"wo{l}"] + kt + 1)
                    gated(FFN[l], l, 2, kt, B[kt % 2][:], c0)
                    los(1)
                    if l:
                        if kt >= NS:
                            mlo(kt - NS)
                        clear_experts(kt)

            mixer(0)
            stats(FFN[0], 0)
            los(4)
            modulated(FFN[0], 0, 1)

            def ffn_step(i, loop=False):
                def hidden(b):
                    dve.wait_ge(sil_ready, i * 2 + (b + 1))
                    dve.wait_ge(sub_used, i * 8 + (S0["ffn"] + (3, 7)[b] + 1))
                    dst = hid[:, bass.ds(i * 2 + b, 1), :].rearrange("p f n -> p (f n)") if loop else hid[:, 2 * i + b, :]
                    tt(dst, sil[:, b, :], B[2 * b + 1][:], ALU.mult).then_inc(hid_ready, 1)

                one = (lambda: lo(i - 1)) if loop else (lambda: los(1))
                for _ in range(3):
                    one()
                hidden(0)
                for _ in range(4):
                    one()
                if not loop and i == FFN_IT - 1:
                    modulation(1, (0, ADA_G), range(2))
                hidden(1)
                if loop or i < FFN_IT - 1:
                    one()

            ffn_step(0)
            j0 = nxt[0]
            with dve.Fori(1, FFN_IT - 1) as i:
                ffn_step(i, True)
            nxt[0] = j0 + 8 * (FFN_IT - 2)
            ffn_step(FFN_IT - 1)
            for f in range(22):
                dve.wait_ge(hs_hi, f + 1)
                tt(u_lo[:, f % KT, :], hid[:, f, :], u_hi[:, f % KT, :].bitcast(f32), ALU.subtract).then_inc(hs_lo, 1)
                if f >= KT or f == 0:
                    los(1)
            los(KT - LAST_F)
            for kt in range(KT):
                if kt < KT - 1:
                    dve.wait_ge(down_mm, kt + 1)
                else:
                    dve.wait_ge(sub_used, S0["down"] + 22)
                gated(MIX[1], 0, 5, kt, B[kt][:], 0)
            mixer(1)

            stats(FFN[1], CTX)
            dve.wait_ge(bcast_mm, FFN[1] + 1)
            for kt in range(KT):
                nc.vector.scalar_tensor_tensor(v32[:, kt, :], h[:, kt, CTX:], gain[:, 1, 1, kt, 1:2], B[6][:, CTX:],
                                               ALU.mult, ALU.mult).then_inc(hn_ready, 1)
            nc.vector.memset(msil, 0.0).then_inc(mh_ready, 1)
            dve.wait_ge(rt_mm, 1)
            link(nc.vector.tensor_copy(r_log, B[0][:, 0:16]))
            for c in range(2):
                link(nc.vector.max(r_top[:, 8 * c:8 * c + 8], r_log[:, 8 * c:8 * c + 8]))
                link(nc.vector.max_index(r_idx[:, 8 * c:8 * c + 8], r_top[:, 8 * c:8 * c + 8], r_log[:, 8 * c:8 * c + 8]))
            link(nc.vector.tensor_copy(r_idf, r_idx))
            for c in range(2):
                ins = tt(r_d[:, c:c + 1], r_top[:, 8 * c + 1:8 * c + 2], r_top[:, 8 * c:8 * c + 1], ALU.subtract)
            ins.then_inc(rt_in, 1)
            for c in range(2):
                for k in range(2):
                    link(nc.vector.tensor_scalar(r_m[:, k, 8 * c:8 * c + 8], e_iota, r_idf[:, 8 * c + k:8 * c + k + 1],
                                                 None, ALU.is_equal))
            tt(r_mask, r_m[:, 0], r_m[:, 1], ALU.add).then_inc(mask_ready, 1)
            dve.wait_ge(e_ready, 2)
            link(nc.vector.tensor_scalar(r_w[:, 0:2], r_e, 1.0, None, ALU.add))
            link(nc.vector.reciprocal(r_w[:, 0:2], r_w[:, 0:2]))
            link(tt(r_w[:, 2:4], r_e, r_w[:, 0:2], ALU.mult))
            for c in range(2):
                s = slice(8 * c, 8 * c + 8)
                link(nc.vector.tensor_scalar(r_comb[:, s], r_m[:, 0, s], r_w[:, c:c + 1], None, ALU.mult))
                link(nc.vector.scalar_tensor_tensor(r_comb[:, s], r_m[:, 1, s], r_w[:, 2 + c:3 + c], r_comb[:, s],
                                                    ALU.mult, ALU.add))
            dve.wait_ge(pos_mm, 1)
            two = lambda ap: ap.rearrange("p (c e) -> p c e", c=2)
            link(nc.vector.scalar_tensor_tensor(r_pos[:, :, 0:NE], two(B[1][:, 0:16]), 1.0, two(r_mask), ALU.add, ALU.mult))
            link(nc.vector.tensor_scalar(r_pos[:, :, 0:NE], r_pos[:, :, 0:NE], -1.0, None, ALU.add))
            link(nc.vector.tensor_scalar(r_pos[:, :, NE], r_pos[:, :, 0], -float(SLOTS), None, ALU.add))
            link(nc.vector.tensor_reduce(r_w[:, 0:1], B[1][:, 16:24], AX.X, ALU.max))
            link(nc.vector.tensor_scalar(r_w[:, 1:2], r_w[:, 0:1], SLOTS + 0.5, 1.0, ALU.is_gt, ALU.add))
            nc.vector.tensor_copy(npass_i[:], r_w[:, 1:2]).then_inc(route_ready, 1)
            dve.wait_ge(route_ready, 1)
            npass = dve.value_load(npass_i[0:1, 0:1], min_val=1, max_val=2)

            def slot_matrix(e):
                for c in range(2):
                    ins = nc.vector.tensor_scalar(pbuf[:, c, :], slot_iota, column(r_pos[:, c, :], e), None, ALU.is_equal)
                ins.then_inc(p_ready, 1)

            def column(ap, e):
                return ap[:, e:e + 1] if isinstance(e, int) else ap[:, bass.ds(e, 1)]

            def gathered(n):
                for g in range(2):
                    dve.wait_ge(xg_h, n * 2 + (g + 1))
                    tt(xg_lo[:, 4 * g:4 * g + 4, :].rearrange("p k n -> p (k n)"), B[2 + g][:],
                       xg_hi[:, 4 * g:4 * g + 4, :].rearrange("p k n -> p (k n)").bitcast(f32),
                       ALU.subtract).then_inc(xg_l, 1)

            def scattered(n, groups):
                for g in groups:
                    dve.wait_ge(sc_mm, n * 4 + (g + 1))
                    ya = yacc[:, 2 * g:2 * g + 2, :]
                    tt(ya, ya, B[(4, 5, 2, 3)[g]][:].rearrange("p (k n) -> p k n", k=2), ALU.add).then_inc(sc_ev, 1)

            slot_matrix(0)
            gathered(0)
            dve.wait_ge(sc_ev, 4)
            with dve.Fori(0, npass) as ps:
                with dve.Fori(0, NE) as e:
                    it = ps * NE + e
                    for s in range(MOE_S):
                        for what, c in M_EVENTS.get(s, ()):
                            if what == "up":
                                dve.wait_ge(msil_ready, it * FC + (c + 1))
                                dve.wait_ge(sub_used, it * MOE_S + (S0["moe"] + s + 1))
                                tt(mh[:, c % 2, :], msil, B[2 * (c % 2) + 1][:], ALU.mult).then_inc(mh_ready, 1)
                            elif what == "ht":
                                dve.wait_ge(ht_h, it * FC + (c + 1))
                                tt(ht_lo[:, c % 2, :], B[4 + c % 2][:], ht_hi[:, c % 2, :].bitcast(f32),
                                   ALU.subtract).then_inc(ht_l, 1)
                            elif what == "scatter":
                                scattered(it, (2 * c, 2 * c + 1))
                            elif what == "slots":
                                for c in range(2):
                                    ins = nc.vector.tensor_scalar(pw[:, c, :], slot_iota, column(r_pos[:, c, :], e),
                                                                  r_comb[:, bass.ds(e + 8 * c, 1)], ALU.is_equal, ALU.mult)
                                ins.then_inc(pw_ready, 1)
                                slot_matrix(e + 1)
                            elif what == "gather":
                                gathered(it + 1)
                        if s == MOE_S - 1:
                            dve.wait_ge(sub_used, it * MOE_S + (S0["moe"] + MOE_S))
                            nc.vector.tensor_copy(ybuf[:, 512:1024], B[7][:]).then_inc(y_ev, 1)
                        mlo(s + NS, it)
                nc.vector.tensor_scalar(slot_iota, slot_iota, float(SLOTS), None, ALU.add).then_inc(slot_step, 1)
                dve.wait_ge(slot_step, ps + 1)
            for g in range(4):
                scattered(npass * NE, (g,))
                dve.wait_ge(sc_ev, npass * (4 * NE) + (4 + g + 1))
                for kt in (2 * g, 2 * g + 1):
                    gated(4, 1, 5, kt, yacc[:, kt, :], CTX)
            stats(4, CTX)
            dve.wait_ge(bcast_mm, 5)
            for kt in range(KT):
                nc.vector.scalar_tensor_tensor(v32[:, kt, :], h[:, kt, CTX:], vec[:, V_FIN + kt:V_FIN + kt + 1],
                                               B[6][:, CTX:], ALU.mult, ALU.mult).then_inc(hn_ready, 1)
            for g in range(2):
                dve.wait_ge(out_tr, 2 * g + 2)
                nc.vector.tensor_copy(osb[:, g, 512:1024], B[3 + 2 * g][:]).then_inc(out_ev[1], 1)

        @block.gpsimd
        def _(pool):
            for n, c0 in enumerate((0, 0, 0, CTX, CTX)):
                for kt in range(1, KT):
                    pool.wait_ge(sq_ready, KT * n + kt + 1)
                    if kt == 1:
                        ins = nc.gpsimd.tensor_tensor(sq_sum[:, c0:], sq[:, 0, c0:], sq[:, 1, c0:], ALU.add)
                        ins.then_inc(sq_used, 2)
                    else:
                        ins = nc.gpsimd.tensor_tensor(sq_sum[:, c0:], sq_sum[:, c0:], sq[:, kt % 2, c0:], ALU.add)
                        ins.then_inc(sq_used, 1)
                    pool.wait_ge(sq_used, KT * n + kt + 1)
                pool.nop().then_inc(sq_summed, 1)

        @block.tensor
        def _(pe):
            nxt = [0]
            mm = nc.tensor.matmul

            def wsub(j):
                return w_hi[:, j % NS, :], w_lo[:, j % NS, :]

            def mm3(out, lh, ll, rh, rl, start, stop):
                mm(out, lh, rh, start=start, stop=False)
                mm(out, lh, rl, start=False, stop=False)
                return mm(out, ll, rh, start=False, stop=stop)

            def stats(n, c0):
                pe.wait_ge(sq_summed, n + 1)
                for c in range(c0 // 128, NCH):
                    ins = mm(B[6][:, c:c + 1], sq_sum[:, c * 128:(c + 1) * 128], ones_d[:, 0:1], start=True, stop=True)
                ins.then_inc(mean_sq, 1)

            def spread(n, c0):
                pe.wait_ge(diag_ready, n + 1)
                mm(B[6][:, c0:], ones[:], ndiag[:, c0 // 128:NCH].rearrange("p c n -> p (c n)"),
                   start=True, stop=True).then_inc(bcast_mm, 1)

            pe.wait_ge(vec_in, 32)
            pe.wait_ge(const_in, 16)
            nc.tensor.transpose(B[6][:, 0:96], vrow[0:96, 0, :], ident[0:96, 0:96]).then_inc(vec_tr, 1)
            nc.tensor.transpose(B[6][:, 96:184], vrow[0:88, 1, :], ident[0:88, 0:88]).then_inc(vec_tr, 1)

            def ada_sub(j, k, bank, i=0):
                pe.wait_ge(lo_done, i * 8 + (j + 1))
                wh, wl = (w.rearrange("p (k n) -> p k n", k=2) for w in wsub(j))
                for kk in range(2):
                    kt = 2 * k + kk
                    mm(bank[:], c4[:, kt, :], wh[:, kk], start=(kt == 0), stop=False)
                    ins = mm(bank[:], c4[:, kt, :], wl[:, kk], start=False, stop=(kt == KT - 1))
                ins.then_inc(sub_used, 1)

            def ada_cols(g, b, i=0, step=1):
                pe.wait_ge(row_ev, i * step + (g + 1))
                for k in range(4):
                    if isinstance(i, int):
                        o = B[7][:, 8 * (g % ADA_G) + 2 * k:8 * (g % ADA_G) + 2 * k + 2]
                    else:
                        o = B[7][:, bass.ds(i * (8 * step) + (8 * (g % ADA_G) + 2 * k), 2)]
                    ins = mm(o, row[0:4, b, k * 128:(k + 1) * 128], sel[:], start=True, stop=True)
                ins.then_inc(row_used, 1)

            pe.wait_ge(x_in, 32)
            for kt in range(KT):
                if kt >= 4:
                    pe.wait_ge(h_ready, KT * 0 + kt - 3)
                for c in range(NCH):
                    ins = nc.tensor.transpose(B[kt % 4][:, c * 128:(c + 1) * 128], xin[:, c, kt * 128:(kt + 1) * 128], ident)
                ins.then_inc(x_tr, 1)
            pe.wait_ge(ones_ready, 4)

            def take_sub():
                j = nxt[0]
                nxt[0] += 1
                pe.wait_ge(lo_done, j + 1)
                return j

            def token_major(l, chunks, k):
                j = take_sub()
                wh, wl = (w.rearrange("p (k n) -> p k n", k=2) for w in wsub(j))
                for kk in range(2):
                    kt = 2 * k + kk
                    for c in chunks:
                        t = slice(c * 128, (c + 1) * 128)
                        ins = mm3(B[2 + c][:], u_hi[:, kt, t], u_lo[:, kt, t], wh[:, kk], wl[:, kk], kt == 0, kt == KT - 1)
                ins.then_inc(sub_used, 1)

            def block_fm(bank, c0):
                j = take_sub()
                wh, wl = (w.rearrange("p (k n) -> p k n", k=KT) for w in wsub(j))
                for kt in range(KT):
                    mm3_(bank[:, c0:], wh[:, kt], wl[:, kt], kt, c0)
                last[0].then_inc(sub_used, 1)

            def block_pair(banks, j, c0, kts, ready):
                pe.wait_ge(lo_done, j + 2)
                for n_, kt in enumerate(kts):
                    ready(kt)
                    for b, bank in enumerate(banks):
                        wh, wl = (w.rearrange("p (k n) -> p k n", k=KT)[:, kt] for w in wsub(j + b))
                        ins = mm3(bank[:, c0:], wh, wl, u_hi[:, kt, c0:], u_lo[:, kt, c0:], n_ == 0, n_ == KT - 1)
                        if n_ == KT - 1:
                            ins.then_inc(sub_used, 1)

            def first_blocks(banks, j, n):
                block_pair(banks, j, 0, range(KT), lambda kt: pe.wait_ge(u_ready, KT * n + kt + 1))

            last = [None]

            def mm3_(out, wh, wl, kt, c0):
                last[0] = mm3(out, wh, wl, u_hi[:, kt, c0:], u_lo[:, kt, c0:], kt == 0, kt == KT - 1)

            def mixer(l):
                n, c0 = MIX[l], c0s[l]
                TL = tiles(l)
                t0, nt = TL[0], len(TL)
                blk = [0]
                if l:
                    stats(n, 0)
                    spread(n, 0)

                def proj_block(cc):
                    if blk[0] >= 2:
                        pe.wait_ge(proj_ev[l], blk[0] - 1)
                    block_fm(B[2 + blk[0] % 2], cc)
                    blk[0] += 1

                if l:
                    first_blocks((B[2], B[3]), nxt[0], n)
                    nxt[0] += 2
                    blk[0] += 2
                    for _ in range(2):
                        proj_block(0)
                    for _ in range(4):
                        proj_block(c0)
                else:
                    pe.wait_ge(c_lo, 1)
                    for kind, g in FIRST:
                        if (kind, g) == ("p", 0):
                            first_blocks((B[2], B[3]), nxt[0], n)
                            nxt[0] += 2
                            blk[0] += 2
                        elif kind == "p" and g > 1:
                            proj_block(0)
                        for k in range(4 * (kind == "a")):
                            ada_sub(take_sub(), k, B[4 + g % 2])
                            if k == 3 and g == 0:
                                stats(0, 0)
                            if k == 1 and g == 2:
                                spread(0, 0)
                            if k == 1 and g >= 1:
                                if g == SHIFT_SCALE_G + 1:
                                    pe.wait_ge(mod_ready, 1)
                                ada_cols(g - 1, (g - 1) % 2)
                    ada_cols(ADA_G - 1, (ADA_G - 1) % 2)
                pe.wait_ge(proj_ev[l], 8)
                token_major(l, range(NCH), 0)

                def scan(d, fill):
                    qh, kh = (1, 0) if d == 0 else (0, 1)
                    pe.wait_ge(scan_ready[l][d], 1)
                    if d == 1:
                        pe.wait_ge(o_ev[l][0], len(outs_ch[l]))
                    for g in range(nt // 4):
                        for t in range(4):
                            ti = TL[4 * g + t]
                            ins = mm(SB[g][:, t * 128:(t + 1) * 128], ks[:, ti * 128:(ti + 1) * 128],
                                     q_t[:, ti * 128:(ti + 1) * 128], start=True, stop=True)
                        ins.then_inc(diag_mm[l][d], 1)
                    pe.wait_ge(diag_ev[l][d], nt // 4)
                    for L in range(LEVELS):
                        m = 1 << L
                        pe.wait_ge(scan_ready[l][d], L + 1)
                        if L >= 2:
                            pe.wait_ge(lvl_ev[l][d], (L - 1) * (nt // 8))
                        for g in range(nt // 8):
                            for t in range(8):
                                ti = TL[8 * g + t]
                                ins = mm(SB[2 * (L % 2) + g][:, t * 64:(t + 1) * 64], ks[:, ti * 128:(ti + 1) * 128],
                                         seg(qp, ti, 1, m, qh), start=True, stop=True)
                            ins.then_inc(lvl_mm[l][d], 1)
                        fill(L)
                    pe.wait_ge(scan_ready[l][d], LEVELS + 1)
                    pe.wait_ge(lvl_ev[l][d], LEVELS * (nt // 8))
                    for g in range(3):
                        for hh in range(HEADS):
                            ti = order[d][g] * HEADS + hh
                            ins = nc.tensor.transpose(SB[g][:, hh * 128:(hh + 1) * 128], ks[:, ti * 128:(ti + 1) * 128], ident)
                        ins.then_inc(kst_tr[l][d], 1)
                    fill("keys")
                    for g in range(3):
                        c = order[d][g]
                        pe.wait_ge(kst_ev[l][d], g + 1)
                        for hh in range(HEADS):
                            ti = c * HEADS + hh
                            ins = mm(SB[(3, 0, 1)[g]][:, hh * 128:(hh + 1) * 128], ks[:, ti * 128:(ti + 1) * 128],
                                     v_t[:, c, hh * 128:(hh + 1) * 128], start=True, stop=True)
                        ins.then_inc(st_mm[l][d], 1)
                    fill("states")
                    pe.wait_ge(st_ev[l][d], 3)
                    for c in outs_ch[l]:
                        pos = order[d].index(c)
                        for hh in range(HEADS):
                            ti = c * HEADS + hh
                            o = SB[c][:, hh * 128:(hh + 1) * 128]
                            ins = mm(o, v_t[:, c, hh * 128:(hh + 1) * 128], amat[:, ti * 128:(ti + 1) * 128],
                                     start=True, stop=(pos == 0))
                            if pos:
                                ins = mm(o, s_t[:, pos - 1, hh, :], qp[:, ti * 128:(ti + 1) * 128], start=False, stop=True)
                        ins.then_inc(o_mm[l][d], 1)

                def fill0(L):
                    if L == "keys":
                        pe.wait_ge(proj_ev[l], 12)
                        token_major(l, outs_ch[l], 0)
                    elif L == "states":
                        token_major(l, outs_ch[l], 1)
                    elif L < 3:
                        token_major(l, range(NCH), L + 1)
                    else:
                        if L == 3:
                            pe.wait_ge(i_ev[l], NCH)
                        proj_block(0)

                u0 = U0[f"pm{l}"]

                def fill1(L):
                    if L == 0:
                        token_major(l, outs_ch[l], 3)
                    elif L in (1, 2, 3, 4):
                        if L == 1:
                            pe.wait_ge(pv_ev[l], len(outs_ch[l]))
                        proj_block(c0)
                    elif L == 5:
                        for k in range(2 - l):
                            pe.wait_ge(raw_in[(u0 + k) % NR], 16 * ((u0 + k) // NR + 1))
                        pe.wait_ge(wp_in, 16 * (l + 1))
                        pe.wait_ge(proj_ev[l], 16)
                        diff_block(0)
                        diff_block(1)
                    elif L == 6:
                        diff_block(2)
                        diff_block(3)
                        pool_block(0)
                        pool_block(1)
                    elif L == "keys":
                        pool_block(2)
                        pool_block(3)

                def diff_block(g):
                    for side in ([0, 1] if l == 0 else [1]):
                        mat = raw[:, (u0 + side - l) % NR, :].rearrange("p (s g n) -> p s g n", s=2, g=4)
                        for s in range(2):
                            ins = mm(B[2 + g][:, side * 256:(side + 1) * 256], pv[:, 2 * side + s, g * 128:(g + 1) * 128],
                                     mat[:, s, g, :], start=(s == 0), stop=(s == 1))
                    ins.then_inc(diff_mm[l], 1)

                def pool_block(g):
                    pe.wait_ge(diff_ev[l], g + 1)
                    mm(B[2 + g][:, c0:], wp[:, g, :], diff[:, g, c0:], start=True, stop=True).then_inc(pool_mm[l], 1)

                scan(0, fill0)
                token_major(l, outs_ch[l], 2)
                scan(1, fill1)
                pe.wait_ge(o_ev[l][1], len(outs_ch[l]))
                for hh in range(HEADS):
                    pe.wait_ge(osq[l], hh + 1)
                    for c in outs_ch[l]:
                        ins = mm(B[6][:, NCH * hh + c:NCH * hh + c + 1], sq_o[:, hh, c * 128:(c + 1) * 128], ones_hd[:, 0:1],
                                 start=True, stop=True)
                    ins.then_inc(oms[l], 1)
                pe.wait_ge(pool_lo[l], 4)
                for hh in range(HEADS):
                    pe.wait_ge(odg[l], hh + 1)
                    mm(B[2 + hh][:, c0:], ones[:], odiag[:, hh, c0 // 128:].rearrange("p c n -> p (c n)"),
                       start=True, stop=True).then_inc(obc[l], 1)
                block_pair((B[0], B[1]), nxt[0], c0, (4, 5, 6, 7, 0, 1, 2, 3),
                           lambda kt: pe.wait_ge(a_lo[l], kt + 1) if kt < HEADS else None)
                nxt[0] += 2
                for j in range(2, 8):
                    pe.wait_ge(h_ready, KT * FFN[l] + j - 1)
                    block_fm(B[j % 2], c0)

            mixer(0)
            for k in range(4):
                ada_sub(S0["ada1"] + k, k, B[4])
            stats(FFN[0], 0)
            ada_cols(ADA_G, 0)
            spread(FFN[0], 0)
            base = S0["ffn"]

            def ffn_step(i, dyn):
                def block(s, b, k):
                    jj = base + s
                    pe.wait_ge(lo_done, i * 8 + (jj + 1))
                    if k == 0 and (dyn or i > 0):
                        pe.wait_ge(hid_ready, i * 2 + (b - 1))
                    wh, wl = (w.rearrange("p (k n) -> p k n", k=KT) for w in wsub(jj))
                    for kt in range(KT):
                        mm3_(B[2 * b + k][:], wh[:, kt], wl[:, kt], kt, 0)
                    last[0].then_inc(sub_used, 1)

                for k in range(2):
                    ada_sub(base + k, k, B[4], i)
                if dyn or i > 0:
                    block(2, 0, 0)
                    block(3, 0, 1)
                else:
                    first_blocks((B[0], B[1]), base + 2, FFN[0])
                for k in range(2):
                    ada_sub(base + 4 + k, 2 + k, B[4], i)
                block(6, 1, 0)
                ada_cols(ADA_G + 1, 0, i) if dyn else ada_cols(ADA_G + 1 + i, 0)
                block(7, 1, 1)

            ffn_step(0, False)
            with pe.Fori(1, FFN_IT - 1) as i:
                ffn_step(i, True)
            ffn_step(FFN_IT - 1, False)
            nxt[0] = S0["down"]
            pe.wait_ge(hid_ready, 22)
            for f in range(22 - LAST_F):
                j = take_sub()
                wh, wl = wsub(j)
                pe.wait_ge(hs_lo, f + 1)
                if f == 0:
                    pe.wait_ge(mod_ready, 3)
                for d in range(KT):
                    dd = slice(d * 128, (d + 1) * 128)
                    ins = mm3(B[d][:], wh[:, dd], wl[:, dd], u_hi[:, f % KT, :], u_lo[:, f % KT, :], f == 0, False)
                ins.then_inc(sub_used, 1)
            js = [take_sub() for _ in range(LAST_F)]
            pe.wait_ge(hs_lo, 22)
            for d in range(KT):
                dd = slice(d * 128, (d + 1) * 128)
                for f, j in zip(range(22 - LAST_F, 22), js):
                    wh, wl = wsub(j)
                    ins = mm3(B[d][:], wh[:, dd], wl[:, dd], u_hi[:, f % KT, :], u_lo[:, f % KT, :], False, f == 21)
                if d < KT - 1:
                    ins.then_inc(down_mm, 1)
            ins.then_inc(sub_used, LAST_F)
            pe.wait_ge(h_ready, KT * MIX[1] + KT)
            mixer(1)
            pe.wait_ge(h_ready, KT * FFN[1] + KT)
            stats(FFN[1], CTX)
            spread(FFN[1], CTX)
            pe.wait_ge(rw_in, 16)
            for kt in range(KT):
                pe.wait_ge(uh_ready, KT * FFN[1] + kt + 1)
                for c in range(2):
                    ins = mm(B[0][:, 8 * c:8 * c + 8], v32[:, kt, c * 128:(c + 1) * 128], rt[:, kt * 8:kt * 8 + 8],
                             start=(kt == 0 and c == 0), stop=(kt == KT - 1), skip_group_check=True)
            ins.then_inc(rt_mm, 1)

            def tokens(gs):
                for g in gs:
                    for k in range(4):
                        kt = 4 * (g % 2) + k
                        ins = nc.tensor.transpose(B[2 + g][:, k * 128:(k + 1) * 128],
                                                  v32[:, kt, (g // 2) * 128:(g // 2 + 1) * 128], ident)
                    ins.then_inc(vtok_tr, 1)

            tokens((0, 1))
            pe.wait_ge(mask_ready, 1)
            mm(B[1][:, 0:8], tri, r_mask[:, 0:8], start=True, stop=True)
            mm(B[1][:, 8:16], tri, r_mask[:, 8:16], start=True, stop=False)
            mm(B[1][:, 8:16], ones[:], r_mask[:, 0:8], start=False, stop=True)
            mm(B[1][:, 16:24], ones[:], r_mask[:, 0:8], start=True, stop=False)
            mm(B[1][:, 16:24], ones[:], r_mask[:, 8:16], start=False, stop=True).then_inc(pos_mm, 1)
            tokens((2, 3))
            pe.wait_ge(vtok_ev, 4)
            pe.wait_ge(route_ready, 1)
            npass = pe.value_load(npass_i[0:1, 0:1], min_val=1, max_val=2)
            S_M = S0["moe"]

            def gather(n):
                pe.wait_ge(p_ready, n + 1)
                for g in range(2):
                    for k in range(4):
                        kt = 4 * g + k
                        for c in range(2):
                            ins = mm(B[2 + g][:, k * 128:(k + 1) * 128], vtok[:, c, kt * 128:(kt + 1) * 128],
                                     pbuf[:, c, :], start=(c == 0), stop=(c == 1))
                    ins.then_inc(xg_mm, 1)

            def scatter(n, pair):
                if pair == 0:
                    pe.wait_ge(y_ev, n * 2 + 2)
                    pe.wait_ge(pwt_ev, n + 1)
                for g in (2 * pair, 2 * pair + 1):
                    for k in range(2):
                        kt = 2 * g + k
                        ins = mm(B[(4, 5, 2, 3)[g]][:, k * 256:(k + 1) * 256], ybuf[:, kt * 128:(kt + 1) * 128], pwt,
                                 start=True, stop=True)
                    ins.then_inc(sc_mm, 1)

            gather(0)
            with pe.Fori(0, npass) as ps:
                with pe.Fori(0, NE) as e:
                    it = ps * NE + e
                    for g in range(2):
                        pe.wait_ge(xg_l, it * 2 + (g + 1))

                    def hidden_tr(c):
                        pe.wait_ge(mh_ready, it * FC + (c + 2))
                        for k in range(4):
                            ins = nc.tensor.transpose(B[4 + c % 2][:, k * 128:(k + 1) * 128],
                                                      mh[:, c % 2, k * 128:(k + 1) * 128], ident)
                        ins.then_inc(ht_tr, 1)

                    s = 0
                    for n, (kind, c, b) in enumerate(MOE_ORDER):
                        if b == 0 and kind == "u" and c >= 1:
                            hidden_tr(c - 1)
                        if b == 0 and kind == "g" and c == 1:
                            pe.wait_ge(pw_ready, it + 1)
                            for cc in range(2):
                                ins = nc.tensor.transpose(B[6][:, cc * 128:(cc + 1) * 128], pw[:, cc, :], ident)
                            ins.then_inc(pwt_tr, 1)
                            pe.wait_ge(sc_ev, it * 4 + 8)
                        if b == 0 and kind == "d" and c == 0:
                            pe.wait_ge(pwt_ev, it + 2)
                        if b == 0 and kind == "d" and c == FC - 2:
                            gather(it + 1)
                        if b == 0 and kind == "d":
                            if c == FC - 1:
                                hidden_tr(c)
                            pe.wait_ge(ht_l, it * FC + (c + 1))
                        for half in range(2):
                            pe.wait_ge(lo_done, it * MOE_S + (S_M + s + 1))
                            wh, wl = wsub(S_M + s)
                            if kind == "d":
                                ft = 2 * b + half
                                lh, ll = (w[:, c % 2, ft * 128:(ft + 1) * 128] for w in (ht_hi, ht_lo))
                                first, final = (c == 0 and ft == 0), (c == FC - 1 and ft == 3)
                                for nb in range(2):
                                    cc = slice(nb * 512, (nb + 1) * 512)
                                    mm(B[6 + nb][:], lh, wh[:, cc], start=first, stop=False)
                                    mm(B[6 + nb][:], lh, wl[:, cc], start=False, stop=False)
                                for nb in range(2):
                                    ins = mm(B[6 + nb][:], ll, wh[:, nb * 512:(nb + 1) * 512], start=False, stop=final)
                            else:
                                bank = B[2 * (c % 2) + (kind == "u")]
                                for kk in range(2):
                                    kt = 4 * b + 2 * half + kk
                                    ins = mm3(bank[:], xg_hi[:, kt, :], xg_lo[:, kt, :], wh[:, kk * 512:(kk + 1) * 512],
                                              wl[:, kk * 512:(kk + 1) * 512], kt == 0, kt == KT - 1)
                            ins.then_inc(sub_used, 1)
                            if s in (3, 4):
                                scatter(it, s - 3)
                            s += 1
            for pair in range(2):
                scatter(npass * NE, pair)
            stats(4, CTX)
            spread(4, CTX)
            pe.wait_ge(hn_ready, KT * 4 + KT)
            for c in range(2):
                for g in range(2):
                    for k in range(4):
                        ins = nc.tensor.transpose(B[2 + 2 * c + g][:, k * 128:(k + 1) * 128],
                                                  v32[:, 4 * g + k, c * 128:(c + 1) * 128], ident)
                    ins.then_inc(out_tr, 1)


def pooling_matrices():
    import numpy as np
    def line(n, k):
        m = np.zeros((n, n))
        for t in range(n):
            lo, hi = max(t - k // 2, 0), min(t + k - 1 - k // 2 + 1, n)
            m[lo:hi, t] = 1.0 / (hi - lo)
        return m
    mats = np.zeros((2, 256, 4, 256))
    for g, k in enumerate((2, 4, 8, 16)):
        mats[0, :, g, :] = line(CTX, k) - np.eye(CTX)
        mats[1, :, g, :] = np.kron(line(LAT // 64, k), line(64, k)) - np.eye(LAT)
    return np.ascontiguousarray(mats.reshape(2, 2, 128, 4, 256).transpose(0, 2, 1, 3, 4), dtype=np.float32)


def level_masks():
    import numpy as np
    out = np.zeros((128, 2, LEVELS, 64), np.float32)
    s = np.arange(128)[:, None]
    t = np.arange(64)[None, :]
    for L in range(LEVELS):
        m = 1 << L
        same = (s // (2 * m)) == (t // m)
        out[:, 0, L] = same & ((s // m) % 2 == 0)
        out[:, 1, L] = same & ((s // m) % 2 == 1)
    return out.reshape(128, -1)


def kernel(**inputs):
    import numpy as np
    import concourse.bacc as bacc
    from concourse.bass_utils import run_bass_kernel_spmd

    a = {k: np.ascontiguousarray(v) for k, v in inputs.items()}
    rows = lambda v: v.reshape(-1, 128)
    vecs = np.concatenate([rows(a["b_ada"]), rows(a["norm_w"]), rows(a["hgrn_lb_raw"]), rows(a["hgrn_norm_w"]),
                           rows(a["pool_scale"]), rows(a["final_norm_w"]), rows(a["c_ctx"]), rows(a["c"])])
    i = np.arange(128)
    cf32 = np.concatenate([np.eye(128), (i[:, None] < i[None, :]), np.tile(i, (128, 1)),
                           np.tile(np.arange(8), (128, 1))], axis=1).astype(np.float32)
    ins = [("x", a["x"][0]), ("ctx_in", a["ctx"][0]), ("vecs", vecs), ("w_ada", a["w_ada"]), ("w_in", a["w_in"]),
           ("w_pool", a["w_pool"]), ("w_out", a["w_out"]), ("ffn_wg", a["ffn_wg"][0]), ("ffn_wu", a["ffn_wu"][0]),
           ("ffn_wd", a["ffn_wd"][0]), ("router_w", a["router_w"][0]), ("moe_wg", a["moe_wg"][0]),
           ("moe_wu", a["moe_wu"][0]), ("moe_wd", a["moe_wd"][0]), ("cf32", cf32),
           ("pool_mats", pooling_matrices()), ("masks", level_masks())]
    nc = bacc.Bacc("TRN2", target_bir_lowering=False, num_devices=1)
    arrays, aps = {}, []
    for name, v in ins:
        arrays[f"in_{name}"] = v
        aps.append(nc.dram_tensor(f"in_{name}", v.shape, mybir.dt.from_np(v.dtype), kind="ExternalInput").ap())
    o = nc.dram_tensor("out_lat", (LAT, D), mybir.dt.float32, kind="ExternalOutput").ap()
    bass_hybrid_trunk(nc, *aps, o)
    r = run_bass_kernel_spmd(nc, [arrays], core_ids=[0])
    return r.results[0]["out_lat"].reshape(1, LAT, D)
```
